# Optimizing a Trainium2 kernel written in Bass

```python
import jax, jax.numpy as jnp
from jax import lax
import numpy as np
import jax
import jax.numpy as jnp

D_MODEL = 1024
BATCH = 1
SEQ = 256
DEPTH = 2

N_A_LAYERS = DEPTH // 2
N_B_LAYERS = DEPTH - N_A_LAYERS
D_FF = 4 * D_MODEL
NORM_EPS = 1e-6
CHUNK = 128
SGU_WIDTH = D_MODEL
SGU_GROUPS = 8
SGU_GROUP_DIM = SGU_WIDTH // SGU_GROUPS
N_HEADS = 16
N_KV_HEADS = 4
HEADS_PER_GROUP = N_HEADS // N_KV_HEADS
HEAD_DIM = D_MODEL // N_HEADS
CMP_BLOCK = 32
CMP_STRIDE = 16
CMP_HIDDEN = 4 * HEAD_DIM
SEL_BLOCK = 64
N_SELECT = 16
WINDOW = 512
Q_BLOCK = 16
N_BRANCH = 3
FORCE_SCORE = 1e4


def rms_norm(x, g):
    xf = x.astype(jnp.float32)
    y = xf * lax.rsqrt(jnp.mean(xf * xf, axis=-1, keepdims=True) + NORM_EPS)
    return (y * g.astype(jnp.float32)).astype(x.dtype)

def layer_norm(x, g, b):
    xf = x.astype(jnp.float32)
    mu = jnp.mean(xf, axis=-1, keepdims=True)
    var = jnp.mean(jnp.square(xf - mu), axis=-1, keepdims=True)
    y = (xf - mu) * lax.rsqrt(var + NORM_EPS) * g.astype(jnp.float32) + b.astype(jnp.float32)
    return y.astype(x.dtype)

def modulate(h, shift, scale):
    return h * (1.0 + scale[:, None, :]) + shift[:, None, :]

def masked_softmax(s, mask):
    s = jnp.where(mask, s.astype(jnp.float32), -jnp.inf)
    m = jnp.max(s, axis=-1, keepdims=True)
    m = jnp.where(jnp.isfinite(m), m, 0.0)
    e = jnp.exp(s - m)
    den = jnp.sum(e, axis=-1, keepdims=True)
    return e / jnp.where(den > 0, den, 1.0)

def gmlp_mixer(h, w_in, ln_g, ln_b, w_s, b_s, w_out):
    B, T, _ = h.shape
    z = jax.nn.gelu(h @ w_in)
    u, v = jnp.split(z, 2, axis=-1)
    v = layer_norm(v, ln_g, ln_b)
    v = v.reshape(B, T // CHUNK, CHUNK, SGU_GROUPS, SGU_GROUP_DIM)
    causal = jnp.tril(jnp.ones((CHUNK, CHUNK), dtype=bool))
    w = jnp.where(causal[None], w_s, 0.0).astype(v.dtype)
    mixed = jnp.einsum('gts,bcsgd->bctgd', w, v) + b_s.T[:, :, None]
    out = u * mixed.reshape(B, T, SGU_WIDTH)
    return out @ w_out

def nsa_shared_kv(x, c_act, ada_w, ada_b, norm_g, w_kv, cmp_pos, cmp_w1, cmp_b1, cmp_w2, cmp_b2):
    B, T, _ = x.shape
    shift, scale = jnp.split(c_act @ ada_w + ada_b, 2, axis=-1)
    h = modulate(rms_norm(x, norm_g), shift, scale)
    kv = (h @ w_kv).reshape(B, T, 2 * N_BRANCH, N_KV_HEADS, HEAD_DIM)
    k_cmp_raw, v_cmp_raw = kv[:, :, 0], kv[:, :, 1]
    k_sel, v_sel = kv[:, :, 2], kv[:, :, 3]
    k_win, v_win = kv[:, :, 4], kv[:, :, 5]
    n_cmp = (T - CMP_BLOCK) // CMP_STRIDE + 1
    tok = jnp.arange(n_cmp)[:, None] * CMP_STRIDE + jnp.arange(CMP_BLOCK)[None, :]

    def compress(raw, j):
        blk = raw[:, tok] + cmp_pos[j][None, None, :, None, :]
        blk = blk.transpose(0, 1, 3, 2, 4).reshape(B, n_cmp, N_KV_HEADS, CMP_BLOCK * HEAD_DIM)
        hid = jax.nn.gelu(blk @ cmp_w1[j] + cmp_b1[j])
        return hid @ cmp_w2[j] + cmp_b2[j]

    n_sel = T // SEL_BLOCK

    def to_blocks(a):
        return a.reshape(B, n_sel, SEL_BLOCK, N_KV_HEADS, HEAD_DIM).transpose(0, 3, 1, 2, 4)

    pad = ((0, 0), (WINDOW, 0), (0, 0), (0, 0))
    return (compress(k_cmp_raw, 0), compress(v_cmp_raw, 1), to_blocks(k_sel), to_blocks(v_sel),
            jnp.pad(k_win, pad), jnp.pad(v_win, pad))

def nsa_mixer(h, w_in, w_out, k_cmp, v_cmp, k_sel, v_sel, k_win, v_win):
    B, T, _ = h.shape
    HD = N_HEADS * HEAD_DIM
    proj = h @ w_in
    q = proj[..., :HD].reshape(B, T, N_KV_HEADS, HEADS_PER_GROUP, HEAD_DIM) * (HEAD_DIM ** -0.5)
    gates = jax.nn.sigmoid(proj[..., HD:].astype(jnp.float32)).reshape(
        B, T, N_KV_HEADS, HEADS_PER_GROUP, N_BRANCH)
    pos = jnp.arange(T)

    n_cmp = k_cmp.shape[1]
    cmp_end = jnp.arange(n_cmp) * CMP_STRIDE + CMP_BLOCK - 1
    s_cmp = jnp.einsum('btghd,bcgd->bghtc', q, k_cmp)
    p_cmp = masked_softmax(s_cmp, cmp_end[None, :] <= pos[:, None])
    o_cmp = jnp.einsum('bghtc,bcgd->btghd', p_cmp.astype(v_cmp.dtype), v_cmp)

    n_blocks = k_sel.shape[2]
    ci = jnp.arange(n_cmp)[:, None] * CMP_STRIDE
    sj = jnp.arange(n_blocks)[None, :] * SEL_BLOCK
    overlap = ((ci < sj + SEL_BLOCK) & (ci + CMP_BLOCK > sj)).astype(jnp.float32)
    imp = jnp.einsum('bghtc,cj->bgtj', p_cmp, overlap)
    cur = (pos // SEL_BLOCK)[:, None]
    js = jnp.arange(n_blocks)[None, :]
    imp = jnp.where(js > cur, -1.0, imp)
    forced = (js == 0) | (js == cur) | (js == cur - 1)
    imp = jnp.where(forced, FORCE_SCORE, imp)
    n_top = min(N_SELECT, n_blocks)
    _, sel_idx = lax.top_k(imp, n_top)

    bi = jnp.arange(B)[:, None, None, None]
    gi = jnp.arange(N_KV_HEADS)[None, :, None, None]
    in_blk = jnp.arange(SEL_BLOCK)
    win_off = jnp.arange(WINDOW + Q_BLOCK)

    def block_step(start):
        tq = start + jnp.arange(Q_BLOCK)
        qb = lax.dynamic_slice_in_dim(q, start, Q_BLOCK, axis=1)
        gb = lax.dynamic_slice_in_dim(gates, start, Q_BLOCK, axis=1)
        ocb = lax.dynamic_slice_in_dim(o_cmp, start, Q_BLOCK, axis=1)
        ib = lax.dynamic_slice_in_dim(sel_idx, start, Q_BLOCK, axis=2)
        ks = k_sel[bi, gi, ib].reshape(B, N_KV_HEADS, Q_BLOCK, n_top * SEL_BLOCK, HEAD_DIM)
        vs = v_sel[bi, gi, ib].reshape(B, N_KV_HEADS, Q_BLOCK, n_top * SEL_BLOCK, HEAD_DIM)
        kpos = (ib[..., None] * SEL_BLOCK + in_blk).reshape(B, N_KV_HEADS, 1, Q_BLOCK, n_top * SEL_BLOCK)
        s_sel = jnp.einsum('bqghd,bgqmd->bghqm', qb, ks)
        p_sel = masked_softmax(s_sel, kpos <= tq[None, None, None, :, None])
        o_sel = jnp.einsum('bghqm,bgqmd->bqghd', p_sel.astype(vs.dtype), vs)
        kw = lax.dynamic_slice_in_dim(k_win, start, WINDOW + Q_BLOCK, axis=1)
        vw = lax.dynamic_slice_in_dim(v_win, start, WINDOW + Q_BLOCK, axis=1)
        kpos_w = start - WINDOW + win_off
        dist = tq[:, None] - kpos_w[None, :]
        mask_w = (dist >= 0) & (dist < WINDOW) & (kpos_w[None, :] >= 0)
        s_w = jnp.einsum('bqghd,bkgd->bghqk', qb, kw)
        p_w = masked_softmax(s_w, mask_w)
        o_win = jnp.einsum('bghqk,bkgd->bqghd', p_w.astype(vw.dtype), vw)
        o = gb[..., 0:1] * ocb + gb[..., 1:2] * o_sel + gb[..., 2:3] * o_win
        return o.reshape(B, Q_BLOCK, HD).astype(h.dtype)

    starts = jnp.arange(T // Q_BLOCK) * Q_BLOCK
    o = lax.map(block_step, starts)
    o = o.transpose(1, 0, 2, 3).reshape(B, T, HD)
    return o @ w_out

def first_inputs(seed: int = 0) -> dict:
    key = jax.random.key(seed)
    ks = jax.random.split(key, 32)
    f32 = jnp.float32
    D = D_MODEL
    n = lambda k, shape, s: jax.random.normal(k, shape, f32) * s
    HD = N_HEADS * HEAD_DIM
    return {
        'x': n(ks[0], (BATCH, SEQ, D), 1.0),
        'c': n(ks[1], (BATCH, D), 1.0),
        'ada_w': n(ks[2], (DEPTH, D, 6 * D), D ** -0.5),
        'ada_b': n(ks[3], (DEPTH, 6 * D), 0.05),
        'norm_g': 1.0 + n(ks[4], (DEPTH, 4, D), 0.1),
        'a_w_in': n(ks[5], (N_A_LAYERS, D, 2 * SGU_WIDTH), D ** -0.5),
        'a_ln_g': 1.0 + n(ks[6], (N_A_LAYERS, SGU_WIDTH), 0.1),
        'a_ln_b': n(ks[7], (N_A_LAYERS, SGU_WIDTH), 0.05),
        'a_w_s': n(ks[8], (N_A_LAYERS, SGU_GROUPS, CHUNK, CHUNK), CHUNK ** -0.5),
        'a_b_s': 1.0 + n(ks[9], (N_A_LAYERS, SGU_GROUPS, CHUNK), 0.1),
        'a_w_out': n(ks[10], (N_A_LAYERS, SGU_WIDTH, D), SGU_WIDTH ** -0.5),
        'kv_ada_w': n(ks[11], (D, 2 * D), D ** -0.5),
        'kv_ada_b': n(ks[12], (2 * D,), 0.05),
        'kv_norm_g': 1.0 + n(ks[13], (D,), 0.1),
        'kv_w': n(ks[14], (D, 2 * N_BRANCH * N_KV_HEADS * HEAD_DIM), D ** -0.5),
        'cmp_pos': n(ks[15], (2, CMP_BLOCK, HEAD_DIM), 0.5),
        'cmp_w1': n(ks[16], (2, CMP_BLOCK * HEAD_DIM, CMP_HIDDEN), (CMP_BLOCK * HEAD_DIM) ** -0.5),
        'cmp_b1': n(ks[17], (2, CMP_HIDDEN), 0.05),
        'cmp_w2': n(ks[18], (2, CMP_HIDDEN, HEAD_DIM), CMP_HIDDEN ** -0.5),
        'cmp_b2': n(ks[19], (2, HEAD_DIM), 0.05),
        'b_w_in': n(ks[20], (N_B_LAYERS, D, HD + N_BRANCH * N_HEADS), D ** -0.5),
        'b_w_out': n(ks[21], (N_B_LAYERS, HD, D), HD ** -0.5),
        'ff_w_in': n(ks[22], (DEPTH, D, D_FF), D ** -0.5),
        'ff_w_out': n(ks[23], (DEPTH, D_FF, D), D_FF ** -0.5),
    }

def first_block(x, c, ada_w, ada_b, norm_g, a_w_in, a_ln_g, a_ln_b, a_w_s, a_b_s, a_w_out,
              kv_ada_w, kv_ada_b, kv_norm_g, kv_w, cmp_pos, cmp_w1, cmp_b1, cmp_w2, cmp_b2,
              b_w_in, b_w_out, ff_w_in, ff_w_out):
    c_act = jax.nn.silu(c)
    shared = None
    for layer in range(DEPTH):
        mod = c_act @ ada_w[layer] + ada_b[layer]
        sh1, sc1, g1, sh2, sc2, g2 = jnp.split(mod, 6, axis=-1)
        h = modulate(rms_norm(x, norm_g[layer, 0]), sh1, sc1)
        if layer < N_A_LAYERS:
            y = gmlp_mixer(h, a_w_in[layer], a_ln_g[layer], a_ln_b[layer], a_w_s[layer],
                           a_b_s[layer], a_w_out[layer])
        else:
            if layer == N_A_LAYERS:
                shared = nsa_shared_kv(x, c_act, kv_ada_w, kv_ada_b, kv_norm_g, kv_w,
                                       cmp_pos, cmp_w1, cmp_b1, cmp_w2, cmp_b2)
            j = layer - N_A_LAYERS
            y = nsa_mixer(h, b_w_in[j], b_w_out[j], *shared)
        x = x + g1[:, None, :] * rms_norm(y, norm_g[layer, 1])
        h = modulate(rms_norm(x, norm_g[layer, 2]), sh2, sc2)
        y = jnp.square(jax.nn.relu(h @ ff_w_in[layer])) @ ff_w_out[layer]
        x = x + g2[:, None, :] * rms_norm(y, norm_g[layer, 3])
    return x


DEPTH_2 = 1

GRID_W = 64
CTX_LEN = 256
D_MIX = D_MODEL
GLA_WIDTH = D_MIX // 2
GLA_HEADS = 4
GLA_DV = GLA_WIDTH // GLA_HEADS
GLA_DK = GLA_DV // 2
GLA_QK = GLA_HEADS * GLA_DK
GLA_LOWRANK = 16
GLA_TAU = 16.0
GLA_CHUNK = 64
SC_WIDTH = D_MIX - GLA_WIDTH
D_FF_2 = 2816
EPS = 1e-6

COL_K = 0
COL_V = COL_K + GLA_QK
COL_AF = COL_V + GLA_WIDTH
COL_AB = COL_AF + GLA_LOWRANK
COL_Q = COL_AB + GLA_LOWRANK
COL_OG = COL_Q + GLA_QK
COL_SB = COL_OG + GLA_WIDTH
COL_SC = COL_SB + SC_WIDTH
COL_SX = COL_SC + SC_WIDTH
D_IN = COL_SX + SC_WIDTH


def rmsnorm(x, g):
    xf = x.astype(jnp.float32)
    y = xf * lax.rsqrt(jnp.mean(xf * xf, axis=-1, keepdims=True) + EPS)
    return (y * g.astype(jnp.float32)).astype(x.dtype)

def adaln(cond, w, b):
    return jax.nn.silu(cond) @ w + b

def modulate_2(h, shift, scale):
    return h * (1.0 + scale) + shift

def flip(a):
    return a[:, ::-1]

def gate_logdecay(a_low, w, b):
    a = (a_low @ w + b).astype(jnp.float32)
    return (jax.nn.log_sigmoid(a) / GLA_TAU).reshape(a.shape[0], a.shape[1], GLA_HEADS, GLA_DK)

def gla_inputs(p, w_af, b_af, w_ab, b_ab):
    bsz, t, _ = p.shape
    k = p[..., COL_K:COL_V].reshape(bsz, t, GLA_HEADS, GLA_DK)
    v = p[..., COL_V:COL_AF].reshape(bsz, t, GLA_HEADS, GLA_DV)
    g_f = gate_logdecay(p[..., COL_AF:COL_AB], w_af, b_af)
    g_b = gate_logdecay(p[..., COL_AB:COL_Q], w_ab, b_ab)
    return k, v, g_f, g_b

def gla_final_state(k, v, g):
    b = jnp.cumsum(g.astype(jnp.float32), axis=1)
    w = jnp.exp(b[:, -1:] - b)
    return jnp.einsum('bthk,bthv->bhkv', k.astype(jnp.float32) * w, v.astype(jnp.float32))

def gla_chunked(q, k, v, g, s0, strict):
    bsz, t, h, dk = q.shape
    dv = v.shape[-1]
    n = t // GLA_CHUNK

    def chunks(a):
        a = a.astype(jnp.float32).reshape(bsz, n, GLA_CHUNK, h, a.shape[-1])
        return jnp.moveaxis(a, 1, 0)

    pos = jnp.arange(GLA_CHUNK)
    mask = (pos[None, :] < pos[:, None]) if strict else (pos[None, :] <= pos[:, None])
    mask = mask[None, :, :, None, None]

    def step(s, inp):
        qc, kc, vc, gc = inp
        b = jnp.cumsum(gc, axis=1)
        o_inter = jnp.einsum('bihk,bhkv->bihv', qc * jnp.exp(b), s)
        decay = jnp.exp(jnp.where(mask, b[:, :, None] - b[:, None, :], -jnp.inf))
        att = jnp.einsum('bihk,bjhk,bijhk->bijh', qc, kc, decay)
        o_intra = jnp.einsum('bijh,bjhv->bihv', att, vc)
        b_last = b[:, -1]
        s_new = s * jnp.exp(b_last)[..., None] + jnp.einsum('bjhk,bjhv->bhkv', kc * jnp.exp(b_last[:, None] - b), vc)
        return s_new, o_inter + o_intra

    _, o = lax.scan(step, s0.astype(jnp.float32), (chunks(q), chunks(k), chunks(v), chunks(g)))
    return jnp.moveaxis(o, 0, 1).reshape(bsz, t, h, dv).astype(v.dtype)

def dwconv_row(u, w, b, rows, width):
    bsz, t, ch = u.shape
    up = jnp.pad(u.reshape(bsz, rows, width, ch), ((0, 0), (0, 0), (1, 1), (0, 0)))
    y = w[0] * up[:, :, :-2] + w[1] * up[:, :, 1:-1] + w[2] * up[:, :, 2:] + b
    return y.reshape(bsz, t, ch)

def dwconv_grid(u, w, b, rows, width):
    bsz, t, ch = u.shape
    up = jnp.pad(u.reshape(bsz, rows, width, ch), ((0, 0), (1, 1), (1, 1), (0, 0)))
    y = b
    for dr in range(3):
        for dc in range(3):
            y = y + w[dr, dc] * up[:, dr:dr + rows, dc:dc + width]
    return y.reshape(bsz, t, ch)

def token_mixers(p, s_f, s_b, rows, width, w_af, b_af, w_ab, b_ab, g_head, w_sc, b_sc):
    bsz, t, _ = p.shape
    k, v, g_f, g_b = gla_inputs(p, w_af, b_af, w_ab, b_ab)
    q = p[..., COL_Q:COL_OG].reshape(bsz, t, GLA_HEADS, GLA_DK) * (GLA_DK ** -0.5)
    og = p[..., COL_OG:COL_SB]
    o_f = gla_chunked(q, k, v, g_f, s_f, False)
    o_b = flip(gla_chunked(flip(q), flip(k), flip(v), flip(g_b), s_b, True))
    o_gla = rmsnorm(o_f + o_b, g_head).reshape(bsz, t, GLA_WIDTH) * jax.nn.silu(og)
    sb = p[..., COL_SB:COL_SC]
    sc = p[..., COL_SC:COL_SX]
    sx = p[..., COL_SX:D_IN]
    o_sc = sb * dwconv_row(sc * sx, w_sc, b_sc, rows, width)
    return jnp.concatenate([o_gla, o_sc], axis=-1)

def conv_ffn(h, rows, width, w_up, w_cf, b_cf, w_down):
    u, gate = jnp.split(h @ w_up, 2, axis=-1)
    u = dwconv_grid(u, w_cf, b_cf, rows, width)
    return (jax.nn.silu(u) * gate) @ w_down

def second_inputs(seed: int = 0) -> dict:
    key = jax.random.key(seed)
    ks = jax.random.split(key, 24)

    def nrm(k, shape, s):
        return jax.random.normal(k, shape, jnp.float32) * s

    L = DEPTH_2
    return {
        'x': nrm(ks[0], (BATCH, SEQ, D_MODEL), 1.0),
        'c': nrm(ks[1], (BATCH, D_MODEL), 1.0),
        'ctx': nrm(ks[2], (BATCH, CTX_LEN, D_MODEL), 1.0),
        'c_ctx': nrm(ks[3], (D_MODEL,), 1.0),
        'w_ada': nrm(ks[4], (L, D_MODEL, 6 * D_MODEL), D_MODEL ** -0.5),
        'b_ada': nrm(ks[5], (L, 6 * D_MODEL), 0.01),
        'g_pre_mix': 1.0 + nrm(ks[6], (L, D_MODEL), 0.05),
        'g_post_mix': 1.0 + nrm(ks[7], (L, D_MODEL), 0.05),
        'g_pre_ffn': 1.0 + nrm(ks[8], (L, D_MODEL), 0.05),
        'g_post_ffn': 1.0 + nrm(ks[9], (L, D_MODEL), 0.05),
        'w_in': nrm(ks[10], (L, D_MODEL, D_IN), D_MODEL ** -0.5),
        'w_af': nrm(ks[11], (L, GLA_LOWRANK, GLA_QK), GLA_LOWRANK ** -0.5),
        'b_af': nrm(ks[12], (L, GLA_QK), 0.1),
        'w_ab': nrm(ks[13], (L, GLA_LOWRANK, GLA_QK), GLA_LOWRANK ** -0.5),
        'b_ab': nrm(ks[14], (L, GLA_QK), 0.1),
        'g_head': 1.0 + nrm(ks[15], (L, GLA_DV), 0.05),
        'w_sc': nrm(ks[16], (L, 3, SC_WIDTH), 0.5),
        'b_sc': nrm(ks[17], (L, SC_WIDTH), 0.01),
        'w_out': nrm(ks[18], (L, D_MIX, D_MODEL), D_MIX ** -0.5),
        'w_up': nrm(ks[19], (L, D_MODEL, 2 * D_FF_2), D_MODEL ** -0.5),
        'w_cf': nrm(ks[20], (L, 3, 3, D_FF_2), 1.0 / 3.0),
        'b_cf': nrm(ks[21], (L, D_FF_2), 0.01),
        'w_down': nrm(ks[22], (L, D_FF_2, D_MODEL), D_FF_2 ** -0.5),
    }

def second_block(x, c, ctx, c_ctx, w_ada, b_ada, g_pre_mix, g_post_mix, g_pre_ffn, g_post_ffn,
              w_in, w_af, b_af, w_ab, b_ab, g_head, w_sc, b_sc, w_out, w_up, w_cf, b_cf, w_down):
    rows = x.shape[1] // GRID_W
    ctx_len = ctx.shape[1]
    for i in range(DEPTH_2):
        update_ctx = i + 1 < DEPTH_2
        sh1, sc1, gt1, sh2, sc2, gt2 = jnp.split(adaln(c, w_ada[i], b_ada[i])[:, None, :], 6, axis=-1)
        csh1, csc1, cgt1, csh2, csc2, cgt2 = jnp.split(adaln(c_ctx, w_ada[i], b_ada[i]), 6, axis=-1)
        gla_p = (w_af[i], b_af[i], w_ab[i], b_ab[i])

        hc = modulate_2(rmsnorm(ctx, g_pre_mix[i]), csh1, csc1)
        pc = hc @ (w_in[i] if update_ctx else w_in[i][:, :COL_Q])
        kc, vc, gfc, gbc = gla_inputs(pc, *gla_p)
        s_f = gla_final_state(kc, vc, gfc)
        s_b = gla_final_state(flip(kc), flip(vc), flip(gbc))

        hx = modulate_2(rmsnorm(x, g_pre_mix[i]), sh1, sc1)
        yx = token_mixers(hx @ w_in[i], s_f, s_b, rows, GRID_W, *gla_p, g_head[i], w_sc[i], b_sc[i])
        x = x + gt1 * rmsnorm(yx @ w_out[i], g_post_mix[i])

        hx = modulate_2(rmsnorm(x, g_pre_ffn[i]), sh2, sc2)
        x = x + gt2 * rmsnorm(conv_ffn(hx, rows, GRID_W, w_up[i], w_cf[i], b_cf[i], w_down[i]), g_post_ffn[i])

        if update_ctx:
            zero_state = jnp.zeros_like(s_f)
            yc = token_mixers(pc, zero_state, zero_state, 1, ctx_len, *gla_p, g_head[i], w_sc[i], b_sc[i])
            ctx = ctx + cgt1 * rmsnorm(yc @ w_out[i], g_post_mix[i])
            hc = modulate_2(rmsnorm(ctx, g_pre_ffn[i]), csh2, csc2)
            ctx = ctx + cgt2 * rmsnorm(conv_ffn(hc, 1, ctx_len, w_up[i], w_cf[i], b_cf[i], w_down[i]), g_post_ffn[i])
    return x


def setup_inputs(seed=0):
    out = dict(first_inputs(seed))
    for name, value in second_inputs(seed + 1).items():
        if name != "x":
            out[name + "_2"] = value
    return out


def reference(
    x, c, ada_w, ada_b, norm_g, a_w_in, a_ln_g, a_ln_b, a_w_s, a_b_s, a_w_out, kv_ada_w,
    kv_ada_b, kv_norm_g, kv_w, cmp_pos, cmp_w1, cmp_b1, cmp_w2, cmp_b2, b_w_in, b_w_out,
    ff_w_in, ff_w_out, c_2, ctx_2, c_ctx_2, w_ada_2, b_ada_2, g_pre_mix_2, g_post_mix_2,
    g_pre_ffn_2, g_post_ffn_2, w_in_2, w_af_2, b_af_2, w_ab_2, b_ab_2, g_head_2, w_sc_2, b_sc_2,
    w_out_2, w_up_2, w_cf_2, b_cf_2, w_down_2,
):
    x = first_block(
        x, c, ada_w, ada_b, norm_g, a_w_in, a_ln_g, a_ln_b, a_w_s, a_b_s, a_w_out, kv_ada_w,
        kv_ada_b, kv_norm_g, kv_w, cmp_pos, cmp_w1, cmp_b1, cmp_w2, cmp_b2, b_w_in, b_w_out,
        ff_w_in, ff_w_out,
    )
    return second_block(
        x, c_2, ctx_2, c_ctx_2, w_ada_2, b_ada_2, g_pre_mix_2, g_post_mix_2, g_pre_ffn_2,
        g_post_ffn_2, w_in_2, w_af_2, b_af_2, w_ab_2, b_ab_2, g_head_2, w_sc_2, b_sc_2, w_out_2,
        w_up_2, w_cf_2, b_cf_2, w_down_2,
    )


_drawn_inputs = setup_inputs


def setup_inputs(seed=0):
    import zlib

    import numpy as np

    out = dict(_drawn_inputs(seed))
    spreads = {}
    factors = {'a_ln_b': 3.484,
     'cmp_b1': 5.343,
     'cmp_b2': 3.077,
     'ctx_2': 3.372,
     'b_ada_2': 4.681,
     'g_post_mix_2': 3.356,
     'g_post_ffn_2': 3.361,
     'b_af_2': 5.338,
     'b_ab_2': 5.387,
     'g_head_2': 8.0,
     'b_sc_2': 32.502,
     'b_cf_2': 8.0}
    for name, (base, spread) in spreads.items():
        noise = np.random.default_rng([zlib.crc32(name.encode()), seed]).standard_normal(out[name].shape)
        drawn = base * np.exp(spread * noise) if base else spread * noise
        out[name] = jnp.asarray(drawn.astype(out[name].dtype))
    for name, factor in factors.items():
        out[name] = (out[name] * factor).astype(out[name].dtype)
    return out
```

```python
import concourse.bass as bass
from concourse import mybir

F32 = mybir.dt.float32
F32R = mybir.dt.float32r
BF16 = mybir.dt.bfloat16
I8 = mybir.dt.int8
ALU = mybir.AluOpType
ACT = mybir.ActivationFunctionType
AX = mybir.AxisListType

P = 128
T = 256
D = 1024
KT = D // P
EPS = 1e-6
NEG = -1e30
CH = 2048
RAW = 6
SPL = 3
MID = 3

STAGES = ["x", "gmlp", "ffn0", "attn", "ffn1", "gla", "ffn2"]


class Plan:

    def __init__(self):
        self.src, self.kind, self.order = [], [], []
        self.nm, self.na, self.um, self.ua = [], [], [], []
        self.width = []
        self.u = 0

    def m(self, src, mids=1, width=CH):
        self.nm.append(len(self.src))
        self.um.append(self.u)
        self.u += mids
        self.kind.append("M")
        self.order.append(len(self.nm) - 1)
        self.width.append(width)
        self.src.append(src)
        return len(self.nm) - 1

    def a(self, src):
        self.na.append(len(self.src))
        self.ua.append(self.u)
        self.u += 1
        self.kind.append("A")
        self.order.append(len(self.na) - 1)
        self.src.append(src)


def cols(w, c0, n=256):
    return w.rearrange("(k p) n -> p k n", p=P)[:, :, c0:c0 + n]


def rows(w, r0, n=2):
    return w.rearrange("(k p) n -> p k n", p=P)[:, r0:r0 + n, :]


def build(nc, I, out, upto="ffn2"):
    stage_n = STAGES.index(upto)

    def has(s):
        return stage_n >= STAGES.index(s)

    pl = Plan()
    ada = {0: I["ada_w"][0], 1: I["ada_w"][1], 2: I["w_ada_2"][0], "kv": I["kv_ada_w"]}
    BATCH = [(0, 0), (0, 1), (0, 2), (1, 0), ("kv", 0), (1, 1), (1, 2), (2, 0), (2, 1), (2, 2)]
    B0SH, B0G, B0SC, B1SH, BKV, B1G, B1SC, B2SH, B2G, B2SC = range(10)

    def ada_half(b, half):
        w, third = BATCH[b]
        for j in range(4 * half, 4 * half + 4):
            pl.a(cols(ada[w], 2048 * third + 256 * j))

    def ada_batch(b):
        ada_half(b, 0)
        ada_half(b, 1)

    ada_batch(B0SH)
    if has("gmlp"):
        M_V = [pl.m(cols(I["a_w_in"][0], 1024 + 256 * j)) for j in range(4)]
        M_U = [pl.m(cols(I["a_w_in"][0], 256 * j)) for j in range(4)]
        ada_batch(B0G)
        ada_batch(B0SC)
        M_AO = [pl.m(cols(I["a_w_out"][0], 256 * j), 0) for j in range(4)]
    M_FF = {}
    if has("ffn0"):
        ada_batch(B1SH)

    def ffn_chunks(f):
        m0 = pl.m(cols(I["ff_w_in"][f], 0))
        for c in range(15):
            pl.m(cols(I["ff_w_in"][f], 256 * (c + 1)))
            pl.m(rows(I["ff_w_out"][f], 2 * c), 0)
        pl.m(rows(I["ff_w_out"][f], 30), 0)
        M_FF[f] = m0

    if has("ffn0"):
        ffn_chunks(0)
    if has("attn"):
        ada_batch(BKV)
        M_KC, M_VC, M_KS, M_KW, M_VS, M_VW = [pl.m(cols(I["kv_w"], 256 * j)) for j in (0, 1, 2, 4, 3, 5)]
        M_CW, M_Q = [], []
        for j in range(2):
            M_CW.append([pl.m(rows(I["cmp_w1"][j], 8 * c, 8), 0) for c in range(2)])
            M_Q += [pl.m(cols(I["b_w_in"][0], 512 * j + 256 * c)) for c in range(2)]
        M_GT = pl.m(cols(I["b_w_in"][0], 1024, 48), 1, 384)
        ada_batch(B1G)
        M_BO = [pl.m(cols(I["b_w_out"][0], 256 * j), 0) for j in range(4)]
    if has("ffn1"):
        ada_batch(B1SC)
        ffn_chunks(1)
    if has("gla"):
        ada_batch(B2SH)
        w2 = I["w_in_2"][0]
        M_K2 = pl.m(cols(w2, 0), 2)
        M_V2 = [pl.m(cols(w2, 256 + 256 * j), 2) for j in range(2)]
        M_AL = pl.m(cols(w2, 768, 128), 2, 1024)
        M_Q2 = pl.m(cols(w2, 800))
        M_OG = [pl.m(cols(w2, 1056 + 256 * j)) for j in range(2)]
        M_SC = [pl.m(cols(w2, 2080 + 256 * j)) for j in range(2)]
        M_SX = [pl.m(cols(w2, 2592 + 256 * j)) for j in range(2)]
        M_SB = [pl.m(cols(w2, 1568 + 256 * j)) for j in range(2)]
        ada_batch(B2G)
        M_WO = [pl.m(cols(I["w_out_2"][0], 256 * j), 0) for j in range(4)]
    if has("ffn2"):
        ada_batch(B2SC)
        wup, wdn = I["w_up_2"][0], I["w_down_2"][0]
        M_UP = pl.m(cols(wup, 0), 0)
        pl.m(cols(wup, 2816), 0)
        for c in range(10):
            pl.m(cols(wup, 256 * (c + 1)), 0)
            pl.m(cols(wup, 2816 + 256 * (c + 1)), 0)
            pl.m(rows(wdn, 2 * c), 0)
        pl.m(rows(wdn, 20), 0)
    NM, NN = len(pl.nm), len(pl.src)

    at = [16512]

    def take(nbytes):
        o = at[0]
        at[0] += (nbytes + 31) // 32 * 32
        return o

    def sb(name, shape, dt=F32, off=None):
        size = 1
        for s in shape[1:]:
            size *= s
        size *= {F32: 4, F32R: 4, BF16: 2, I8: 1}[dt]
        return nc.alloc_sbuf_tensor_at(name, shape, dt, offset=take(size) if off is None else off)

    raw = sb("raw", [P, RAW, CH])
    whi = sb("whi", [P, SPL, CH], F32R)
    wlo = sb("wlo", [P, SPL, CH], F32R)
    x = sb("x", [P, KT, T])
    hh = sb("hh", [P, KT, T], F32R)
    hl = sb("hl", [P, KT, T], F32R)
    oK = take(16384)
    gh = sb("gh", [P, KT, T], F32R, oK)
    gl = sb("gl", [P, KT, T], F32R, oK + 8192)
    oS = take(24576)
    sq = sb("sq", [P, KT, T], F32, oS)
    tt_ = sb("tt_", [P, KT, T], F32, oS + 8192)
    h32 = sb("h32", [P, KT, T], F32, oS + 16384)
    ident = sb("ident", [P, P])
    onesm = sb("onesm", [P, P])
    one1 = sb("one1", [P, 256])
    eps = sb("eps", [P, 1])
    zb = sb("zb", [P, 512], BF16)
    NV = [96, 107, 99, 99, 112, 48]
    V0 = [sum(NV[:i]) for i in range(7)]
    vec = sb("vec", [P, V0[6]])
    mod = sb("mod", [P, 11, 16])
    coef = sb("coef", [P, 14, KT])
    csil = sb("csil", [P, 24])
    cpad = sb("cpad", [P, 2, KT, 32])
    stage = sb("stage", [P, 4, 256])
    G = sb("G", [16, 2, 4, P])
    Gc = sb("Gc", [16, 4, P])
    vv = sb("vv", [P, T])
    lnv = sb("lnv", [P, T])
    r0 = sb("r0", [P, T])
    n1 = sb("n1", [P, T])
    rs = sb("rs", [P, T])
    oP = at[0]
    LIMIT = 229368

    def region(base, end):
        pos = [base]

        def f(name, shape, dt=F32):
            size = 1
            for s in shape[1:]:
                size *= s
            size *= {F32: 4, F32R: 4, BF16: 2, I8: 1}[dt]
            o = pos[0]
            pos[0] += (size + 31) // 32 * 32
            assert pos[0] <= end, (name, pos[0], end)
            return nc.alloc_sbuf_tensor_at(name, shape, dt, offset=o)

        return f

    r = region(oP, LIMIT)
    wT = r("wT", [P, 8, P])
    bs_b = r("bs_b", [P, 8, P])
    lng = r("lng", [P, D])
    lnb = r("lnb", [P, D])
    ws = r("ws", [P, 8, P])
    bst = r("bst", [P, 2, 2, 6])
    mv = r("mv", [P, 2, 2])
    lr = r("lr", [P, 4, 2])
    rK = region(oK, oK + 16384)
    v_tm = rK("v_tm", [P, 2, D])
    u_fm = rK("u_fm", [P, KT, T])
    x_tm = sb("x_tm", [P, 2, D], F32, oS + 8192)
    vrow = sb("vrow", [P, 6, P], F32, oS + 16384)
    r = region(oP, LIMIT)
    fr = r("fr", [P, 512])
    fm = r("fm", [P, 512])
    fhi = r("fhi", [P, 3, 512], F32R)
    flo = r("flo", [P, 3, 512], F32R)
    y_tm = sb("y_tm", [P, 2, D], F32, oS + 8192)

    NC, NCP, HD, NG, NH = 15, 16, 64, 4, 16
    r = region(oP, LIMIT)
    kc = r("kc", [P, NG, NCP + T])
    kw = r("kw", [P, NG, T])
    v_s = r("v_s", [P, 2, NG * HD])
    v_w = r("v_w", [P, 2, NG * HD])
    ks_fm = r("ks_fm", [P, 2, T])
    kw_fm = r("kw_fm", [P, 2, T])
    cmask = r("cmask", [P, T])
    cmm = r("cmm", [P, 2, NCP])
    cm01 = r("cm01", [P, 2, NCP])
    gate = r("gate", [P, 2, 48])
    hid = r("hid", [P, 2, 2, 60])
    w2k = r("w2k", [P, 2, P])
    w2v = r("w2v", [P, 2, HD])
    b2k = r("b2k", [P, 1])
    b2v = r("b2v", [NCP, HD])
    vcs = r("vcs", [NCP, NG, HD])
    mx = r("mx", [P, 2, 6])
    nb = r("nb", [P, 2, 6])
    den = r("den", [P, 2, 6])
    rec = r("rec", [P, 2, 6])
    cf = r("cf", [P, 2, 6])
    qT = sb("qT", [P, KT, T], F32, oK)
    pp = sb("pp", [P, 2, 800], F32, oK + 8192)
    bsh = [sb(f"bsh{j}", [P, NG, T], F32, oS + 8192 + 4096 * j) for j in range(2)]
    pts = sb("pts", [P, 2, 1024], F32, oS + 8192)
    rS = region(oS + 16384, oS + 24576)
    blk = rS("blk", [P, 16, NG, NC])
    kc_fm = rS("kc_fm", [P, 2, T])
    vc_fm = rS("vc_fm", [P, 2, T])
    rS = region(oS, oS + 8192)
    bhi = rS("bhi", [P, 16, 60], F32R)
    blo = rS("blo", [P, 16, 60], F32R)

    GHD = 4
    r = region(oP, LIMIT)
    qk = r("qk", [P, 4, T])
    kctx = r("kctx", [P, 2, T])
    o_v = oP + 6144
    vx = r("vx", [P, 2, 512])
    vctx = r("vctx", [P, 2, 512])
    cx = sb("cx", [P, KT, T], F32, o_v)
    alx = r("alx", [33, T])
    alc = r("alc", [33, T])
    wab = r("wab", [33, 512])
    st = r("st", [P, 2, 2, P])
    trif = r("trif", [P, P])
    trib = r("trib", [P, P])
    lmask = r("lmask", [P, 7, P], I8)
    tot = r("tot", [P, 2])
    ctx_tm = sb("ctx_tm", [P, 2, D], F32, oK)
    rK = region(oK, oK + 16384)
    gc = rK("gc", [P, 2, 512])
    wc = rK("wc", [P, 2, 512])
    gx = rK("gx", [P, 4, T])
    bx = rK("bx", [P, 4, T])
    a_x = sb("a_x", [P, 2, 2, 2, P], F32, oK)
    a_d = sb("a_d", [P, 2, 2, 2, P], F32, oK + 4096)
    qi = sb("qi", [P, 4, T], F32, oK + 8192)
    ln4 = sb("ln4", [P, 4, T], F32, oK)
    r4 = sb("r4", [P, 4, T], F32, oK + 4096)
    v4 = sb("v4", [P, 4, T], F32, oK + 8192)
    n4 = sb("n4", [P, 4, T], F32, oK + 12288)
    rS = region(oS, oS + 24576)
    og = rS("og", [P, 4, T])
    sbt = rS("sbt", [P, 4, T])
    ct = rS("ct", [P, 4, T])
    sct = rS("sct", [P, 4, T])
    eb = rS("eb", [P, 2, 4, T])
    o2 = sb("o2", [P, 4, T], F32, oS + 16384)
    o4 = sb("o4", [P, 4, T], F32, oS + 20480)

    CF = I["w_down_2"].shape[1] // 256
    r = region(oP, LIMIT)
    ut = r("ut", [P, 2, T])
    cvt = r("cvt", [P, 2, T])
    sl = r("sl", [P, 2, T])
    fa = r("fa", [P, 2, T])
    chi = r("chi", [P, 2, 512], F32R)
    clo = r("clo", [P, 2, 512], F32R)

    ps = [nc.alloc_psum_tensor(f"bank{i}", [P, 512], F32) for i in range(8)]
    stat = ps[7][:, 0:256]
    small = ps[7][:, 256:272]
    smallc = ps[7][:, 272:288]

    sems = {}

    def sem(name):
        if name not in sems:
            sems[name] = nc.alloc_semaphore(name)
        return sems[name]

    raw_full = [sem(f"raw_full{i}") for i in range(RAW)]
    s_hi, s_lo, s_mm = sem("hi_ready"), sem("lo_ready"), sem("chunk_multiplied")
    s_ada = sem("ada_multiplied")
    s_mid = sem("mid_evacuated")

    def vc(tile, row):
        return V0[tile] + row

    C_NORM = [[vc(0, 24 + 8 * (4 * l + i)) for i in range(4)] for l in range(2)]
    C_KVN = vc(0, 88)
    C_PREMIX, C_POSTMIX, C_PREFFN, C_POSTFFN = (vc(1, 8 * i) for i in range(4))
    C_BSC, C_WSC, C_BCF, C_B1, C_GH, C_POS = vc(1, 32), vc(1, 36), vc(1, 48), vc(1, 70), vc(1, 74), vc(1, 75)
    C_WCF = V0[2]
    C_ADAB = V0[4]
    BIAS = [C_ADAB + {0: 0, 1: 48, "kv": 96, 2: 112}[w] + 16 * t for w, t in BATCH]

    (A_N0, G_N1, A_N2, G_N3, A_KV, A_N4, G_N5, A_N6, G_N7, A_N8, A_N9, G_N10, A_N11, G_N12) = range(14)
    SH = lambda b: mod[:, b, 0:8]
    SC = lambda b: mod[:, b, 8:16]
    COEFS = {
        B0SH: [(A_N0, "A", SC(B0SH), C_NORM[0][0])],
        B0G: [(G_N1, "G", SH(B0G), C_NORM[0][1])],
        B0SC: [(A_N2, "A", SH(B0SC), C_NORM[0][2]), (G_N3, "G", SC(B0SC), C_NORM[0][3])],
        B1SH: [(A_N4, "A", SC(B1SH), C_NORM[1][0])],
        BKV: [(A_KV, "A", SC(BKV), C_KVN)],
        B1G: [(G_N5, "G", SH(B1G), C_NORM[1][1])],
        B1SC: [(A_N6, "A", SH(B1SC), C_NORM[1][2]), (G_N7, "G", SC(B1SC), C_NORM[1][3])],
        B2SH: [(A_N8, "A", SC(B2SH), C_PREMIX), (A_N9, "A", SC(10), C_PREMIX)],
        B2G: [(G_N10, "G", SH(B2G), C_POSTMIX)],
        B2SC: [(A_N11, "A", SH(B2SC), C_PREFFN), (G_N12, "G", SC(B2SC), C_POSTFFN)],
    }

    s_vrow, s_x0, s_gm = sem("vec_rows_loaded"), sem("x_loaded"), sem("gmlp_rows_loaded")
    s_const, s_cpad0 = sem("constants_ready"), sem("cpad_zeroed")
    s_vT, s_vec = sem("vec_transposed"), sem("vec_ready")
    s_sg, s_cp = sem("c_silu"), sem("c_padded")
    s_xT, s_x = sem("x_transposed"), sem("x_ready")
    s_stage, s_G = sem("ada_rows_staged"), sem("ada_rows_gathered")
    s_fin, s_mod = sem("ada_columns_summed"), sem("mod_ready")
    s_sq, s_stat, s_r0, s_rs = sem("squares"), sem("mean_square"), sem("rsqrt_guess"), sem("rsqrt_ready")
    s_ln = sem("mean_square_logged")
    s_t, s_h32, s_h = sem("normed"), sem("shifted"), sem("h_split")
    s_yfree = sem("y_banks_free")
    s_vln, s_lnr, s_vn = sem("v_variance"), sem("v_rsqrt_guess"), sem("v_normed")
    s_wsT, s_wTc, s_wT = sem("ws_transposed"), sem("ws_copied"), sem("ws_masked")
    s_mix, s_oa = sem("mixed"), sem("gmlp_out_split")
    s_fsq, s_fh, s_fact = sem("ffn_squared"), sem("ffn_hi"), sem("ffn_act_ready")
    s_oT, s_oc, s_out = sem("out_transposed"), sem("out_copied"), sem("out_stored")
    s_bsh = [sem("k_cmp_shifted"), sem("v_cmp_shifted")]
    s_kcp, s_asm, s_aw = sem("keys_doubled"), sem("attention_masks_ready"), sem("cmp_weights_loaded")
    s_blk, s_hid, s_w2, s_kv = sem("cmp_blocks_split"), sem("cmp_hidden"), sem("cmp_second"), sem("keys_values_ready")
    s_gt = sem("gates_ready")
    s_S, s_Sev, s_nb, s_exp, s_p = sem("scores"), sem("scores_evacuated"), sem("max_ready"), sem("exp_done"), sem("probs_ready")
    s_T, s_Tev, s_TevD, s_O, s_oev, s_oh = (sem("probs_transposed"), sem("sel_probs_copied"), sem("win_probs_copied"),
                                            sem("heads_done"), sem("pairs_evacuated"), sem("pairs_split"))
    s_ctx, s_cT, s_cx = sem("ctx_loaded"), sem("ctx_transposed"), sem("ctx_ready")
    s_wz, s_wab, s_al, s_gm3 = sem("gate_weights_zeroed"), sem("gate_weights_loaded"), sem("gate_rows_ready"), sem("gla_masks_ready")
    s_gp, s_la, s_g = sem("gates_multiplied"), sem("gates_logged"), sem("log_decays_ready")
    s_cum, s_wc, s_kd, s_st, s_ste = (sem("decays_summed"), sem("decays_to_end"), sem("ctx_keys_decayed"),
                                      sem("states_multiplied"), sem("states_ready"))
    s_qev, s_vev, s_B, s_qe, s_qi = (sem("q_k_ready"), sem("v_ready"), sem("decays_cumulated"), sem("state_decays"),
                                     sem("q_for_states"))
    s_D, s_Ex, s_E, s_lev, s_A = (sem("level_differences"), sem("level_decays"), sem("level_operands"),
                                  sem("level_multiplied"), sem("attention_filled"))
    s_og, s_sc, s_sx, s_sb, s_cv = sem("out_gate"), sem("sc_ready"), sem("sx_ready"), sem("sb_ready"), sem("conv_split")
    s_o4, s_o2, s_ms4, s_l4, s_r4, s_gs = (sem("gla_heads_done"), sem("gla_squares"), sem("gla_mean_squares"),
                                     sem("gla_mean_squares_logged"), sem("gla_rsqrt_guess"), sem("gla_out_split"))
    s_ue, s_tap, s_sil, s_fa, s_chi, s_cact = (sem("conv_input_ready"), sem("taps_added"), sem("conv_silu"),
                                               sem("conv_gated"), sem("conv_hi"), sem("conv_act_ready"))
    d_ch, a_ch, g_ch = sem("vector_chain"), sem("scalar_chain"), sem("gpsimd_chain")

    def G_after(b, half=1):
        n = 2 * b + half + 1
        return 64 * n + 64 * (max(0, min(2, n - 2 * B2SH)))

    N_UPD = [0, 1, 2, 3, 4, 5, 6][stage_n]
    def part(qt, br):
        nk = P * (qt + 1)
        at0 = 0 if qt == 0 else NCP + 2 * P
        lo_, n = [(0, NCP), (NCP, nk), (NCP + nk, nk)][br]
        return slice(at0 + lo_, at0 + lo_ + n)

    def score_psum(qt, br):
        nk = P * (qt + 1)
        if qt == 0:
            return ps[0][:, part(0, br)]
        return ps[2][:, 0:T] if br == 2 else ps[1][:, [slice(0, NCP), slice(NCP, NCP + T)][br]]

    block = nc.Block()
    with block:

        def full(eng, n, i=0, per=1):
            eng.wait_ge(raw_full[n % RAW], 16 * (n // RAW + 1) + 16 * i)

        @block.sync
        def _(sp):
            x_rows = I["x"][0].rearrange("(t p) d -> p t d", p=P)

            def load(n, i=0, src=None, freed=None):
                if freed is None and n >= RAW:
                    k = pl.order[n - RAW]
                    if pl.kind[n - RAW] == "M":
                        sp.wait_ge(s_lo, k + 1)
                    else:
                        sp.wait_ge(s_ada, k + 1)
                elif freed is not None:
                    sp.wait_ge(s_lo, freed)
                s = pl.src[n] if src is None else src
                k, w = s.shape[1], s.shape[2]
                sp.dma_start(raw[:, n % RAW, 0:k * w].rearrange("p (k n) -> p k n", n=w), s)\
                  .then_inc(raw_full[n % RAW], 16)

            def ffn_loads(f):
                m0 = M_FF[f]
                n0 = pl.nm[m0]
                for n in range(n0, n0 + 7):
                    load(n)
                win = I["ff_w_in"][f].rearrange("(k p) n -> p k n", p=P)
                wout = I["ff_w_out"][f].rearrange("(k p) n -> p k n", p=P)
                with sp.Fori(1, 5) as i:
                    for j in range(3):
                        load(n0 + 1 + 2 * j, src=win[:, :, bass.ds(768 * i + 256 * (j + 1), 256)],
                             freed=m0 + 1 + 2 * j - 6 + 6 * i + 1)
                        load(n0 + 2 + 2 * j, src=wout[:, bass.ds(6 * i + 2 * j, 2), :],
                             freed=m0 + 2 + 2 * j - 6 + 6 * i + 1)
                load(n0 + 31)
                return n0 + 32

            def conv_loads():
                n0 = pl.nm[M_UP]
                for n in range(n0, n0 + 8):
                    load(n)
                wup_ = wup.rearrange("(k p) n -> p k n", p=P)
                wdn_ = wdn.rearrange("(k p) n -> p k n", p=P)
                ff2 = 256 * CF
                with sp.Fori(0, 4) as i:
                    for j in range(2):
                        c = 2 + j
                        for k, src in enumerate((wup_[:, :, bass.ds(512 * i + 256 * (c + 1), 256)],
                                                 wup_[:, :, bass.ds(512 * i + ff2 + 256 * (c + 1), 256)],
                                                 wdn_[:, bass.ds(4 * i + 2 * c, 2), :])):
                            m = 3 * c + 2 + k
                            load(n0 + m, src=src, freed=M_UP + m - 6 + 1 + 6 * i)
                load(n0 + 32)
                return n0 + 33

            sp.dma_start(x_tm[:, :, :], x_rows).then_inc(s_x0, 16)
            n = 0
            while n < NN:
                if pl.kind[n] == "M" and pl.order[n] in M_FF.values():
                    f = [k for k in M_FF if M_FF[k] == pl.order[n]][0]
                    n = ffn_loads(f)
                elif has("ffn2") and n == pl.nm[M_UP]:
                    n = conv_loads()
                else:
                    load(n)
                    n += 1
            sp.wait_ge(s_oc, 4)
            sp.dma_start(out[0].rearrange("(t p) d -> p t d", p=P), y_tm[:, :, :]).then_inc(s_out, 16)
            sp.wait_ge(s_out, 16)

        @block.scalar
        def _(act):
            chain = [0]

            def link(ins):
                ins.then_inc(a_ch, 1)
                chain[0] += 1
                act.wait_ge(a_ch, chain[0])

            def load_rows(tile, row, src):
                n = src.shape[0]
                act.dma_start(vrow[row:row + n, tile, :], src).then_inc(s_vrow, 16)

            v8 = lambda a: a.rearrange("(r p) -> r p", p=P)
            load_rows(0, 0, v8(I["c"][0]))
            load_rows(0, 8, v8(I["c_2"][0]))
            load_rows(0, 16, v8(I["c_ctx_2"]))
            load_rows(0, 24, I["norm_g"].rearrange("l i (r p) -> (l i r) p", p=P))
            load_rows(0, 88, v8(I["kv_norm_g"]))
            load_rows(4, 0, I["ada_b"].rearrange("l (r p) -> (l r) p", p=P))
            load_rows(4, 96, v8(I["kv_ada_b"]))
            load_rows(1, 0, v8(I["g_pre_mix_2"][0]))
            load_rows(1, 8, v8(I["g_post_mix_2"][0]))
            load_rows(1, 16, v8(I["g_pre_ffn_2"][0]))
            load_rows(1, 24, v8(I["g_post_ffn_2"][0]))
            load_rows(1, 32, v8(I["b_sc_2"][0]))
            load_rows(1, 36, I["w_sc_2"][0].rearrange("w (r p) -> (w r) p", p=P))
            load_rows(1, 48, v8(I["b_cf_2"][0]))
            load_rows(1, 70, I["cmp_b1"].rearrange("j (r p) -> (j r) p", p=P))
            load_rows(1, 74, I["g_head_2"])
            load_rows(1, 75, I["cmp_pos"].rearrange("j (r a) d -> (j r) (a d)", a=2))
            wcf = I["w_cf_2"][0].rearrange("a b (r p) -> (a b r) p", p=P)
            load_rows(2, 0, wcf[0:99, :])
            load_rows(3, 0, wcf[99:198, :])
            load_rows(5, 0, v8(I["b_ada_2"][0]))
            act.dma_start(ws[:, :, :], I["a_w_s"][0].rearrange("g t s -> t g s")).then_inc(s_gm, 16)
            act.dma_start(bs_b[:, :, :], I["a_b_s"][0:1].broadcast_to([P, 8, P])).then_inc(s_gm, 16)
            act.dma_start(lng[:, :], I["a_ln_g"][0:1].broadcast_to([P, D])).then_inc(s_gm, 16)
            act.dma_start(lnb[:, :], I["a_ln_b"][0:1].broadcast_to([P, D])).then_inc(s_gm, 16)

            act.wait_ge(s_vec, 1)
            act.activation(csil[:, :], vec[:, 0:24], ACT.Silu).then_inc(s_sg, 1)

            split_next = [0]

            def hi(m, i=0):
                full(act, pl.nm[m], i)
                if m >= SPL:
                    act.wait_ge(s_mm, m - SPL + 1 + 6 * i)
                w = pl.width[m]
                act.activation(whi[:, m % SPL, 0:w], raw[:, pl.nm[m] % RAW, 0:w], ACT.Copy).then_inc(s_hi, 1)

            def splits(upto_m):
                while split_next[0] < min(upto_m, NM):
                    hi(split_next[0])
                    split_next[0] += 1

            def ada_rows(b, half):
                for j in range(4):
                    a = 8 * b + 4 * half + j
                    u = pl.ua[a]
                    act.wait_ge(s_ada, a + 1)
                    if j == 0 and (b or half):
                        act.wait_ge(s_G, G_after(b, half - 1) if half else G_after(b - 1))
                    act.activation(stage[:, j, :], ps[4 + u % MID][:, 0:256], ACT.Copy).then_inc(s_mid, 1)
                act.wait_ge(s_mid, pl.ua[8 * b + 4 * half + 3] + 1)
                if b >= 2:
                    act.wait_ge(s_fin, b - 1)
                for g in range(4):
                    src = stage[32 * g:32 * g + 1, :, :].rearrange("p j n -> p (j n)")
                    dst = G[8 * half:8 * half + 8, b % 2, g, :]
                    act.dma_start(dst, src).then_inc(s_G, 16)
                    if b == B2SH:
                        src = stage[32 * g + 1:32 * g + 2, :, :].rearrange("p j n -> p (j n)")
                        act.dma_start(Gc[8 * half:8 * half + 8, g, :], src).then_inc(s_G, 16)

            def squares(k, src, wait):
                for b in range(4):
                    wait(b)
                    if k and b == 0:
                        act.wait_ge(s_stat, k)
                    act.activation(sq[:, 2 * b:2 * b + 2, :], src(b), ACT.Square).then_inc(s_sq, 1)

            def guess(k):
                act.wait_ge(s_stat, k + 1)
                if k:
                    act.wait_ge(s_rs, k)
                act.activation(lnv[:, :], stat, ACT.Ln, bias=eps_col, scale=1.0).then_inc(s_ln, 1)
                act.wait_ge(s_ln, k + 1)
                act.activation(r0[:, :], lnv[:, :], ACT.Exp, scale=-0.5).then_inc(s_r0, 1)

            def shift(o, b):
                for kt in range(KT):
                    act.wait_ge(s_t, 8 * o + kt + 1)
                    if o and kt % 2 == 0:
                        act.wait_ge(s_h, 4 * o - 3 + kt // 2)
                    act.activation(h32[:, kt, :], tt_[:, kt, :], ACT.Identity, bias=mod[:, b[0], b[1] + kt:b[1] + kt + 1])\
                       .then_inc(s_h32, 1)

            def linear_y_squares(k, ms):
                def wait(b):
                    splits(min(ms[b] + 3, ms[3] + 1))
                    act.wait_ge(s_mm, ms[b] + 1)
                squares(k, from_y, wait)

            eps_col = eps[:, 0:1]
            act.wait_ge(s_const, 5)
            from_x = lambda b: x[:, 2 * b:2 * b + 2, :]
            from_y = lambda b: ps[b][:, :].rearrange("p (k t) -> p k t", t=T)

            squares(0, from_x, lambda b: act.wait_ge(s_x, b + 1))
            guess(0)
            ada_rows(B0SH, 0)
            splits(2)
            ada_rows(B0SH, 1)
            splits(3)
            act.wait_ge(s_mod, 1)
            shift(0, (B0SH, 0))
            if has("gmlp"):
                for j in range(4):
                    m = M_V[j]
                    act.wait_ge(s_mm, m + 1)
                    act.activation(v_tm[:, :, 256 * j:256 * j + 256], ps[4 + pl.um[m] % MID][:, :].rearrange("p (t n) -> p t n", t=2),
                                   ACT.Gelu_apprx_tanh).then_inc(s_mid, 1)
                    splits(m + 4)
                for j in range(4):
                    m = M_U[j]
                    act.wait_ge(s_mm, m + 1)
                    act.activation(u_fm[:, 2 * j:2 * j + 2, :], ps[4 + pl.um[m] % MID][:, :].rearrange("p (k t) -> p k t", t=T),
                                   ACT.Gelu_apprx_tanh).then_inc(s_mid, 1)
                    splits(min(m + 4, M_AO[0]))
                ada_rows(B0G, 0)
                ada_rows(B0G, 1)
                act.wait_ge(s_vln, 1)
                link(act.activation(lr[:, 0, :], mv[:, :, 1], ACT.Ln, bias=eps_col, scale=1.0))
                act.activation(lr[:, 1, :], lr[:, 0, :], ACT.Exp, scale=-0.5).then_inc(s_lnr, 1)
                ada_rows(B0SC, 0)
                ada_rows(B0SC, 1)
                splits(M_AO[3])
                linear_y_squares(1, M_AO)
                guess(1)
            def boundary(k, nx, o, cols_b, b1=None, last=None):
                if b1 is not None:
                    ada_rows(b1, 0)
                    ada_rows(b1, 1)
                squares(k + 1, from_x, lambda b: act.wait_ge(s_x, 4 * nx + b + 1))
                guess(k + 1)
                if last is not None:
                    act.wait_ge(s_mod, last)
                shift(o, cols_b)

            def ffn(f, nxt):
                m0, c0 = M_FF[f], 16 * f
                u0 = pl.um[m0]

                def epi(c, m, i=0):
                    u = u0 + c
                    act.wait_ge(s_mm, m + 1 + 6 * i)
                    if c0 + c > 0:
                        act.wait_ge(s_fh, c0 + c + 3 * i)
                        act.wait_ge(s_fsq, c0 + c + 3 * i)
                    act.activation(fr[:, :], ps[4 + u % MID][:, :], ACT.Relu).then_inc(s_mid, 1)
                    act.wait_ge(s_mid, pl.um[m0] + c + 1 + 3 * i)
                    if c0 + c > 0:
                        act.wait_ge(s_fact, c0 + c + 3 * i)
                    act.activation(fm[:, :], fr[:, :], ACT.Square).then_inc(s_fsq, 1)

                epi(0, m0)
                splits(m0 + 4)
                with act.Fori(0, 4) as i:
                    for j in range(3):
                        c = 1 + j
                        epi(c, m0 + 2 * c - 1, i)
                        hi(m0 + 2 * c + 2, i)
                        hi(m0 + 2 * c + 3, i)
                split_next[0] = m0 + 28
                for c in range(13, 16):
                    epi(c, m0 + 2 * c - 1)
                    splits(min(m0 + 2 * c + 4, m0 + 32))

            if has("ffn0"):
                boundary(1, 1, 1, (B0G, 8), B1SH)
                splits(M_FF[0] + 3)
                ffn(0, 3)
                squares(3, from_y, lambda b: act.wait_ge(s_mm, M_FF[0] + 32))
                guess(3)

            if has("attn"):
                ada_rows(BKV, 0)
                ada_rows(BKV, 1)
                act.dma_start(w2k[:, :, 0:HD], I["cmp_w2"][0].rearrange("(k p) n -> p k n", p=P)).then_inc(s_aw, 16)
                act.dma_start(w2k[:, :, HD:P], I["cmp_w2"][0].rearrange("(k p) n -> p k n", p=P)).then_inc(s_aw, 16)
                act.dma_start(w2v[:, :, :], I["cmp_w2"][1].rearrange("(k p) n -> p k n", p=P)).then_inc(s_aw, 16)
                act.dma_start(b2k[0:HD, :], I["cmp_b2"][0].rearrange("(p a) -> p a", a=1)).then_inc(s_aw, 16)
                act.dma_start(b2k[HD:P, :], I["cmp_b2"][0].rearrange("(p a) -> p a", a=1)).then_inc(s_aw, 16)
                act.dma_start(b2v[:, :], I["cmp_b2"][1:2].broadcast_to([NCP, HD])).then_inc(s_aw, 16)
                squares(4, from_x, lambda b: act.wait_ge(s_x, 8 + b + 1))
                guess(4)
                act.wait_ge(s_mod, BKV + 1)
                shift(2, (BKV, 0))
                shift(3, (B1SH, 0))
                splits(M_KC + 3)
                act.wait_ge(s_h, 16)

                def mid_of(m):
                    return ps[4 + pl.um[m] % MID]

                def evac(m, dst, view):
                    act.wait_ge(s_mm, m + 1)
                    act.activation(dst, view(mid_of(m)), ACT.Copy).then_inc(s_mid, 1)

                two = lambda b: b[:, :].rearrange("p (k t) -> p k t", k=2)
                for j, (m, fm_) in enumerate(((M_KC, kc_fm), (M_VC, vc_fm))):
                    evac(m, fm_[:, :, :], two)
                    act.wait_ge(s_mid, pl.um[m] + 1)
                    for half in range(2):
                        for par in range(2):
                            act.dma_start(bsh[j][64 * half:64 * half + 64, par:4:2, 0:T - half],
                                          fm_[64 * par:64 * par + 64, :, half:T]).then_inc(s_bsh[j], 16)
                    splits(m + 4)
                for m, fm_, to in ((M_KS, ks_fm, kc[:, :, NCP:NCP + T]), (M_KW, kw_fm, kw[:, :, :])):
                    evac(m, fm_[:, :, :], two)
                    act.wait_ge(s_mid, pl.um[m] + 1)
                    for half in range(2):
                        for par in range(2):
                            act.dma_start(to[64 * half:64 * half + 64, par:4:2, :], fm_[64 * par:64 * par + 64, :, :])\
                               .then_inc(s_kcp, 16)
                    splits(m + 4)
                evac(M_VS, v_s[:, :, :], two)
                splits(M_VS + 4)
                evac(M_VW, v_w[:, :, :], two)
                splits(M_VW + 4)
                for j in range(2):
                    splits(M_CW[j][0] + 3)
                    for c in range(2):
                        m = M_Q[2 * j + c]
                        splits(m)
                        splits(m + 1)
                        splits(min(m + 2, M_GT + 1))
                        act.wait_ge(s_mm, m + 1)
                        act.activation(qT[:, 4 * j + 2 * c:4 * j + 2 * c + 2, :], two(mid_of(m)), ACT.Copy).then_inc(s_mid, 1)
                        splits(min(m + 4, M_GT + 1))
                act.wait_ge(s_mm, M_GT + 1)
                act.activation(gate[:, :, :], mid_of(M_GT)[:, 0:96].rearrange("p (t n) -> p t n", t=2), ACT.Exp, scale=-1.0)\
                   .then_inc(s_mid, 1)
                for j in range(2):
                    for nt in range(2):
                        act.activation(hid[:, j, nt, :], ps[2 * j + nt][:, 0:60], ACT.Gelu_apprx_tanh,
                                       bias=vec[:, C_B1 + 2 * j + nt:C_B1 + 2 * j + nt + 1]).then_inc(s_hid, 1)
                ada_rows(B1G, 0)
                ada_rows(B1G, 1)
                splits(M_BO[0] + 3)

                def exps(h):
                    hb = h % 2
                    act.wait_ge(s_nb, h + 1)
                    for qt in range(2):
                        for br in range(3):
                            c = 3 * qt + br
                            p_ = pp[:, hb, part(qt, br)]
                            ins = act.activation(p_, p_, ACT.Exp, bias=nb[:, hb, c:c + 1], scale=HD ** -0.5,
                                                 accum_out=den[:, hb, c:c + 1] if br else None)
                    ins.then_inc(s_exp, 1)

                exps(0)
                for h in range(NH):
                    if h + 1 < NH:
                        exps(h + 1)
                    act.wait_ge(s_T, h + 1)
                    if h >= 2:
                        act.wait_ge(s_O, h - 1)
                    act.activation(pts[:, h % 2, 0:384], ps[3][:, 0:384], ACT.Copy).then_inc(s_Tev, 1)
                    act.activation(pts[0:NCP, h % 2, 384:512], ps[3][0:NCP, 384:512], ACT.Copy).then_inc(s_Tev, 1)
                    if h % 2 == 0 and h:
                        act.wait_ge(s_O, h)
                        act.activation(h32[:, h // 2 - 1, :], ps[5 + (h // 2 - 1) % 2][:, 0:T], ACT.Copy).then_inc(s_oev, 1)
                act.wait_ge(s_O, NH)
                act.activation(h32[:, 7, :], ps[6][:, 0:T], ACT.Copy).then_inc(s_oev, 1)
                linear_y_squares(5, M_BO)
                guess(5)

            if has("ffn1"):
                boundary(5, 3, 4, (B1G, 8), B1SC)
                splits(M_FF[1] + 3)
                if has("gla"):
                    act.dma_start(ctx_tm[:, :, :], I["ctx_2"][0].rearrange("(t p) d -> p t d", p=P)).then_inc(s_ctx, 16)
                ffn(1, 3)
                squares(7, from_y, lambda b: act.wait_ge(s_mm, M_FF[1] + 32))
                guess(7)

            if has("gla"):
                act.wait_ge(s_wz, 1)
                act.dma_start(wab[0:16, 0:256], I["w_af_2"][0]).then_inc(s_wab, 16)
                act.dma_start(wab[16:32, 256:512], I["w_ab_2"][0]).then_inc(s_wab, 16)
                act.dma_start(wab[32:33, 0:256], I["b_af_2"]).then_inc(s_wab, 16)
                act.dma_start(wab[32:33, 256:512], I["b_ab_2"]).then_inc(s_wab, 16)
                ada_rows(B2SH, 0)
                ada_rows(B2SH, 1)
                squares(8, from_x, lambda b: act.wait_ge(s_x, 16 + b + 1))
                guess(8)
                squares(9, lambda b: cx[:, 2 * b:2 * b + 2, :], lambda b: act.wait_ge(s_cx, b + 1))
                act.wait_ge(s_mod, B2SH + 1)
                shift(5, (B2SH, 0))
                guess(9)
                shift(6, (10, 0))
                splits(M_K2 + 3)
                two = lambda b: b[:, :].rearrange("p (k t) -> p k t", k=2)

                def evac2(m, which, dst, func=ACT.Copy, scale=1.0, view=two):
                    if which == 0:
                        act.wait_ge(s_mm, m + 1)
                    u = pl.um[m] + which
                    act.activation(dst, view(ps[4 + u % MID]), func, scale=scale).then_inc(s_mid, 1)

                evac2(M_K2, 0, qk[:, 2:4, :])
                evac2(M_K2, 1, kctx[:, :, :])
                splits(M_K2 + 4)
                for j in range(2):
                    evac2(M_V2[j], 0, vx[:, :, 256 * j:256 * j + 256])
                    evac2(M_V2[j], 1, vctx[:, :, 256 * j:256 * j + 256])
                    splits(M_V2[j] + 4)
                evac2(M_AL, 0, alx[0:32, :], view=lambda b: b[0:32, 0:T])
                evac2(M_AL, 1, alc[0:32, :], view=lambda b: b[0:32, 0:T])
                splits(M_AL + 4)
                evac2(M_Q2, 0, qk[:, 0:2, :], scale=0.125)
                splits(M_Q2 + 4)
                act.wait_ge(s_gp, 1)
                lt = [wc[:, 0, :], wc[:, 1, :], bx[:, 0:2, :].rearrange("p k t -> p (k t)"),
                      bx[:, 2:4, :].rearrange("p k t -> p (k t)")]
                for b in range(4):
                    ins = act.activation(lt[b], ps[b][:, :], ACT.Abs)
                link(ins)
                for b in range(4):
                    ins = act.activation(lt[b], lt[b], ACT.Exp, scale=-1.0)
                link(ins)
                for b in range(4):
                    act.activation(lt[b], lt[b], ACT.Ln, bias=one1[:, 0:1], scale=1.0).then_inc(s_la, 1)
                for j in range(2):
                    evac2(M_OG[j], 0, og[:, 2 * j:2 * j + 2, :], func=ACT.Silu)
                    splits(M_OG[j] + 4)
                act.wait_ge(s_cum, 1)
                act.wait_ge(s_g, 2)
                for tt in range(2):
                    act.activation(wc[:, tt, :], ps[tt][:, :], ACT.Exp, scale=1.0 / 16).then_inc(s_wc, 1)
                for j in range(2):
                    evac2(M_SC[j], 0, sct[:, 2 * j:2 * j + 2, :])
                    splits(M_SC[j] + 4)
                act.wait_ge(s_st, 1)
                act.activation(st[:, :, :, :], ps[2][:, :].rearrange("p (a b c) -> p a b c", a=2, b=2), ACT.Copy).then_inc(s_ste, 1)
                for j in range(2):
                    evac2(M_SX[j], 0, ct[:, 2 * j:2 * j + 2, :])
                    splits(min(M_SX[j] + 4, M_SB[1] + 1))
                for j in range(2):
                    evac2(M_SB[j], 0, sbt[:, 2 * j:2 * j + 2, :])
                act.wait_ge(s_B, 1)
                act.activation(qi[:, 0:2, :], bx[:, 0:2, :], ACT.Exp, scale=1.0 / 16)
                for j in range(2):
                    ins = act.activation(qi[:, 2 + j, :], bx[:, 2 + j, :], ACT.Exp, bias=tot[:, j:j + 1], scale=-1.0 / 16)
                ins.then_inc(s_qe, 1)
                for l in range(8):
                    act.wait_ge(s_D, l + 1)
                    act.activation(eb[:, l % 2, :, :], eb[:, l % 2, :, :], ACT.Exp, scale=1.0 / 16).then_inc(s_Ex, 1)
                    if l == 3:
                        ada_rows(B2G, 0)
                ada_rows(B2G, 1)
                splits(M_WO[0] + 3)
                act.wait_ge(s_o4, 1)
                for b in range(2):
                    ins = act.activation(o2[:, 2 * b:2 * b + 2, :], two(ps[2 + b]), ACT.Square)
                ins.then_inc(s_o2, 1)
                act.wait_ge(s_ms4, 1)
                for b in range(2):
                    ins = act.activation(ln4[:, 2 * b:2 * b + 2, :], two(ps[b]), ACT.Ln, bias=eps_col, scale=D / P)
                ins.then_inc(s_l4, 1)
                act.wait_ge(s_l4, 1)
                act.activation(r4[:, :, :], ln4[:, :, :], ACT.Exp, scale=-0.5).then_inc(s_r4, 1)
                linear_y_squares(10, M_WO)
                guess(10)

            if has("ffn2"):
                boundary(10, 5, 7, (B2G, 8), B2SC)
                splits(M_UP + 2)

                def conv_epi(c, i=0):
                    m = M_UP + (3 * c - 1 if c else 0)
                    act.wait_ge(s_mm, m + 1 + 6 * i)
                    if c:
                        act.wait_ge(s_tap, 8 * c + 16 * i)
                        act.wait_ge(s_sil, c + 2 * i)
                    bank = ps[4 + c % 2]
                    act.activation(ut[:, :, :], bank[:, :].rearrange("p (k t) -> p k t", t=T), ACT.Copy)
                    for k in range(2):
                        b_, w_ = C_BCF + 2 * c + k, C_WCF + 22 * 4 + 2 * c + k
                        ins = act.activation(cvt[:, k, :], bank[:, T * k:T * k + T], ACT.Identity,
                                             bias=vec[:, bass.ds(b_ + 4 * i, 1)], scale=vec[:, bass.ds(w_ + 4 * i, 1)])
                    ins.then_inc(s_ue, 1)
                    hi(M_UP + 3 * c + 2, i)
                    if c < CF - 1:
                        hi(M_UP + 3 * c + 3, i)
                    act.wait_ge(s_tap, 8 * c + 8 + 16 * i)
                    if c:
                        act.wait_ge(s_fa, c + 2 * i)
                    act.activation(sl[:, :, :], cvt[:, :, :], ACT.Silu).then_inc(s_sil, 1)
                    if c < CF - 1:
                        hi(M_UP + 3 * c + 4, i)
                    act.wait_ge(s_fa, c + 1 + 2 * i)
                    act.activation(chi[:, c % 2, :], fa[:, :, :].rearrange("p k t -> p (k t)"), ACT.Copy).then_inc(s_chi, 1)

                conv_epi(0)
                with act.Fori(0, 4) as i:
                    for j in range(2):
                        conv_epi(1 + j, i)
                conv_epi(9)
                conv_epi(10)
                split_next[0] = NM
                squares(12, from_y, lambda b: act.wait_ge(s_mm, M_UP + 33))
                guess(12)

        @block.vector
        def _(dve):
            chain = [0]

            def link(ins):
                ins.then_inc(d_ch, 1)
                chain[0] += 1
                dve.wait_ge(d_ch, chain[0])

            split_next = [0]

            def lo(m, i=0):
                dve.wait_ge(s_hi, m + 1 + 6 * i)
                w = pl.width[m]
                dve.tensor_tensor(wlo[:, m % SPL, 0:w], raw[:, pl.nm[m] % RAW, 0:w], whi[:, m % SPL, 0:w],
                                  ALU.subtract).then_inc(s_lo, 1)

            def splits(upto_m):
                while split_next[0] < min(upto_m, NM):
                    lo(split_next[0])
                    split_next[0] += 1

            def refine(k):
                dve.wait_ge(s_ln, k + 1)
                link(dve.tensor_scalar(vv[:, :], stat, EPS, None, ALU.add))
                dve.wait_ge(s_r0, k + 1)
                link(dve.tensor_tensor(n1[:, :], r0[:, :], r0[:, :], ALU.mult))
                link(dve.scalar_tensor_tensor(out=n1[:, :], in0=n1[:, :], scalar=-0.5, in1=vv[:, :], op0=ALU.mult, op1=ALU.mult))
                dve.scalar_tensor_tensor(out=rs[:, :], in0=n1[:, :], scalar=1.5, in1=r0[:, :], op0=ALU.add, op1=ALU.mult)\
                   .then_inc(s_rs, 1)
                dve.wait_ge(s_rs, k + 1)

            def mods(b):
                dve.wait_ge(s_fin, b + 1)
                link(dve.tensor_tensor(mod[:, b, :], small, vec[:, BIAS[b]:BIAS[b] + 16], ALU.add))
                if b == B2SH:
                    link(dve.tensor_tensor(mod[:, 10, :], smallc, vec[:, BIAS[b]:BIAS[b] + 16], ALU.add))
                for j, (c, kind, m, g) in enumerate(COEFS[b]):
                    if kind == "A":
                        ins = dve.scalar_tensor_tensor(out=coef[:, c, :], in0=m, scalar=1.0, in1=vec[:, g:g + 8],
                                                       op0=ALU.add, op1=ALU.mult)
                    else:
                        ins = dve.tensor_tensor(coef[:, c, :], m, vec[:, g:g + 8], ALU.mult)
                    link(ins)
                dve.tensor_copy(n1[:, 0:1], coef[:, 0, 0:1]).then_inc(s_mod, 1)
                dve.wait_ge(s_mod, b + 1)

            def scale_x(o, c, src=None, free=None):
                s = x if src is None else src
                for kt in range(KT):
                    if o:
                        dve.wait_ge(s_h32, 8 * o - 7 + kt)
                    dve.scalar_tensor_tensor(out=tt_[:, kt, :], in0=s[:, kt, :], scalar=coef[:, c, kt:kt + 1], in1=rs[:, :],
                                             op0=ALU.mult, op1=ALU.mult).then_inc(s_t, 1)

            def split_h(o, dh, dl, free=0):
                if free:
                    dve.wait_ge(s_mm, free)
                for b in range(4):
                    dve.wait_ge(s_h32, 8 * o + 2 * b + 2)
                    link(dve.tensor_copy(dh[:, 2 * b:2 * b + 2, :], h32[:, 2 * b:2 * b + 2, :]))
                    dve.tensor_tensor(dl[:, 2 * b:2 * b + 2, :], h32[:, 2 * b:2 * b + 2, :], dh[:, 2 * b:2 * b + 2, :],
                                      ALU.subtract).then_inc(s_h, 1)

            def update_x(c, nx):
                for kt in range(KT):
                    yk = ps[kt // 2][:, (kt % 2) * T:(kt % 2) * T + T]
                    ins = dve.scalar_tensor_tensor(out=tt_[:, kt, :], in0=yk, scalar=coef[:, c, kt:kt + 1], in1=rs[:, :],
                                                   op0=ALU.mult, op1=ALU.mult)
                    if kt % 2:
                        b = kt // 2
                        ins.then_inc(s_yfree, 1)
                        dve.wait_ge(s_yfree, 4 * (nx - 1) + b + 1)
                        dve.wait_ge(d_ch, chain[0])
                        dve.tensor_tensor(x[:, 2 * b:2 * b + 2, :], x[:, 2 * b:2 * b + 2, :], tt_[:, 2 * b:2 * b + 2, :],
                                          ALU.add).then_inc(s_x, 1)
                    else:
                        link(ins)

            for i in range(6):
                dve.wait_ge(s_vT, i + 1)
                dve.tensor_copy(vec[:, V0[i]:V0[i + 1]], ps[7][:, 0:NV[i]] if i % 2 == 0 else ps[6][:, 0:NV[i]])\
                   .then_inc(s_vec, 1)
                if i == 0:
                    for b in range(4):
                        dve.wait_ge(s_xT, b + 1)
                        dve.tensor_copy(x[:, 2 * b:2 * b + 2, :], ps[b][:, :].rearrange("p (k t) -> p k t", t=T)).then_inc(s_x, 1)
                    dve.wait_ge(s_cpad0, 1)
                    dve.wait_ge(s_sg, 1)
                    dve.tensor_copy(cpad[:, 0, :, 0], csil[:, 0:8]).then_inc(s_cp, 1)
                    dve.tensor_copy(cpad[:, 1, :, 0], csil[:, 8:16]).then_inc(s_cp, 1)
                    dve.tensor_copy(cpad[:, 1, :, 1], csil[:, 16:24]).then_inc(s_cp, 1)
            dve.wait_ge(s_vec, 6)
            dve.wait_ge(s_x, 4)
            if has("gmlp"):
                for b in range(2):
                    dve.wait_ge(s_wsT, b + 1)
                    dve.tensor_copy(wT[:, 4 * b:4 * b + 4, :], ps[b][:, :].rearrange("p (g t) -> p g t", g=4)).then_inc(s_wTc, 1)
            refine(0)
            splits(2)
            mods(B0SH)
            scale_x(0, A_N0)
            split_h(0, hh, hl)
            splits(3)
            if has("gmlp"):
                for j in range(8):
                    splits(min(j + 4, 8))
                    if j == 5:
                        dve.wait_ge(s_mid, pl.um[M_V[3]] + 1)
                        dve.wait_ge(s_gm, 64)
                        for tt in range(2):
                            for f in range(2):
                                link(dve.bn_stats(bst[:, tt, f, :], v_tm[:, tt, 512 * f:512 * f + 512]))
                        link(dve.bn_aggr(mv[:, 0, :], bst[:, 0, :, :]))
                        dve.bn_aggr(mv[:, 1, :], bst[:, 1, :, :]).then_inc(s_vln, 1)
                        dve.wait_ge(s_vln, 1)
                        link(dve.tensor_scalar(lr[:, 2, :], mv[:, :, 1], EPS, None, ALU.add))
                mods(B0G)
                dve.wait_ge(s_lnr, 1)
                link(dve.tensor_tensor(lr[:, 3, :], lr[:, 1, :], lr[:, 1, :], ALU.mult))
                link(dve.scalar_tensor_tensor(out=lr[:, 3, :], in0=lr[:, 3, :], scalar=-0.5, in1=lr[:, 2, :], op0=ALU.mult, op1=ALU.mult))
                link(dve.scalar_tensor_tensor(out=lr[:, 2, :], in0=lr[:, 3, :], scalar=1.5, in1=lr[:, 1, :], op0=ALU.add, op1=ALU.mult))
                for tt in range(2):
                    link(dve.tensor_scalar(v_tm[:, tt, :], v_tm[:, tt, :], mv[:, tt, 0:1], lr[:, 2, tt:tt + 1], ALU.subtract, ALU.mult))
                for tt in range(2):
                    link(dve.tensor_tensor(v_tm[:, tt, :], v_tm[:, tt, :], lng[:, :], ALU.mult))
                    dve.tensor_tensor(v_tm[:, tt, :], v_tm[:, tt, :], lnb[:, :], ALU.add).then_inc(s_vn, 1)
                dve.wait_ge(s_h32, 8)
                dve.wait_ge(s_mid, pl.um[M_U[3]] + 1)
                dve.wait_ge(s_mm, M_U[3] + 1)
                for b in range(4):
                    dve.wait_ge(s_mix, b + 1)
                    bias = bs_b[:, 2 * b:2 * b + 2, :].rearrange("p g (a t) -> p g a t", a=1).broadcast_to([P, 2, 2, P])
                    link(dve.tensor_tensor(tt_[:, 2 * b:2 * b + 2, :].rearrange("p g (a t) -> p g a t", a=2),
                                           ps[b][:, :].rearrange("p (g a t) -> p g a t", g=2, a=2), bias, ALU.add))
                    link(dve.tensor_tensor(h32[:, 2 * b:2 * b + 2, :], tt_[:, 2 * b:2 * b + 2, :], u_fm[:, 2 * b:2 * b + 2, :], ALU.mult))
                    link(dve.tensor_copy(hh[:, 2 * b:2 * b + 2, :], h32[:, 2 * b:2 * b + 2, :]))
                    dve.tensor_tensor(hl[:, 2 * b:2 * b + 2, :], h32[:, 2 * b:2 * b + 2, :], hh[:, 2 * b:2 * b + 2, :], ALU.subtract)\
                       .then_inc(s_oa, 1)
                mods(B0SC)
                dve.wait_ge(s_oa, 4)
                splits(M_AO[3] + 1)
                refine(1)
                update_x(G_N1, 1)

            def boundary(k, nx, o, c, b1, free, dh=hh, dl=hl, src=None):
                dve.wait_ge(s_x, 4 * nx + 4)
                refine(k + 1)
                if b1 is not None:
                    mods(b1)
                scale_x(o, c)
                split_h(o, hh, hl, free)

            def ffn(f):
                m0, c0 = M_FF[f], 16 * f
                mid0 = pl.um[m0]

                def epi(c, i=0, first=False):
                    dve.wait_ge(s_mid, mid0 + c + 1 + 3 * i)
                    if c >= 3:
                        dve.wait_ge(s_mm, m0 + 2 * (c - 3) + 3 + 6 * i)
                    dve.tensor_tensor(fhi[:, c % 3, :], fr[:, :], fr[:, :], ALU.mult).then_inc(s_fh, 1)
                    dve.wait_ge(s_fh, c0 + c + 1 + 3 * i)
                    dve.wait_ge(s_fsq, c0 + c + 1 + 3 * i)
                    dve.tensor_tensor(flo[:, c % 3, :], fm[:, :], fhi[:, c % 3, :], ALU.subtract).then_inc(s_fact, 1)

                epi(0)
                splits(m0 + 4)
                for c in range(1, 4):
                    epi(c)
                    splits(m0 + 2 * c + 4)
                with dve.Fori(0, 3) as i:
                    for j in range(3):
                        c = 4 + j
                        epi(c, i)
                        lo(m0 + 2 * c + 2, i)
                        lo(m0 + 2 * c + 3, i)
                split_next[0] = m0 + 28
                for c in range(13, 16):
                    epi(c)
                    splits(min(m0 + 2 * c + 4, m0 + 32))

            if has("ffn0"):
                boundary(1, 1, 1, A_N2, B1SH, M_AO[3] + 1)
                splits(M_FF[0] + 3)
                ffn(0)
                refine(3)
                dve.wait_ge(s_h32, 16)
                update_x(G_N3, 2)

            if has("attn"):
                dve.wait_ge(s_x, 12)
                refine(4)
                mods(BKV)
                scale_x(2, A_KV)
                split_h(2, gh, gl)
                scale_x(3, A_N4)
                split_h(3, hh, hl, M_FF[0] + 32)
                splits(M_KW + 1)

                def compress(j):
                    dve.wait_ge(s_bsh[j], 64)
                    if j:
                        dve.wait_ge(s_mm, M_CW[0][1] + 1)
                    for half in range(2):
                        src = bsh[j][:, :, 16 * half:16 * half + 240].rearrange("p g (c i two) -> p i g c two", c=NC, two=2)[:, :, :, :, 0]
                        pos = vec[:, C_POS + 16 * j + 8 * half:C_POS + 16 * j + 8 * half + 8]
                        pos = pos.rearrange("p (i a b) -> p i a b", a=1, b=1).broadcast_to([P, 8, NG, NC])
                        link(dve.tensor_tensor(blk[:, 8 * half:8 * half + 8, :, :], src, pos, ALU.add))
                    b60 = blk[:, :, :, :].rearrange("p i g c -> p i (g c)")
                    link(dve.tensor_copy(bhi[:, :, :], b60))
                    dve.tensor_tensor(blo[:, :, :], b60, bhi[:, :, :], ALU.subtract).then_inc(s_blk, 1)
                    dve.wait_ge(s_blk, j + 1)

                compress(0)
                splits(M_CW[1][0] + 1)
                compress(1)
                splits(M_GT + 1)
                dve.wait_ge(s_mid, pl.um[M_GT] + 1)
                link(dve.tensor_scalar(gate[:, :, :], gate[:, :, :], 1.0, None, ALU.add))
                dve.reciprocal(gate[:, :, :], gate[:, :, :]).then_inc(s_gt, 1)
                dve.wait_ge(s_gt, 1)
                dve.wait_ge(s_aw, 96)
                dve.wait_ge(s_w2, 1)
                link(dve.memset(kc[:, :, NC:NCP], 0.0))
                dve.tensor_scalar(kc[:, :, 0:NC], ps[0][:, 0:60].rearrange("p (g c) -> p g c", g=NG), b2k[:, 0:1], None, ALU.add)\
                   .then_inc(s_kv, 1)
                bias = b2v[0:NC, :].rearrange("p (a n) -> p a n", a=1).broadcast_to([NC, NG, HD])
                dve.tensor_tensor(vcs[0:NC, :, :], ps[1][0:NC, 0:256].rearrange("p (g n) -> p g n", g=NG), bias, ALU.add)\
                   .then_inc(s_kv, 1)
                dve.wait_ge(s_kv, 2)
                splits(M_BO[0] + 3)
                dve.wait_ge(s_asm, 3)

                def scores_out(h):
                    hb = h % 2
                    dve.wait_ge(s_S, h + 1)
                    if h >= 2:
                        dve.wait_ge(s_T, h - 1)
                    for qt in range(2):
                        for br in range(3):
                            mask = cmm[:, qt, :] if br == 0 else cmask[:, P * (1 - qt):T]
                            c = 3 * qt + br
                            ins = dve.tensor_tensor_reduce(pp[:, hb, part(qt, br)], score_psum(qt, br), mask, 1.0, -3e38,
                                                           ALU.add, ALU.max, mx[:, hb, c:c + 1])
                    ins.then_inc(s_Sev, 1)
                    dve.wait_ge(s_Sev, h + 1)
                    dve.tensor_scalar(nb[:, hb, :], mx[:, hb, :], -HD ** -0.5, None, ALU.mult).then_inc(s_nb, 1)

                def gated(h):
                    hb = h % 2
                    dve.wait_ge(s_exp, h + 1)
                    for qt in range(2):
                        p_ = pp[:, hb, part(qt, 0)]
                        link(dve.tensor_tensor_reduce(p_, p_, cm01[:, qt, :], 1.0, 0.0, ALU.mult, ALU.add,
                                                      den[:, hb, 3 * qt:3 * qt + 1]))
                    link(dve.tensor_scalar(rec[:, hb, :], den[:, hb, :], 1e-30, None, ALU.max))
                    link(dve.reciprocal(rec[:, hb, :], rec[:, hb, :]))
                    link(dve.tensor_tensor(cf[:, hb, :].rearrange("p (t b) -> p t b", t=2),
                                           rec[:, hb, :].rearrange("p (t b) -> p t b", t=2), gate[:, :, 3 * h:3 * h + 3], ALU.mult))
                    for qt in range(2):
                        for br in range(3):
                            c = 3 * qt + br
                            p_ = pp[:, hb, part(qt, br)]
                            ins = dve.tensor_scalar(p_, p_, cf[:, hb, c:c + 1], None, ALU.mult)
                    ins.then_inc(s_p, 1)
                    dve.wait_ge(s_p, h + 1)

                scores_out(0)
                for h in range(NH):
                    if h + 1 < NH:
                        scores_out(h + 1)
                    gated(h)
                    dve.wait_ge(s_T, h + 1)
                    if h >= 2:
                        dve.wait_ge(s_O, h - 1)
                    dve.tensor_copy(pts[:, h % 2, 512:896], ps[4][:, 0:384]).then_inc(s_TevD, 1)
                    dve.tensor_copy(pts[0:NCP, h % 2, 896:1024], ps[4][0:NCP, 384:512]).then_inc(s_TevD, 1)
                    if h % 2 == 0 and h:
                        k = h // 2 - 1
                        dve.wait_ge(s_oev, k + 1)
                        link(dve.tensor_copy(hh[:, k, :], h32[:, k, :]))
                        dve.tensor_tensor(hl[:, k, :], h32[:, k, :], hh[:, k, :], ALU.subtract).then_inc(s_oh, 1)
                dve.wait_ge(s_oev, 8)
                link(dve.tensor_copy(hh[:, 7, :], h32[:, 7, :]))
                dve.tensor_tensor(hl[:, 7, :], h32[:, 7, :], hh[:, 7, :], ALU.subtract).then_inc(s_oh, 1)
                dve.wait_ge(s_oh, 8)
                mods(B1G)
                splits(M_BO[3] + 1)
                refine(5)
                update_x(G_N5, 3)

            if has("ffn1"):
                boundary(5, 3, 4, A_N6, B1SC, M_BO[3] + 1)
                splits(M_FF[1] + 3)
                ffn(1)
                refine(7)
                dve.wait_ge(s_h32, 40)
                update_x(G_N7, 4)

            if has("gla"):
                for b in range(4):
                    dve.wait_ge(s_cT, b + 1)
                    dve.tensor_copy(cx[:, 2 * b:2 * b + 2, :], ps[b][:, :].rearrange("p (k t) -> p k t", t=T)).then_inc(s_cx, 1)
                refine(8)
                mods(B2SH)
                scale_x(5, A_N8)
                split_h(5, hh, hl, M_FF[1] + 32)
                dve.wait_ge(s_cx, 4)
                refine(9)
                scale_x(6, A_N9, cx)
                split_h(6, gh, gl)
                splits(M_Q2 + 4)
                lt = [wc[:, 0, :], wc[:, 1, :], bx[:, 0:2, :].rearrange("p k t -> p (k t)"),
                      bx[:, 2:4, :].rearrange("p k t -> p (k t)")]
                gt = [gc[:, 0, :], gc[:, 1, :], gx[:, 0:2, :].rearrange("p k t -> p (k t)"),
                      gx[:, 2:4, :].rearrange("p k t -> p (k t)")]
                for b in range(4):
                    dve.wait_ge(s_la, b + 1)
                    dve.scalar_tensor_tensor(out=gt[b], in0=ps[b][:, :], scalar=0.0, in1=lt[b], op0=ALU.min, op1=ALU.subtract)                       .then_inc(s_g, 1)
                splits(M_OG[0] + 4)
                dve.wait_ge(s_g, 4)
                link(dve.memset(bx[:, 2:4, 0:1], 0.0))
                for j in range(4):
                    n = T if j < 2 else T - 1
                    ins = dve.tensor_tensor_scan(bx[:, j, T - n:T], one1[:, 0:n], gx[:, j, 0:n], 0.0, ALU.mult, ALU.add)
                link(ins)
                link(dve.tensor_tensor(tot[:, :], bx[:, 2:4, T - 1], gx[:, 2:4, T - 1], ALU.add))
                dve.tensor_scalar(tot[:, :], tot[:, :], 1.0 / 16, None, ALU.mult).then_inc(s_B, 1)
                splits(M_OG[1] + 4)
                for tt in range(2):
                    dve.wait_ge(s_wc, tt + 1)
                    w_ = wc[:, tt, :].rearrange("p (f n) -> p f n", f=2)
                    ins = dve.tensor_tensor(w_, w_, kctx[:, tt:tt + 1, :].broadcast_to([P, 2, T]), ALU.mult)
                ins.then_inc(s_kd, 1)
                for j in range(2):
                    splits(M_SC[j] + 4)
                splits(M_SB[1] + 1)
                for j in range(2):
                    dve.wait_ge(s_mid, pl.um[M_SX[j]] + 1)
                    ins = dve.tensor_tensor(ct[:, 2 * j:2 * j + 2, :], ct[:, 2 * j:2 * j + 2, :], sct[:, 2 * j:2 * j + 2, :], ALU.mult)
                link(ins)
                row = lambda a, k: a[:, k, :].rearrange("p (r w) -> p r w", w=64)
                tap = lambda w, k: vec[:, C_WSC + 4 * w + k:C_WSC + 4 * w + k + 1]
                for k in range(4):
                    ins = dve.tensor_scalar(sct[:, k, :], ct[:, k, :], tap(1, k), vec[:, C_BSC + k:C_BSC + k + 1], ALU.mult, ALU.add)
                link(ins)
                for w, to, frm in ((0, slice(1, 64), slice(0, 63)), (2, slice(0, 63), slice(1, 64))):
                    for k in range(4):
                        ins = dve.scalar_tensor_tensor(out=row(sct, k)[:, :, to], in0=row(ct, k)[:, :, frm], scalar=tap(w, k),
                                                       in1=row(sct, k)[:, :, to], op0=ALU.mult, op1=ALU.add)
                    link(ins)
                dve.wait_ge(s_mid, pl.um[M_SB[1]] + 1)
                link(dve.tensor_tensor(sct[:, :, :], sct[:, :, :], sbt[:, :, :], ALU.mult))
                dve.wait_ge(s_mm, M_SB[1] + 1)
                link(dve.tensor_copy(hh[:, 4:8, :], sct[:, :, :]))
                dve.tensor_tensor(hl[:, 4:8, :], sct[:, :, :], hh[:, 4:8, :], ALU.subtract).then_inc(s_cv, 1)
                dve.wait_ge(s_qe, 1)
                q_ = qk[:, 0:2, :].rearrange("p (a k) t -> p a k t", a=1).broadcast_to([P, 2, 2, T])
                qi_ = qi[:, :, :].rearrange("p (a k) t -> p a k t", a=2)
                dve.tensor_tensor(qi_, qi_, q_, ALU.mult).then_inc(s_qi, 1)

                def operands(l):
                    dve.wait_ge(s_Ex, l + 1)
                    dve.tensor_tensor(eb[:, l % 2, :, :], eb[:, l % 2, :, :], qk[:, :, :], ALU.mult).then_inc(s_E, 1)

                def fill(n):
                    dve.wait_ge(s_lev, n + 1)
                    for par in range(2):
                        src = ps[2 * (n % 2) + par][:, :].rearrange("p (c i) -> p c i", i=P)
                        dst = (a_x if n == 1 else a_d)[:, par, :, :, :].rearrange("p t g i -> p (t g) i")
                        if n < 2:
                            ins = dve.tensor_copy(dst, src)
                        else:
                            mask = lmask[:, n - 2:n - 1, :].broadcast_to([P, 4, P])
                            ins = dve.copy_predicated(dst, mask, src)
                    ins.then_inc(s_A, 1)
                    dve.wait_ge(s_A, n + 1)

                dve.wait_ge(s_gm3, 9)
                fill(0)
                operands(0)
                for l in range(8):
                    if l < 7:
                        operands(l + 1)
                    fill(l + 1)
                mods(B2G)
                splits(M_WO[0] + 3)
                dve.wait_ge(s_l4, 1)
                for b in range(2):
                    ins = dve.tensor_scalar(v4[:, 2 * b:2 * b + 2, :], ps[b][:, :].rearrange("p (k t) -> p k t", k=2), D / P, EPS,
                                            ALU.mult, ALU.add)
                link(ins)
                dve.wait_ge(s_r4, 1)
                link(dve.tensor_tensor(n4[:, :, :], r4[:, :, :], r4[:, :, :], ALU.mult))
                link(dve.scalar_tensor_tensor(out=n4[:, :, :], in0=n4[:, :, :], scalar=-0.5, in1=v4[:, :, :], op0=ALU.mult, op1=ALU.mult))
                link(dve.scalar_tensor_tensor(out=r4[:, :, :], in0=n4[:, :, :], scalar=1.5, in1=r4[:, :, :], op0=ALU.add, op1=ALU.mult))
                for b in range(2):
                    ins = dve.scalar_tensor_tensor(out=o4[:, b:4:2, :], in0=ps[2 + b][:, :].rearrange("p (k t) -> p k t", k=2),
                                                   scalar=vec[:, C_GH:C_GH + 1], in1=r4[:, 2 * b:2 * b + 2, :], op0=ALU.mult, op1=ALU.mult)
                link(ins)
                link(dve.tensor_tensor(o4[:, :, :], o4[:, :, :], og[:, :, :], ALU.mult))
                link(dve.tensor_copy(hh[:, 0:4, :], o4[:, :, :]))
                dve.tensor_tensor(hl[:, 0:4, :], o4[:, :, :], hh[:, 0:4, :], ALU.subtract).then_inc(s_gs, 1)
                splits(M_WO[3] + 1)
                refine(10)
                dve.wait_ge(s_gs, 1)
                update_x(G_N10, 5)

            if has("ffn2"):
                boundary(10, 5, 7, A_N11, B2SC, M_WO[3] + 1)
                splits(M_UP + 2)
                TAPS = [(dr, dc) for dr in (-1, 0, 1) for dc in (-1, 0, 1) if (dr, dc) != (0, 0)]
                HROW, WROW = T // 64, 64

                def conv_epi(c, i=0):
                    dve.wait_ge(s_ue, c + 1 + 2 * i)
                    for n, (dr, dc) in enumerate(TAPS):
                        to = (slice(max(0, -dr), HROW - max(0, dr)), slice(max(0, -dc), WROW - max(0, dc)))
                        frm = (slice(max(0, dr), HROW - max(0, -dr)), slice(max(0, dc), WROW - max(0, -dc)))
                        for k in range(2):
                            grid = lambda a: a[:, k, :].rearrange("p (r w) -> p r w", w=WROW)
                            w_ = C_WCF + 22 * (3 * (dr + 1) + dc + 1) + 2 * c + k
                            y = grid(cvt)[:, to[0], to[1]]
                            ins = dve.scalar_tensor_tensor(out=y, in0=grid(ut)[:, frm[0], frm[1]],
                                                           scalar=vec[:, bass.ds(w_ + 4 * i, 1)], in1=y,
                                                           op0=ALU.mult, op1=ALU.add)
                        ins.then_inc(s_tap, 1)
                        dve.wait_ge(s_tap, 8 * c + n + 1 + 16 * i)
                        if n == 3:
                            lo(M_UP + 3 * c + 2, i)
                    if c < CF - 1:
                        lo(M_UP + 3 * c + 3, i)
                    dve.wait_ge(s_mm, M_UP + (3 * c if c else 1) + 1 + 6 * i)
                    dve.wait_ge(s_sil, c + 1 + 2 * i)
                    if c:
                        dve.wait_ge(s_cact, c + 2 * i)
                    dve.tensor_tensor(fa[:, :, :], sl[:, :, :], ps[6 + c % 2][:, :].rearrange("p (k t) -> p k t", t=T), ALU.mult)                       .then_inc(s_fa, 1)
                    if c < CF - 1:
                        lo(M_UP + 3 * c + 4, i)
                    dve.wait_ge(s_fa, c + 1 + 2 * i)
                    dve.wait_ge(s_chi, c + 1 + 2 * i)
                    dve.tensor_tensor(clo[:, c % 2, :], fa[:, :, :].rearrange("p k t -> p (k t)"), chi[:, c % 2, :], ALU.subtract)                       .then_inc(s_cact, 1)

                conv_epi(0)
                with dve.Fori(0, 4) as i:
                    for j in range(2):
                        conv_epi(1 + j, i)
                conv_epi(9)
                conv_epi(10)
                split_next[0] = NM
                refine(12)
                dve.wait_ge(s_h32, 64)
                update_x(G_N12, 6)

            dve.wait_ge(s_x, 4 * N_UPD + 4)
            dve.wait_ge(s_yfree, 4 * N_UPD)
            for b in range(4):
                dve.wait_ge(s_oT, b + 1)
                dve.tensor_copy(y_tm[:, b // 2, 512 * (b % 2):512 * (b % 2) + 512], ps[b][:, :]).then_inc(s_oc, 1)

        @block.tensor
        def _(pe):
            in_bank7 = {"stats": 0, "sums": 0}

            def ada(a, c=0):
                u = pl.ua[a]
                full(pe, pl.na[a])
                if u >= MID:
                    pe.wait_ge(s_mid, u - MID + 1)
                w = raw[:, pl.na[a] % RAW, :].rearrange("p (k n) -> p k n", n=256)
                for kt in range(KT):
                    g = kt % 4
                    mm = pe.matmul(ps[4 + u % MID][32 * g:32 * g + 32, 0:256], cpad[:, c, kt, :], w[:, kt, :],
                                   start=kt < 4, stop=kt >= 4)
                mm.then_inc(s_ada, 1)

            def ada_half(b, half):
                for a in range(8 * b + 4 * half, 8 * b + 4 * half + 4):
                    ada(a, 0 if b < B2SH else 1)

            def ada_sum(b):
                pe.wait_ge(s_G, G_after(b))
                if in_bank7["stats"]:
                    pe.wait_ge(s_rs, in_bank7["stats"])
                if b:
                    pe.wait_ge(s_mod, b)
                in_bank7["sums"] = b + 1
                for g in range(4):
                    mm = pe.matmul(small, G[:, b % 2, g, :], ident[0:16, 0:16], start=g == 0, stop=g == 3)
                if b == B2SH:
                    for g in range(4):
                        mm = pe.matmul(smallc, Gc[:, g, :], ident[0:16, 0:16], start=g == 0, stop=g == 3)
                mm.then_inc(s_fin, 1)

            def mean_square(k):
                if k:
                    pe.wait_ge(s_rs, k)
                if in_bank7["sums"]:
                    pe.wait_ge(s_mod, in_bank7["sums"])
                in_bank7["stats"] = k + 1
                for kt in range(KT):
                    if kt % 2 == 0:
                        pe.wait_ge(s_sq, 4 * k + kt // 2 + 1)
                    mm = pe.matmul(stat, onesm[:, :], sq[:, kt, :], start=kt == 0, stop=kt == KT - 1)
                mm.then_inc(s_stat, 1)

            def w_of(m, kts=KT):
                w = pl.width[m] // kts
                v = slice(0, pl.width[m])
                return (whi[:, m % SPL, v].rearrange("p (k n) -> p k n", n=w),
                        wlo[:, m % SPL, v].rearrange("p (k n) -> p k n", n=w))

            def feature_major(m, dst, ah, al, i=0, kts=KT):
                wh, wl = w_of(m, kts)
                for nt in range(wh.shape[2] // P):
                    for kt in range(kts):
                        n = slice(nt * P, nt * P + P)
                        pe.matmul(dst(nt), wh[:, kt, n], ah[:, kt, :], start=kt == 0, stop=False)
                        pe.matmul(dst(nt), wh[:, kt, n], al[:, kt, :], start=False, stop=False)
                        mm = pe.matmul(dst(nt), wl[:, kt, n], ah[:, kt, :], start=False, stop=kt == kts - 1)
                return mm

            def token_major(m, dst, ah, al):
                wh, wl = w_of(m)
                for tt in range(2):
                    for kt in range(KT):
                        t = slice(tt * P, tt * P + P)
                        pe.matmul(dst(tt), ah[:, kt, t], wh[:, kt, :], start=kt == 0, stop=False)
                        pe.matmul(dst(tt), ah[:, kt, t], wl[:, kt, :], start=False, stop=False)
                        mm = pe.matmul(dst(tt), al[:, kt, t], wh[:, kt, :], start=False, stop=kt == KT - 1)
                return mm

            def split_ready(m, i=0):
                pe.wait_ge(s_lo, m + 1 + 6 * i)

            def mid_free(u, i=0):
                if u >= MID:
                    pe.wait_ge(s_mid, u - MID + 1 + 3 * i)

            def linear_mid(m, ah, al, tm=False, i=0):
                u = pl.um[m]
                split_ready(m, i)
                mid_free(u, i)
                w = pl.width[m] // KT
                if tm:
                    mm = token_major(m, lambda tt: ps[4 + u % MID][:, w * tt:w * tt + w], ah, al)
                else:
                    mm = feature_major(m, lambda nt: ps[4 + u % MID][:, T * nt:T * nt + T], ah, al)
                mm.then_inc(s_mm, 1)

            def linear_y(m, j, ah, al):
                split_ready(m)
                feature_major(m, lambda nt: ps[j][:, T * nt:T * nt + T], ah, al).then_inc(s_mm, 1)

            def open_y():
                for b in range(4):
                    pe.matmul(ps[b][:, :], zb[:, 0:P], zb[:, :], start=True, stop=True)

            def rows_onto_y(m, ah, al):
                wh, wl = w_of(m, 2)
                for k in range(2):
                    t = slice(T * k, T * k + T)
                    for nt in range(KT):
                        y = ps[nt // 2][:, T * (nt % 2):T * (nt % 2) + T]
                        n = slice(nt * P, nt * P + P)
                        pe.matmul(y, wh[:, k, n], ah[:, t], start=False, stop=False, skip_group_check=True)
                        pe.matmul(y, wh[:, k, n], al[:, t], start=False, stop=False, skip_group_check=True)
                        mm = pe.matmul(y, wl[:, k, n], ah[:, t], start=False, stop=False, skip_group_check=True)
                return mm

            def ffn(f, o):
                m0, c0 = M_FF[f], 16 * f
                u0 = pl.um[m0]

                def ff_in(c, m, i=0):
                    split_ready(m, i)
                    if u0 + c >= MID:
                        pe.wait_ge(s_mid, u0 + c - MID + 1 + 3 * i)
                    bank = ps[4 + (u0 + c) % MID]
                    feature_major(m, lambda nt: bank[:, T * nt:T * nt + T], hh, hl).then_inc(s_mm, 1)

                def ff_out(c, m, i=0):
                    split_ready(m, i)
                    pe.wait_ge(s_fact, c0 + c + 1 + 3 * i)
                    rows_onto_y(m, fhi[:, c % 3, :], flo[:, c % 3, :]).then_inc(s_mm, 1)

                pe.wait_ge(s_h, 4 * o + 4)
                ff_in(0, m0)
                open_y()
                with pe.Fori(0, 5) as i:
                    for j in range(3):
                        ff_in(j + 1, m0 + 1 + 2 * j, i)
                        ff_out(j, m0 + 2 + 2 * j, i)
                ff_out(15, m0 + 31)

            def boundary(k, b1):
                mean_square(k)
                if b1 is not None:
                    ada_half(b1, 0)
                    ada_half(b1, 1)
                    mean_square(k + 1)
                    ada_sum(b1)
                else:
                    mean_square(k + 1)

            pe.wait_ge(s_const, 5)
            pe.wait_ge(s_vrow, 16 * 20)
            for i in range(6):
                if i >= 2:
                    pe.wait_ge(s_vec, i - 1)
                dst = ps[7] if i % 2 == 0 else ps[6]
                pe.transpose(dst[:, 0:NV[i]], vrow[0:NV[i], i, :], ident[0:NV[i], 0:NV[i]]).then_inc(s_vT, 1)
                if i == 0:
                    pe.wait_ge(s_x0, 16)
                    for b in range(4):
                        for q in range(4):
                            kt, tt = 2 * b + q // 2, q % 2
                            mm = pe.transpose(ps[b][:, q * P:q * P + P], x_tm[:, tt, kt * P:kt * P + P], ident[:, :])
                        mm.then_inc(s_xT, 1)
            if has("gmlp"):
                pe.wait_ge(s_gm, 64)
                pe.wait_ge(s_x, 4)
                for b in range(2):
                    for q in range(4):
                        mm = pe.transpose(ps[b][:, q * P:q * P + P], ws[:, 4 * b + q, :], ident[:, :])
                    mm.then_inc(s_wsT, 1)
            pe.wait_ge(s_vec, 6)
            mean_square(0)
            pe.wait_ge(s_cp, 3)
            ada_half(B0SH, 0)
            ada_half(B0SH, 1)
            ada_sum(B0SH)
            if has("gmlp"):
                pe.wait_ge(s_h, 4)
                for j in range(4):
                    linear_mid(M_V[j], hh, hl, tm=True)
                for j in range(4):
                    linear_mid(M_U[j], hh, hl)
                ada_half(B0G, 0)
                ada_half(B0G, 1)
                ada_half(B0SC, 0)
                ada_sum(B0G)
                ada_half(B0SC, 1)
                pe.wait_ge(s_wT, 1)
                pe.wait_ge(s_vn, 2)
                pe.wait_ge(s_wTc, 2)
                for b in range(4):
                    for g in (2 * b, 2 * b + 1):
                        for tt in range(2):
                            c0 = (g % 2) * T + tt * P
                            mm = pe.matmul(ps[b][:, c0:c0 + P], v_tm[:, tt, g * P:g * P + P], wT[:, g, :], start=True, stop=True)
                    mm.then_inc(s_mix, 1)
                ada_sum(B0SC)
                pe.wait_ge(s_oa, 4)
                for j in range(4):
                    linear_y(M_AO[j], j, hh, hl)
                if has("ffn0"):
                    boundary(1, B1SH)
                else:
                    mean_square(1)
            if has("ffn0"):
                pe.wait_ge(s_yfree, 4)
                ffn(0, 1)
                mean_square(3)

            if has("attn"):
                ada_half(BKV, 0)
                ada_half(BKV, 1)
                mean_square(4)
                ada_sum(BKV)
                pe.wait_ge(s_h, 12)
                for m in (M_KC, M_VC, M_KS, M_KW):
                    linear_mid(m, gh, gl)
                for m in (M_VS, M_VW):
                    linear_mid(m, gh, gl, tm=True)
                for j in range(2):
                    pe.wait_ge(s_blk, j + 1)
                    for c in range(2):
                        m = M_CW[j][c]
                        split_ready(m)
                        wh, wl = w_of(m)
                        for nt in range(2):
                            n = slice(P * nt, P * nt + P)
                            dst = ps[2 * j + nt][:, 0:60]
                            for i in range(8):
                                ah, al = bhi[:, 8 * c + i, :], blo[:, 8 * c + i, :]
                                pe.matmul(dst, wh[:, i, n], ah, start=c == 0 and i == 0, stop=False)
                                pe.matmul(dst, wh[:, i, n], al, start=False, stop=False)
                                mm = pe.matmul(dst, wl[:, i, n], ah, start=False, stop=c == 1 and i == 7)
                        mm.then_inc(s_mm, 1)
                    pe.wait_ge(s_h, 16)
                    for c in range(2):
                        linear_mid(M_Q[2 * j + c], hh, hl)
                linear_mid(M_GT, hh, hl, tm=True)
                ada_half(B1G, 0)
                ada_half(B1G, 1)
                pe.wait_ge(s_hid, 4)
                pe.wait_ge(s_aw, 96)
                for nt in range(2):
                    pe.matmul(ps[0][:, 0:60], w2k[:, nt, :], hid[:, 0, nt, :], start=nt == 0, stop=nt == 1)
                for g in range(NG):
                    for nt in range(2):
                        mm = pe.matmul(ps[1][0:NC, HD * g:HD * g + HD], hid[:, 1, nt, NC * g:NC * g + NC], w2v[:, nt, :],
                                       start=nt == 0, stop=nt == 1)
                mm.then_inc(s_w2, 1)
                pe.wait_ge(s_kv, 2)
                pe.wait_ge(s_kcp, 128)
                pe.wait_ge(s_mid, pl.ua[8 * B1G + 7] + 1)

                def scores(h):
                    if h:
                        pe.wait_ge(s_Sev, h)
                    b, g = slice(64 * (h % 2), 64 * (h % 2) + 64), h // 4
                    for qt in range(2):
                        q = qT[b, h // 2, P * qt:P * qt + P]
                        nk = P * (qt + 1)
                        pe.matmul(ps[qt][:, 0:NCP + nk], q, kc[b, g, 0:NCP + nk], start=True, stop=True)
                        mm = pe.matmul(score_psum(qt, 2), q, kw[b, g, 0:nk], start=True, stop=True)
                    mm.then_inc(s_S, 1)

                def turn(h):
                    hb = h % 2
                    pe.wait_ge(s_p, h + 1)
                    if h:
                        pe.wait_ge(s_Tev, 2 * h)
                        pe.wait_ge(s_TevD, 2 * h)
                    for br in (1, 2):
                        bank = ps[2 + br]
                        for qt in range(2):
                            at_ = part(qt, br).start
                            for kt in range(qt + 1):
                                pe.transpose(bank[:, (kt * T + (qt - kt) * P):(kt * T + (qt - kt) * P) + P],
                                             pp[:, hb, at_ + P * kt:at_ + P * kt + P], ident[:, :])
                        mm = pe.transpose(bank[0:NCP, 384:512], pp[:, hb, part(br - 1, 0)], ident[:, :])
                    mm.then_inc(s_T, 1)

                def values(h):
                    hb, g = h % 2, h // 4
                    if h % 2 == 0 and h >= 4:
                        pe.wait_ge(s_oev, h // 2 - 1)
                    pe.wait_ge(s_Tev, 2 * h + 2)
                    pe.wait_ge(s_TevD, 2 * h + 2)
                    o = ps[5 + (h // 2) % 2][64 * (h % 2):64 * (h % 2) + 64, :]
                    n = slice(HD * g, HD * g + HD)
                    pe.matmul(o[:, 0:T], v_s[:, 0, n], pts[:, hb, 0:T], start=True, stop=False)
                    pe.matmul(o[:, P:T], v_s[:, 1, n], pts[:, hb, T:T + P], start=False, stop=False)
                    pe.matmul(o[:, P:T], v_w[:, 1, n], pts[:, hb, 512 + T:512 + T + P], start=False, stop=False)
                    for qt in range(2):
                        pe.matmul(o[:, P * qt:P * qt + P], vcs[0:NC, g, :], pts[0:NC, hb, 512 * qt + 384:512 * qt + 512],
                                  start=False, stop=False)
                    pe.matmul(o[:, 0:T], v_w[:, 0, n], pts[:, hb, 512:512 + T], start=False, stop=True).then_inc(s_O, 1)

                scores(0)
                for h in range(NH):
                    if h + 1 < NH:
                        scores(h + 1)
                    turn(h)
                    values(h)
                ada_sum(B1G)
                pe.wait_ge(s_oh, 8)
                for j in range(4):
                    linear_y(M_BO[j], j, hh, hl)
                if not has("ffn1"):
                    mean_square(5)

            if has("ffn1"):
                boundary(5, B1SC)
                pe.wait_ge(s_yfree, 12)
                ffn(1, 4)
                mean_square(7)

            if has("gla"):
                ada_half(B2SH, 0)
                ada_half(B2SH, 1)
                mean_square(8)
                pe.wait_ge(s_ctx, 16)
                for b in range(4):
                    pe.wait_ge(s_yfree, 16 - 3 + b)
                    for q in range(4):
                        kt, tt = 2 * b + q // 2, q % 2
                        mm = pe.transpose(ps[b][:, q * P:q * P + P], ctx_tm[:, tt, kt * P:kt * P + P], ident[:, :])
                    mm.then_inc(s_cT, 1)
                ada_sum(B2SH)
                mean_square(9)

                def linear_two(m, tm):
                    split_ready(m)
                    w = pl.width[m] // KT
                    for i, (ah, al_, t_) in enumerate(((hh, hl, tm[0]), (gh, gl, tm[1]))):
                        u = pl.um[m] + i
                        if i and m == M_K2:
                            pe.wait_ge(s_h, 28)
                        mid_free(u)
                        if t_:
                            mm = token_major(m, lambda tt: ps[4 + u % MID][:, w * tt:w * tt + w], ah, al_)
                        else:
                            mm = feature_major(m, lambda nt: ps[4 + u % MID][:, T * nt:T * nt + T], ah, al_)
                    mm.then_inc(s_mm, 1)

                pe.wait_ge(s_h, 24)
                linear_two(M_K2, (False, True))
                for j in range(2):
                    linear_two(M_V2[j], (True, True))
                linear_two(M_AL, (False, False))
                linear_mid(M_Q2, hh, hl)
                pe.wait_ge(s_mid, pl.um[M_AL] + 2)
                pe.wait_ge(s_wab, 64)
                pe.wait_ge(s_gm3, 2)
                pe.wait_ge(s_cx, 4)
                for tt in range(2):
                    pe.matmul(ps[tt][:, :], alc[:, P * tt:P * tt + P], wab[:, :], start=True, stop=True)
                for j in range(4):
                    mm = pe.matmul(ps[2 + j // 2][:, T * (j % 2):T * (j % 2) + T], wab[:, P * j:P * j + P], alx[:, :], start=True, stop=True)
                mm.then_inc(s_gp, 1)
                for j in range(2):
                    linear_mid(M_OG[j], hh, hl)
                pe.wait_ge(s_gm3, 4)
                pe.wait_ge(s_g, 2)
                ones = one1[:, 0:P]
                pe.matmul(ps[0][:, 0:T], trif[:, :], gc[:, 0, 0:T], start=True, stop=False)
                pe.matmul(ps[0][:, 0:T], ones, gc[:, 1, 0:T], start=False, stop=True)
                pe.matmul(ps[1][:, 0:T], trif[:, :], gc[:, 1, 0:T], start=True, stop=True)
                pe.matmul(ps[0][:, T:512], trib[:, :], gc[:, 0, T:512], start=True, stop=True)
                pe.matmul(ps[1][:, T:512], trib[:, :], gc[:, 1, T:512], start=True, stop=False)
                pe.matmul(ps[1][:, T:512], ones, gc[:, 0, T:512], start=False, stop=True).then_inc(s_cum, 1)
                for j in range(2):
                    linear_mid(M_SC[j], hh, hl)
                pe.wait_ge(s_kd, 1)
                pe.wait_ge(s_g, 4)
                for f in range(2):
                    for h in range(GHD):
                        dst = ps[2][64 * (h % 2):64 * (h % 2) + 64, 256 * f + P * (h // 2):256 * f + P * (h // 2) + P]
                        for tt in range(2):
                            mm = pe.matmul(dst, wc[:, tt, 256 * f + 64 * h:256 * f + 64 * h + 64], vctx[:, tt, P * h:P * h + P],
                                           start=tt == 0, stop=tt == 1)
                mm.then_inc(s_st, 1)
                for j in range(2):
                    linear_mid(M_SX[j], hh, hl)
                for j in range(2):
                    linear_mid(M_SB[j], hh, hl)

                def level(n):
                    if n == 0:
                        pe.wait_ge(s_ste, 1)
                        pe.wait_ge(s_mid, pl.um[M_Q2] + 1)
                        op = qk[:, :, :]
                    else:
                        pe.wait_ge(s_E, n)
                        op = eb[:, (n - 1) % 2, :, :]
                    if n >= 2:
                        pe.wait_ge(s_A, n - 1)
                    for jt in range(2):
                        it = 1 - jt if n == 1 else jt
                        for h in range(GHD):
                            b = slice(64 * (h % 2), 64 * (h % 2) + 64)
                            c = 2 * jt + h // 2
                            mm = pe.matmul(ps[2 * (n % 2) + h % 2][:, P * c:P * c + P], op[b, 2 + h // 2, P * jt:P * jt + P],
                                           op[b, h // 2, P * it:P * it + P], start=True, stop=True)
                    mm.then_inc(s_lev, 1)

                level(0)
                for n in range(1, 9):
                    level(n)
                    ada(8 * B2G + n - 1, 1)
                pe.wait_ge(s_qi, 1)
                pe.wait_ge(s_A, 9)
                for h in range(GHD):
                    b = slice(64 * (h % 2), 64 * (h % 2) + 64)
                    o = ps[2 + h % 2][:, T * (h // 2):T * (h // 2) + T]
                    for f in range(2):
                        pe.matmul(o, st[b, f, h // 2, :], qi[b, 2 * f + h // 2, :], start=f == 0, stop=False)
                    for it in range(2):
                        for jt in range(2):
                            a_ = (a_d if it == jt else a_x)[:, h % 2, jt, h // 2, :]
                            mm = pe.matmul(o[:, P * it:P * it + P], vx[:, jt, P * h:P * h + P], a_, start=False, stop=it + jt == 2)
                mm.then_inc(s_o4, 1)
                pe.wait_ge(s_o2, 1)
                for b in range(2):
                    mm = pe.matmul(ps[b][:, :], onesm[:, :], o2[:, 2 * b:2 * b + 2, :].rearrange("p k t -> p (k t)"), start=True, stop=True)
                mm.then_inc(s_ms4, 1)
                ada_sum(B2G)
                pe.wait_ge(s_cv, 1)
                pe.wait_ge(s_gs, 1)
                for j in range(4):
                    linear_y(M_WO[j], j, hh, hl)
                if not has("ffn2"):
                    mean_square(10)

            if has("ffn2"):
                boundary(10, B2SC)
                pe.wait_ge(s_yfree, 20)
                pe.wait_ge(s_h, 32)
                pe.wait_ge(s_mid, pl.ua[8 * B2SC + 7] + 1)

                def up(m, bank, i=0):
                    split_ready(m, i)
                    feature_major(m, lambda nt: ps[bank][:, T * nt:T * nt + T], hh, hl).then_inc(s_mm, 1)

                def conv_body(c, i=0):
                    if c:
                        pe.wait_ge(s_ue, c + 2 * i)
                    up(M_UP + 3 * c + 2, 4 + (c + 1) % 2, i)
                    if c:
                        pe.wait_ge(s_fa, c + 2 * i)
                    up(M_UP + 3 * c + 3, 6 + (c + 1) % 2, i)
                    down(c, M_UP + 3 * c + 4, i)

                def down(c, m, i=0):
                    split_ready(m, i)
                    pe.wait_ge(s_cact, c + 1 + 2 * i)
                    rows_onto_y(m, chi[:, c % 2, :], clo[:, c % 2, :]).then_inc(s_mm, 1)

                up(M_UP, 4)
                up(M_UP + 1, 6)
                open_y()
                conv_body(0)
                with pe.Fori(0, 4) as i:
                    for j in range(2):
                        conv_body(1 + j, i)
                conv_body(9)
                down(10, M_UP + 32)
                mean_square(12)

            pe.wait_ge(s_x, 4 * N_UPD + 4)
            pe.wait_ge(s_yfree, 4 * N_UPD) if N_UPD else None
            pe.wait_ge(s_wTc, 2) if has("gmlp") else None
            for b in range(4):
                for q in range(4):
                    kt = 4 * (b % 2) + q
                    mm = pe.transpose(ps[b][:, q * P:q * P + P], x[:, kt, (b // 2) * P:(b // 2) * P + P], ident[:, :])
                mm.then_inc(s_oT, 1)

        @block.gpsimd
        def _(pool):
            chain = [0]

            def link(ins):
                ins.then_inc(g_ch, 1)
                chain[0] += 1
                pool.wait_ge(g_ch, chain[0])

            link(pool.memset(ident[:, :], 0.0))
            pool.affine_select(out=ident[:, :], in_=ident[:, :], compare_op=ALU.not_equal, fill=1.0, base=0,
                               pattern=[[-1, P]], channel_multiplier=1).then_inc(s_const, 1)
            pool.memset(onesm[:, :], 1.0 / D).then_inc(s_const, 1)
            pool.memset(zb[:, :], 0.0).then_inc(s_const, 1)
            pool.memset(one1[:, :], 1.0).then_inc(s_const, 1)
            pool.memset(eps[:, :], EPS).then_inc(s_const, 1)
            pool.memset(cpad[:, :, :, :], 0.0).then_inc(s_cpad0, 1)
            if has("gmlp"):
                pool.wait_ge(s_wTc, 2)
                pool.affine_select(out=wT[:, :, :], in_=wT[:, :, :], compare_op=ALU.is_ge, fill=0.0, base=0,
                                   pattern=[[0, 8], [1, P]], channel_multiplier=-1).then_inc(s_wT, 1)

            if has("attn"):
                pool.wait_ge(s_mm, M_FF[0] + 32)
                link(pool.memset(cmask[:, :], 0.0))
                pool.affine_select(out=cmask[:, :], in_=cmask[:, :], compare_op=ALU.is_ge, fill=NEG, base=P,
                                   pattern=[[-1, T]], channel_multiplier=1).then_inc(s_asm, 1)
                for m_, keep, fill in ((cmm, 0.0, NEG), (cm01, 1.0, 0.0)):
                    link(pool.memset(m_[:, :, :], keep))
                    pool.affine_select(out=m_[:, :, :], in_=m_[:, :, :], compare_op=ALU.is_ge, fill=fill, base=-31,
                                       pattern=[[P, 2], [-16, NCP]], channel_multiplier=1).then_inc(s_asm, 1)

            if has("gla"):
                pool.wait_ge(s_mm, M_FF[1] + 32)
                pool.memset(wab[:, :], 0.0).then_inc(s_wz, 1)
                pool.wait_ge(s_wz, 1)
                for n, a in enumerate((alx, alc)):
                    pool.memset(a[32:33, :], 1.0).then_inc(s_gm3, 1)
                    pool.wait_ge(s_gm3, n + 1)
                for tri, cm in ((trif, 1), (trib, -1)):
                    link(pool.memset(tri[:, :], 1.0))
                    pool.affine_select(out=tri[:, :], in_=tri[:, :], compare_op=ALU.is_ge, fill=0.0, base=-1,
                                       pattern=[[-cm, P]], channel_multiplier=cm).then_inc(s_gm3, 1)
                link(pool.memset(lmask[:, :, :], 1.0))
                for n in range(7):
                    s = 64 >> n
                    v = lmask[:, n, :].rearrange("p (b a e) -> p b a e", a=2, e=s)
                    link(pool.affine_select(out=v, in_=v, compare_op=ALU.is_ge, fill=0.0, base=-s,
                                            pattern=[[-2 * s, P // (2 * s)], [s, 2], [0, s]], channel_multiplier=1))
                    ins = pool.affine_select(out=v, in_=v, compare_op=ALU.is_ge, fill=0.0, base=2 * s - 1,
                                             pattern=[[2 * s, P // (2 * s)], [-s, 2], [0, s]], channel_multiplier=-1)
                    if n < 6:
                        link(ins)
                ins.then_inc(s_gm3, 5)
                pool.wait_ge(s_B, 1)
                for l in range(8):
                    s = 128 >> l
                    if l >= 2:
                        pool.wait_ge(s_lev, l)
                    blocks = lambda a: a.rearrange("p k (b e) -> p k b e", e=2 * s)
                    fw, bw = blocks(bx[:, 0:2, :]), blocks(bx[:, 2:4, :])
                    eq, ek = blocks(eb[:, l % 2, 0:2, :]), blocks(eb[:, l % 2, 2:4, :])
                    shape = [P, 2, T // (2 * s), s]
                    fm_, bm = fw[:, :, :, s - 1:s].broadcast_to(shape), bw[:, :, :, s:s + 1].broadcast_to(shape)
                    left, right = slice(0, s), slice(s, 2 * s)
                    pool.tensor_tensor(eq[:, :, :, right], fw[:, :, :, right], fm_, ALU.subtract)
                    pool.tensor_tensor(ek[:, :, :, left], fm_, fw[:, :, :, left], ALU.subtract)
                    pool.tensor_tensor(eq[:, :, :, left], bm, bw[:, :, :, left], ALU.subtract)
                    pool.tensor_tensor(ek[:, :, :, right], bw[:, :, :, right], bm, ALU.subtract).then_inc(s_D, 1)


_INS = ["x", "c", "ada_w", "ada_b", "norm_g", "a_w_in", "a_ln_g", "a_ln_b", "a_w_s", "a_b_s", "a_w_out", "kv_ada_w",
        "kv_ada_b", "kv_norm_g", "kv_w", "cmp_pos", "cmp_w1", "cmp_b1", "cmp_w2", "cmp_b2", "b_w_in", "b_w_out",
        "ff_w_in", "ff_w_out", "c_2", "ctx_2", "c_ctx_2", "w_ada_2", "b_ada_2", "g_pre_mix_2", "g_post_mix_2",
        "g_pre_ffn_2", "g_post_ffn_2", "w_in_2", "w_af_2", "b_af_2", "w_ab_2", "b_ab_2", "g_head_2", "w_sc_2",
        "b_sc_2", "w_out_2", "w_up_2", "w_cf_2", "b_cf_2", "w_down_2"]
_OUTS = [((1, 256, 1024), "float32")]


def kernel(**inputs):
    import numpy as _np
    import concourse.bacc as _bacc
    from concourse import mybir as _mybir
    from concourse.bass_utils import run_bass_kernel_spmd as _run

    nc = _bacc.Bacc("TRN2", target_bir_lowering=False, num_devices=1)
    arrays, args = {}, {}
    for name in _INS:
        a = _np.ascontiguousarray(inputs[name])
        arrays[f"in_{name}_dram"] = a
        args[name] = nc.dram_tensor(f"in_{name}_dram", a.shape, _mybir.dt.from_np(a.dtype), kind="ExternalInput").ap()
    shape, dtype = _OUTS[0]
    res = nc.dram_tensor("out_0_dram", shape, _mybir.dt.from_np(_np.dtype(dtype)), kind="ExternalOutput").ap()
    build(nc, args, res)
    r = _run(nc, [arrays], core_ids=[0])
    return r.results[0]["out_0_dram"]
```

```python
import concourse.bass as bass
from concourse import mybir

F32 = mybir.dt.float32
F32R = mybir.dt.float32r
BF16 = mybir.dt.bfloat16
I8 = mybir.dt.int8
ALU = mybir.AluOpType
ACT = mybir.ActivationFunctionType
AX = mybir.AxisListType

P = 128
T = 256
D = 1024
KT = D // P
EPS = 1e-6
NEG = -1e30
CH = 2048
RAW = 6
SPL = 3
MID = 3

STAGES = ["x", "gmlp", "ffn0", "attn", "ffn1", "gla", "ffn2"]


class Plan:

    def __init__(self):
        self.src, self.kind, self.order = [], [], []
        self.nm, self.na, self.um, self.ua = [], [], [], []
        self.width = []
        self.u = 0
        self.bank = []

    def m(self, src, mids=1, width=CH):
        self.nm.append(len(self.src))
        self.um.append(self.u)
        self.bank += [4 + (self.u + i) % MID for i in range(mids)]
        self.u += mids
        self.kind.append("M")
        self.order.append(len(self.nm) - 1)
        self.width.append(width)
        self.src.append(src)
        return len(self.nm) - 1

    def a(self, src, bank):
        self.na.append(len(self.src))
        self.ua.append(self.u)
        self.bank.append(bank)
        self.u += 1
        self.kind.append("A")
        self.order.append(len(self.na) - 1)
        self.src.append(src)

    def before(self, u):
        return max([v + 1 for v in range(u) if self.bank[v] == self.bank[u]], default=0)


def cols(w, c0, n=256):
    return w.rearrange("(k p) n -> p k n", p=P)[:, :, c0:c0 + n]


def rows(w, r0, n=2):
    return w.rearrange("(k p) n -> p k n", p=P)[:, r0:r0 + n, :]


def build(nc, I, out, upto="ffn2"):
    stage_n = STAGES.index(upto)

    def has(s):
        return stage_n >= STAGES.index(s)

    pl = Plan()
    ada = {0: I["ada_w"][0], 1: I["ada_w"][1], 2: I["w_ada_2"][0], "kv": I["kv_ada_w"]}
    BATCH = [(0, 0), (0, 1), (0, 2), (1, 0), ("kv", 0), (1, 1), (1, 2), (2, 0), (2, 1), (2, 2)]
    B0SH, B0G, B0SC, B1SH, BKV, B1G, B1SC, B2SH, B2G, B2SC = range(10)

    SUMS = {}

    def ada_batch(b, more=0):
        w, third = BATCH[b]
        if b in (B1G, B1SC):
            SUMS[b] = (7, T + 32 * (b - B1G))
            banks = [7, 7]
        else:
            SUMS[b] = (4 + (pl.u + 8 + more + 2) % MID, 0)
            banks = [k for k in (4, 5, 6) if k != SUMS[b][0]]
        for j in range(8):
            pl.a(cols(ada[w], 2048 * third + 256 * j), banks[j % 2])

    ada_batch(B0SH)
    if has("gmlp"):
        M_V = [pl.m(cols(I["a_w_in"][0], 1024 + 256 * j)) for j in range(4)]
        M_U = [pl.m(cols(I["a_w_in"][0], 256 * j)) for j in range(4)]
        ada_batch(B0G, 8)
        ada_batch(B0SC)
        M_AO = [pl.m(cols(I["a_w_out"][0], 256 * j), 0) for j in range(4)]
    M_FF = {}
    if has("ffn0"):
        ada_batch(B1SH)

    def ffn_chunks(f):
        m0 = pl.m(cols(I["ff_w_in"][f], 0))
        for c in range(15):
            pl.m(cols(I["ff_w_in"][f], 256 * (c + 1)))
            pl.m(rows(I["ff_w_out"][f], 2 * c), 0)
        pl.m(rows(I["ff_w_out"][f], 30), 0)
        M_FF[f] = m0

    if has("ffn0"):
        ffn_chunks(0)
    if has("attn"):
        ada_batch(BKV)
        M_KC, M_VC, M_KS, M_KW, M_VS, M_VW = [pl.m(cols(I["kv_w"], 256 * j)) for j in (0, 1, 2, 4, 3, 5)]
        M_Q = [pl.m(cols(I["b_w_in"][0], 256 * c)) for c in range(4)]
        M_GT = pl.m(cols(I["b_w_in"][0], 1024, 48), 1, 384)
        M_CW = [[pl.m(rows(I["cmp_w1"][j], 8 * c, 8), 0) for c in range(2)] for j in range(2)]
        ada_batch(B1G)
        ada_batch(B1SC)
        M_BO = [pl.m(cols(I["b_w_out"][0], 256 * j), 0) for j in range(4)]
    if has("ffn1"):
        ada_batch(B2SH)
        ffn_chunks(1)
    if has("gla"):
        ada_batch(B2G)
        w2 = I["w_in_2"][0]
        M_K2 = pl.m(cols(w2, 0), 2)
        M_V2 = [pl.m(cols(w2, 256 + 256 * j), 2) for j in range(2)]
        M_AL = pl.m(cols(w2, 768, 128), 2, 1024)
        M_Q2 = pl.m(cols(w2, 800))
        M_OG = [pl.m(cols(w2, 1056 + 256 * j)) for j in range(2)]
        M_SC = [pl.m(cols(w2, 2080 + 256 * j)) for j in range(2)]
        M_SX = [pl.m(cols(w2, 2592 + 256 * j)) for j in range(2)]
        M_SB = [pl.m(cols(w2, 1568 + 256 * j)) for j in range(2)]
        ada_batch(B2SC)
        M_WO = [pl.m(cols(I["w_out_2"][0], 256 * j), 0) for j in range(4)]
    if has("ffn2"):
        wup, wdn = I["w_up_2"][0], I["w_down_2"][0]
        M_UP = pl.m(cols(wup, 0), 0)
        pl.m(cols(wup, 2816), 0)
        for c in range(10):
            pl.m(cols(wup, 256 * (c + 1)), 0)
            pl.m(cols(wup, 2816 + 256 * (c + 1)), 0)
            pl.m(rows(wdn, 2 * c), 0)
        pl.m(rows(wdn, 20), 0)
    NM, NN = len(pl.nm), len(pl.src)

    at = [16512]

    def take(nbytes):
        o = at[0]
        at[0] += (nbytes + 31) // 32 * 32
        return o

    def sb(name, shape, dt=F32, off=None):
        size = 1
        for s in shape[1:]:
            size *= s
        size *= {F32: 4, F32R: 4, BF16: 2, I8: 1}[dt]
        return nc.alloc_sbuf_tensor_at(name, shape, dt, offset=take(size) if off is None else off)

    raw = sb("raw", [P, RAW, CH])
    whi = sb("whi", [P, SPL, CH], F32R)
    wlo = sb("wlo", [P, SPL, CH], F32R)
    x = sb("x", [P, KT, T])
    hh = sb("hh", [P, KT, T], F32R)
    hl = sb("hl", [P, KT, T], F32R)
    oK = take(16384)
    gh = sb("gh", [P, KT, T], F32R, oK)
    gl = sb("gl", [P, KT, T], F32R, oK + 8192)
    oS = take(24576)
    sq = sb("sq", [P, KT, T], F32, oS)
    tt_ = sb("tt_", [P, KT, T], F32, oS + 8192)
    h32 = sb("h32", [P, KT, T], F32, oS + 16384)
    ident = sb("ident", [P, P])
    onesm = sb("onesm", [P, P])
    one1 = sb("one1", [P, 256])
    zero1 = sb("zero1", [P, 1])
    zb = sb("zb", [P, 512], BF16)
    NV = [96, 107, 99, 99, 112, 48]
    V0 = [sum(NV[:i]) for i in range(7)]
    vec = sb("vec", [P, V0[6]])
    mod = sb("mod", [P, 11, 16])
    coef = sb("coef", [P, 14, KT])
    csil = sb("csil", [P, 24])
    cpad = sb("cpad", [P, 2, KT, 32])
    stage = sb("stage", [P, 4, 256])
    sel = sb("sel", [P, 2])
    vv = sb("vv", [P, T])
    r0 = sb("r0", [P, T])
    n1 = sb("n1", [P, T])
    rs = sb("rs", [P, T])
    oP = at[0]
    LIMIT = 229368

    def region(base, end):
        pos = [base]

        def f(name, shape, dt=F32):
            size = 1
            for s in shape[1:]:
                size *= s
            size *= {F32: 4, F32R: 4, BF16: 2, I8: 1}[dt]
            o = pos[0]
            pos[0] += (size + 31) // 32 * 32
            assert pos[0] <= end, (name, pos[0], end)
            return nc.alloc_sbuf_tensor_at(name, shape, dt, offset=o)

        return f

    r = region(oP, LIMIT)
    wT = r("wT", [P, 8, P])
    bs_b = r("bs_b", [P, 8, P])
    lng = r("lng", [P, D])
    lnb = r("lnb", [P, D])
    ws = r("ws", [P, 8, P])
    bst = r("bst", [P, 2, 2, 6])
    mv = r("mv", [P, 2, 2])
    lr = r("lr", [P, 4, 2])
    rK = region(oK, oK + 16384)
    v_tm = rK("v_tm", [P, 2, D])
    u_fm = rK("u_fm", [P, KT, T])
    x_tm = sb("x_tm", [P, 2, D], F32, oS + 8192)
    vrow = sb("vrow", [P, 6, P], F32, oS + 16384)
    r = region(oP, LIMIT)
    fr = r("fr", [P, 512])
    fm = r("fm", [P, 512])
    fhi = r("fhi", [P, 3, 512], F32R)
    flo = r("flo", [P, 3, 512], F32R)
    y_tm = sb("y_tm", [P, 2, D], F32, oS + 8192)

    NC, NCP, HD, NG, NH = 15, 16, 64, 4, 16
    r = region(oP, LIMIT)
    kc = r("kc", [P, NG, NCP + T])
    kw = r("kw", [P, NG, T])
    v_s = r("v_s", [P, 2, NG * HD])
    v_w = r("v_w", [P, 2, NG * HD])
    ks_fm = r("ks_fm", [P, 2, T])
    kw_fm = r("kw_fm", [P, 2, T])
    cmask = r("cmask", [P, T])
    cmm = r("cmm", [P, 2, NCP])
    cm01 = r("cm01", [P, 2, NCP])
    gate = r("gate", [P, 2, 48])
    hid = r("hid", [P, 2, 2, 60])
    w2k = r("w2k", [P, 2, P])
    w2v = r("w2v", [P, 2, HD])
    b2k = r("b2k", [P, 1])
    b2v = r("b2v", [NCP, HD])
    vcs = r("vcs", [NCP, NG, HD])
    mx = r("mx", [P, 2, 6])
    nb = r("nb", [P, 2, 6])
    den = r("den", [P, 2, 6])
    rec = r("rec", [P, 2, 6])
    cf = r("cf", [P, 2, 6])
    qT = sb("qT", [P, KT, T], F32, oK)
    pp = sb("pp", [P, 2, 800], F32, oK + 8192)
    bsh = [sb(f"bsh{j}", [P, NG, T], F32, oS + 8192 + 4096 * j) for j in range(2)]
    pts = sb("pts", [P, 2, 1024], F32, oS + 8192)
    rS = region(oS + 16384, oS + 24576)
    blk = rS("blk", [P, 16, NG, NC])
    kc_fm = rS("kc_fm", [P, 2, T])
    vc_fm = rS("vc_fm", [P, 2, T])
    rS = region(oS, oS + 8192)
    bhi = rS("bhi", [P, 16, 60], F32R)
    blo = rS("blo", [P, 16, 60], F32R)

    GHD = 4
    r = region(oP, LIMIT)
    qk = r("qk", [P, 4, T])
    kctx = r("kctx", [P, 2, T])
    o_v = oP + 6144
    vx = r("vx", [P, 2, 512])
    vctx = r("vctx", [P, 2, 512])
    cx = sb("cx", [P, KT, T], F32, o_v)
    alx = r("alx", [33, T])
    alc = r("alc", [33, T])
    wab = r("wab", [33, 512])
    st = r("st", [P, 2, 2, P])
    trif = r("trif", [P, P])
    trib = r("trib", [P, P])
    lmask = r("lmask", [P, 7, P], I8)
    tot = r("tot", [P, 2])
    ctx_tm = sb("ctx_tm", [P, 2, D], F32, oK)
    rK = region(oK, oK + 16384)
    gc = rK("gc", [P, 2, 512])
    wc = rK("wc", [P, 2, 512])
    gx = rK("gx", [P, 4, T])
    bx = rK("bx", [P, 4, T])
    a_x = sb("a_x", [P, 2, 2, 2, P], F32, oK)
    a_d = sb("a_d", [P, 2, 2, 2, P], F32, oK + 4096)
    qi = sb("qi", [P, 4, T], F32, oK + 8192)
    r4 = sb("r4", [P, 4, T], F32, oK + 4096)
    v4 = sb("v4", [P, 4, T], F32, oK + 8192)
    n4 = sb("n4", [P, 4, T], F32, oK + 12288)
    rS = region(oS, oS + 24576)
    og = rS("og", [P, 4, T])
    sbt = rS("sbt", [P, 4, T])
    ct = rS("ct", [P, 4, T])
    sct = rS("sct", [P, 4, T])
    eb = rS("eb", [P, 2, 4, T])
    o2 = sb("o2", [P, 4, T], F32, oS + 16384)
    o4 = sb("o4", [P, 4, T], F32, oS + 20480)

    CF = I["w_down_2"].shape[1] // 256
    r = region(oP, LIMIT)
    ut = r("ut", [P, 2, T])
    cvt = r("cvt", [P, 2, T])
    sl = r("sl", [P, 2, T])
    fa = r("fa", [P, 2, T])
    chi = r("chi", [P, 2, 512], F32R)
    clo = r("clo", [P, 2, 512], F32R)

    ps = [nc.alloc_psum_tensor(f"bank{i}", [P, 512], F32) for i in range(8)]
    stat = ps[7][:, 0:256]

    def sums(b, c=0):
        bank, at_ = SUMS[b]
        return ps[bank][:, at_:at_ + 32].rearrange("p (n c) -> p n c", c=2)[:, :, c]


    sems = {}

    def sem(name):
        if name not in sems:
            sems[name] = nc.alloc_semaphore(name)
        return sems[name]

    raw_full = [sem(f"raw_full{i}") for i in range(RAW)]
    s_hi, s_lo, s_mm = sem("hi_ready"), sem("lo_ready"), sem("chunk_multiplied")
    s_ada = sem("ada_multiplied")
    s_mid = sem("mid_evacuated")

    def vc(tile, row):
        return V0[tile] + row

    C_NORM = [[vc(0, 24 + 8 * (4 * l + i)) for i in range(4)] for l in range(2)]
    C_KVN = vc(0, 88)
    C_PREMIX, C_POSTMIX, C_PREFFN, C_POSTFFN = (vc(1, 8 * i) for i in range(4))
    C_BSC, C_WSC, C_BCF, C_B1, C_GH, C_POS = vc(1, 32), vc(1, 36), vc(1, 48), vc(1, 70), vc(1, 74), vc(1, 75)
    C_WCF = V0[2]
    C_ADAB = V0[4]
    BIAS = [C_ADAB + {0: 0, 1: 48, "kv": 96, 2: 112}[w] + 16 * t for w, t in BATCH]

    (A_N0, G_N1, A_N2, G_N3, A_KV, A_N4, G_N5, A_N6, G_N7, A_N8, A_N9, G_N10, A_N11, G_N12) = range(14)
    SH = lambda b: mod[:, b, 0:8]
    SC = lambda b: mod[:, b, 8:16]
    COEFS = {
        B0SH: [(A_N0, "A", SC(B0SH), C_NORM[0][0])],
        B0G: [(G_N1, "G", SH(B0G), C_NORM[0][1])],
        B0SC: [(A_N2, "A", SH(B0SC), C_NORM[0][2]), (G_N3, "G", SC(B0SC), C_NORM[0][3])],
        B1SH: [(A_N4, "A", SC(B1SH), C_NORM[1][0])],
        BKV: [(A_KV, "A", SC(BKV), C_KVN)],
        B1G: [(G_N5, "G", SH(B1G), C_NORM[1][1])],
        B1SC: [(A_N6, "A", SH(B1SC), C_NORM[1][2]), (G_N7, "G", SC(B1SC), C_NORM[1][3])],
        B2SH: [(A_N8, "A", SC(B2SH), C_PREMIX), (A_N9, "A", SC(10), C_PREMIX)],
        B2G: [(G_N10, "G", SH(B2G), C_POSTMIX)],
        B2SC: [(A_N11, "A", SH(B2SC), C_PREFFN), (G_N12, "G", SC(B2SC), C_POSTFFN)],
    }

    s_vrow, s_x0, s_gm = sem("vec_rows_loaded"), sem("x_loaded"), sem("gmlp_rows_loaded")
    s_const, s_cpad0 = sem("constants_ready"), sem("cpad_zeroed")
    s_vT, s_vec = sem("vec_transposed"), sem("vec_ready")
    s_sg, s_cp = sem("c_silu"), sem("c_padded")
    s_xT, s_x = sem("x_transposed"), sem("x_ready")
    s_col, s_mod, s_sel = sem("ada_columns_summed"), sem("mod_ready"), sem("row_selector_ready")
    s_v, s_r0, s_v2, s_r2 = sem("variance_ready"), sem("rsqrt_guess"), sem("other_variance_ready"), sem("other_rsqrt_guess")
    s_sq, s_stat, s_rs = sem("squares"), sem("mean_square"), sem("rsqrt_ready")
    s_t, s_hh, s_h = sem("normed"), sem("h_hi_ready"), sem("h_ready")
    s_yb = sem("y_bank_complete")
    s_yfree = sem("y_banks_free")
    s_vn = sem("v_normed")
    s_wsT, s_wTc, s_wT = sem("ws_transposed"), sem("ws_copied"), sem("ws_masked")
    s_mix, s_oa = sem("mixed"), sem("gmlp_out_split")
    s_fsq, s_fh, s_fact = sem("ffn_squared"), sem("ffn_hi"), sem("ffn_act_ready")
    s_oT, s_oc, s_out = sem("out_transposed"), sem("out_copied"), sem("out_stored")
    s_bsh = [sem("k_cmp_shifted"), sem("v_cmp_shifted")]
    s_kcp, s_asm, s_aw = sem("keys_doubled"), sem("attention_masks_ready"), sem("cmp_weights_loaded")
    s_blk, s_hid, s_w2, s_kv = sem("cmp_blocks_split"), sem("cmp_hidden"), sem("cmp_second"), sem("keys_values_ready")
    s_gt = sem("gates_ready")
    s_S, s_Sev, s_nb, s_exp, s_p = sem("scores"), sem("scores_evacuated"), sem("max_ready"), sem("exp_done"), sem("probs_ready")
    s_T, s_Tev, s_TevD, s_O, s_oev, s_oh = (sem("probs_transposed"), sem("sel_probs_copied"), sem("win_probs_copied"),
                                            sem("heads_done"), sem("pairs_evacuated"), sem("pairs_split"))
    s_ctx, s_cT, s_cx = sem("ctx_loaded"), sem("ctx_transposed"), sem("ctx_ready")
    s_wz, s_wab, s_al, s_gm3 = sem("gate_weights_zeroed"), sem("gate_weights_loaded"), sem("gate_rows_ready"), sem("gla_masks_ready")
    s_gp, s_la, s_g = sem("gates_multiplied"), sem("gates_logged"), sem("log_decays_ready")
    s_cum, s_wc, s_kd, s_st, s_ste = (sem("decays_summed"), sem("decays_to_end"), sem("ctx_keys_decayed"),
                                      sem("states_multiplied"), sem("states_ready"))
    s_qev, s_vev, s_B, s_qe, s_qi = (sem("q_k_ready"), sem("v_ready"), sem("decays_cumulated"), sem("state_decays"),
                                     sem("q_for_states"))
    s_D, s_Ex, s_E, s_lev, s_A = (sem("level_differences"), sem("level_decays"), sem("level_operands"),
                                  sem("level_multiplied"), sem("attention_filled"))
    s_og, s_sc, s_sx, s_sb, s_cv = sem("out_gate"), sem("sc_ready"), sem("sx_ready"), sem("sb_ready"), sem("conv_split")
    s_o4, s_o2, s_ms4, s_gs = sem("gla_heads_done"), sem("gla_squares"), sem("gla_mean_squares"), sem("gla_out_split")
    s_ue, s_tap, s_sil, s_fa, s_chi, s_cact = (sem("conv_input_ready"), sem("taps_added"), sem("conv_silu"),
                                               sem("conv_gated"), sem("conv_hi"), sem("conv_act_ready"))
    d_ch, a_ch, g_ch = sem("vector_chain"), sem("scalar_chain"), sem("gpsimd_chain")

    N_UPD = [0, 1, 2, 3, 4, 5, 6][stage_n]
    def part(qt, br):
        nk = P * (qt + 1)
        at0 = 0 if qt == 0 else NCP + 2 * P
        lo_, n = [(0, NCP), (NCP, nk), (NCP + nk, nk)][br]
        return slice(at0 + lo_, at0 + lo_ + n)

    def score_psum(qt, br):
        nk = P * (qt + 1)
        if qt == 0:
            return ps[0][:, part(0, br)]
        return ps[2][:, 0:T] if br == 2 else ps[1][:, [slice(0, NCP), slice(NCP, NCP + T)][br]]

    block = nc.Block()
    with block:

        def full(eng, n, i=0, per=1):
            eng.wait_ge(raw_full[n % RAW], 16 * (n // RAW + 1) + 16 * i)

        @block.sync
        def _(sp):
            x_rows = I["x"][0].rearrange("(t p) d -> p t d", p=P)

            def load(n, i=0, src=None, freed=None):
                if freed is None and n >= RAW:
                    k = pl.order[n - RAW]
                    if pl.kind[n - RAW] == "M":
                        sp.wait_ge(s_lo, k + 1)
                    else:
                        sp.wait_ge(s_ada, k + 1)
                elif freed is not None:
                    sp.wait_ge(s_lo, freed)
                s = pl.src[n] if src is None else src
                k, w = s.shape[1], s.shape[2]
                sp.dma_start(raw[:, n % RAW, 0:k * w].rearrange("p (k n) -> p k n", n=w), s)\
                  .then_inc(raw_full[n % RAW], 16)

            def ffn_loads(f):
                m0 = M_FF[f]
                n0 = pl.nm[m0]
                for n in range(n0, n0 + 7):
                    load(n)
                win = I["ff_w_in"][f].rearrange("(k p) n -> p k n", p=P)
                wout = I["ff_w_out"][f].rearrange("(k p) n -> p k n", p=P)
                with sp.Fori(1, 5) as i:
                    for j in range(3):
                        load(n0 + 1 + 2 * j, src=win[:, :, bass.ds(768 * i + 256 * (j + 1), 256)],
                             freed=m0 + 1 + 2 * j - 6 + 6 * i + 1)
                        load(n0 + 2 + 2 * j, src=wout[:, bass.ds(6 * i + 2 * j, 2), :],
                             freed=m0 + 2 + 2 * j - 6 + 6 * i + 1)
                load(n0 + 31)
                return n0 + 32

            def conv_loads():
                n0 = pl.nm[M_UP]
                for n in range(n0, n0 + 8):
                    load(n)
                wup_ = wup.rearrange("(k p) n -> p k n", p=P)
                wdn_ = wdn.rearrange("(k p) n -> p k n", p=P)
                ff2 = 256 * CF
                with sp.Fori(0, 4) as i:
                    for j in range(2):
                        c = 2 + j
                        for k, src in enumerate((wup_[:, :, bass.ds(512 * i + 256 * (c + 1), 256)],
                                                 wup_[:, :, bass.ds(512 * i + ff2 + 256 * (c + 1), 256)],
                                                 wdn_[:, bass.ds(4 * i + 2 * c, 2), :])):
                            m = 3 * c + 2 + k
                            load(n0 + m, src=src, freed=M_UP + m - 6 + 1 + 6 * i)
                load(n0 + 32)
                return n0 + 33

            sp.dma_start(x_tm[:, :, :], x_rows).then_inc(s_x0, 16)
            n = 0
            while n < NN:
                if pl.kind[n] == "M" and pl.order[n] in M_FF.values():
                    f = [k for k in M_FF if M_FF[k] == pl.order[n]][0]
                    n = ffn_loads(f)
                elif has("ffn2") and n == pl.nm[M_UP]:
                    n = conv_loads()
                else:
                    load(n)
                    n += 1
            sp.wait_ge(s_oc, 4)
            sp.dma_start(out[0].rearrange("(t p) d -> p t d", p=P), y_tm[:, :, :]).then_inc(s_out, 16)
            sp.wait_ge(s_out, 16)

        @block.scalar
        def _(act):
            chain = [0]

            def link(ins):
                ins.then_inc(a_ch, 1)
                chain[0] += 1
                act.wait_ge(a_ch, chain[0])

            def load_rows(tile, row, src):
                n = src.shape[0]
                act.dma_start(vrow[row:row + n, tile, :], src).then_inc(s_vrow, 16)

            v8 = lambda a: a.rearrange("(r p) -> r p", p=P)
            load_rows(0, 0, v8(I["c"][0]))
            load_rows(0, 8, v8(I["c_2"][0]))
            load_rows(0, 16, v8(I["c_ctx_2"]))
            load_rows(0, 24, I["norm_g"].rearrange("l i (r p) -> (l i r) p", p=P))
            load_rows(0, 88, v8(I["kv_norm_g"]))
            load_rows(4, 0, I["ada_b"].rearrange("l (r p) -> (l r) p", p=P))
            load_rows(4, 96, v8(I["kv_ada_b"]))
            load_rows(1, 0, v8(I["g_pre_mix_2"][0]))
            load_rows(1, 8, v8(I["g_post_mix_2"][0]))
            load_rows(1, 16, v8(I["g_pre_ffn_2"][0]))
            load_rows(1, 24, v8(I["g_post_ffn_2"][0]))
            load_rows(1, 32, v8(I["b_sc_2"][0]))
            load_rows(1, 36, I["w_sc_2"][0].rearrange("w (r p) -> (w r) p", p=P))
            load_rows(1, 48, v8(I["b_cf_2"][0]))
            load_rows(1, 70, I["cmp_b1"].rearrange("j (r p) -> (j r) p", p=P))
            load_rows(1, 74, I["g_head_2"])
            load_rows(1, 75, I["cmp_pos"].rearrange("j (r a) d -> (j r) (a d)", a=2))
            wcf = I["w_cf_2"][0].rearrange("a b (r p) -> (a b r) p", p=P)
            load_rows(2, 0, wcf[0:99, :])
            load_rows(3, 0, wcf[99:198, :])
            load_rows(5, 0, v8(I["b_ada_2"][0]))
            act.dma_start(ws[:, :, :], I["a_w_s"][0].rearrange("g t s -> t g s")).then_inc(s_gm, 16)
            act.dma_start(bs_b[:, :, :], I["a_b_s"][0:1].broadcast_to([P, 8, P])).then_inc(s_gm, 16)
            act.dma_start(lng[:, :], I["a_ln_g"][0:1].broadcast_to([P, D])).then_inc(s_gm, 16)
            act.dma_start(lnb[:, :], I["a_ln_b"][0:1].broadcast_to([P, D])).then_inc(s_gm, 16)

            act.wait_ge(s_vec, 1)
            act.activation(csil[:, :], vec[:, 0:24], ACT.Silu).then_inc(s_sg, 1)

            split_next = [0]

            def hi(m, i=0):
                full(act, pl.nm[m], i)
                if m >= SPL:
                    act.wait_ge(s_mm, m - SPL + 1 + 6 * i)
                w = pl.width[m]
                act.activation(whi[:, m % SPL, 0:w], raw[:, pl.nm[m] % RAW, 0:w], ACT.Copy).then_inc(s_hi, 1)

            def splits(upto_m):
                while split_next[0] < min(upto_m, NM):
                    hi(split_next[0])
                    split_next[0] += 1

            def ada_row(b, j):
                a = 8 * b + j
                act.wait_ge(s_ada, a + 1)
                if a >= 4:
                    act.wait_ge(s_col, a - 3)
                act.activation(stage[:, a % 4, :], ps[pl.bank[pl.ua[a]]][:, 0:256], ACT.Copy).then_inc(s_mid, 1)

            def ada_rows(b, j0=0, j1=8):
                for j in range(j0, j1):
                    ada_row(b, j)

            def squares(k, src, wait):
                for b in range(4):
                    wait(b)
                    if k and b == 0:
                        act.wait_ge(s_stat, k)
                    act.activation(sq[:, 2 * b:2 * b + 2, :], src(b), ACT.Square).then_inc(s_sq, 1)

            def guess(k):
                act.wait_ge(s_v, k + 1)
                act.activation(r0[:, :], r0[:, :], ACT.Sqrt, bias=zero_col).then_inc(s_r0, 1)

            def y_gains(c, nx):
                if nx > 1:
                    act.wait_ge(s_x, 4 * nx)
                for kt in range(KT):
                    ins = act.activation(tt_[:, kt, :], ps[kt // 2][:, (kt % 2) * T:(kt % 2) * T + T], ACT.Identity,
                                         scale=coef[:, c, kt:kt + 1], bias=zero_col)
                    if kt % 2:
                        ins.then_inc(s_yfree, 1)

            def shift(o, b, dh=hh, free=0):
                if free:
                    act.wait_ge(s_mm, free)
                for kt in range(KT):
                    act.wait_ge(s_t, 8 * o + kt + 1)
                    act.activation(dh[:, kt, :], tt_[:, kt, :], ACT.Identity, bias=mod[:, b[0], b[1] + kt:b[1] + kt + 1])\
                       .then_inc(s_hh, 1)

            def linear_y_squares(k, ms):
                def wait(b):
                    splits(min(ms[b] + 3, ms[3] + 1))
                    act.wait_ge(s_mm, ms[b] + 1)
                squares(k, from_y, wait)

            zero_col = zero1[:, 0:1]

            def y_done(n, chunks):
                return lambda b: act.wait_ge(s_yb, 3 * n + b + 1) if b < 3 else act.wait_ge(s_mm, chunks)

            act.wait_ge(s_const, 5)
            from_x = lambda b: x[:, 2 * b:2 * b + 2, :]
            from_y = lambda b: ps[b][:, :].rearrange("p (k t) -> p k t", t=T)

            squares(0, from_x, lambda b: act.wait_ge(s_x, b + 1))
            guess(0)
            ada_rows(B0SH)
            splits(3)
            act.wait_ge(s_mod, 1)
            shift(0, (B0SH, 0))
            if has("gmlp"):
                for j in range(4):
                    m = M_V[j]
                    act.wait_ge(s_mm, m + 1)
                    act.activation(v_tm[:, :, 256 * j:256 * j + 256], ps[4 + pl.um[m] % MID][:, :].rearrange("p (t n) -> p t n", t=2),
                                   ACT.Gelu_apprx_tanh).then_inc(s_mid, 1)
                    splits(m + 4)
                for j in range(4):
                    m = M_U[j]
                    act.wait_ge(s_mm, m + 1)
                    act.activation(u_fm[:, 2 * j:2 * j + 2, :], ps[4 + pl.um[m] % MID][:, :].rearrange("p (k t) -> p k t", t=T),
                                   ACT.Gelu_apprx_tanh).then_inc(s_mid, 1)
                    splits(min(m + 4, M_AO[0]))
                ada_rows(B0G)
                act.wait_ge(s_v2, 1)
                act.activation(lr[:, 1, :], lr[:, 1, :], ACT.Sqrt, bias=zero_col).then_inc(s_r2, 1)
                ada_rows(B0SC)
                splits(M_AO[3])
                linear_y_squares(1, M_AO)
                y_gains(G_N1, 1)
                guess(1)
            def boundary(k, nx, o, cols_b, b1=None, free=0):
                if b1 is not None:
                    ada_rows(b1, 0, 5)
                squares(k + 1, from_x, lambda b: act.wait_ge(s_x, 4 * nx + b + 1))
                guess(k + 1)
                if b1 is not None:
                    ada_rows(b1, 5)
                shift(o, cols_b, hh, free)

            def ffn(f):
                m0, c0 = M_FF[f], 16 * f
                u0 = pl.um[m0]

                def epi(c, m, i=0):
                    u = u0 + c
                    act.wait_ge(s_mm, m + 1 + 6 * i)
                    if c0 + c > 0:
                        act.wait_ge(s_fh, c0 + c + 3 * i)
                        act.wait_ge(s_fsq, c0 + c + 3 * i)
                    act.activation(fr[:, :], ps[4 + u % MID][:, :], ACT.Relu).then_inc(s_mid, 1)
                    act.wait_ge(s_mid, pl.um[m0] + c + 1 + 3 * i)
                    if c0 + c > 0:
                        act.wait_ge(s_fact, c0 + c + 3 * i)
                    act.activation(fm[:, :], fr[:, :], ACT.Square).then_inc(s_fsq, 1)

                epi(0, m0)
                splits(m0 + 4)
                with act.Fori(0, 4) as i:
                    for j in range(3):
                        c = 1 + j
                        epi(c, m0 + 2 * c - 1, i)
                        hi(m0 + 2 * c + 2, i)
                        hi(m0 + 2 * c + 3, i)
                split_next[0] = m0 + 28
                for c in range(13, 16):
                    epi(c, m0 + 2 * c - 1)
                    splits(min(m0 + 2 * c + 4, m0 + 32))

            if has("ffn0"):
                boundary(1, 1, 1, (B0G, 8), B1SH, M_AO[3] + 1)
                splits(M_FF[0] + 3)
                ffn(0)
                squares(3, from_y, y_done(0, M_FF[0] + 32))
                y_gains(G_N3, 2)
                guess(3)

            if has("attn"):
                ada_rows(BKV, 0, 5)
                act.dma_start(w2k[:, :, 0:HD], I["cmp_w2"][0].rearrange("(k p) n -> p k n", p=P)).then_inc(s_aw, 16)
                act.dma_start(w2k[:, :, HD:P], I["cmp_w2"][0].rearrange("(k p) n -> p k n", p=P)).then_inc(s_aw, 16)
                act.dma_start(w2v[:, :, :], I["cmp_w2"][1].rearrange("(k p) n -> p k n", p=P)).then_inc(s_aw, 16)
                act.dma_start(b2k[0:HD, :], I["cmp_b2"][0].rearrange("(p a) -> p a", a=1)).then_inc(s_aw, 16)
                act.dma_start(b2k[HD:P, :], I["cmp_b2"][0].rearrange("(p a) -> p a", a=1)).then_inc(s_aw, 16)
                act.dma_start(b2v[:, :], I["cmp_b2"][1:2].broadcast_to([NCP, HD])).then_inc(s_aw, 16)
                squares(4, from_x, lambda b: act.wait_ge(s_x, 8 + b + 1))
                guess(4)
                ada_rows(BKV, 5)
                shift(2, (BKV, 0), gh)
                shift(3, (B1SH, 0), hh, M_FF[0] + 32)
                splits(M_KC + 3)

                def mid_of(m):
                    return ps[4 + pl.um[m] % MID]

                def evac(m, dst, view):
                    act.wait_ge(s_mm, m + 1)
                    act.activation(dst, view(mid_of(m)), ACT.Copy).then_inc(s_mid, 1)

                two = lambda b: b[:, :].rearrange("p (k t) -> p k t", k=2)
                for j, (m, fm_) in enumerate(((M_KC, kc_fm), (M_VC, vc_fm))):
                    evac(m, fm_[:, :, :], two)
                    act.wait_ge(s_mid, pl.um[m] + 1)
                    for half in range(2):
                        for par in range(2):
                            act.dma_start(bsh[j][64 * half:64 * half + 64, par:4:2, 0:T - half],
                                          fm_[64 * par:64 * par + 64, :, half:T]).then_inc(s_bsh[j], 16)
                    splits(m + 4)
                for m, fm_, to in ((M_KS, ks_fm, kc[:, :, NCP:NCP + T]), (M_KW, kw_fm, kw[:, :, :])):
                    evac(m, fm_[:, :, :], two)
                    act.wait_ge(s_mid, pl.um[m] + 1)
                    for half in range(2):
                        for par in range(2):
                            act.dma_start(to[64 * half:64 * half + 64, par:4:2, :], fm_[64 * par:64 * par + 64, :, :])\
                               .then_inc(s_kcp, 16)
                    splits(m + 4)
                evac(M_VS, v_s[:, :, :], two)
                splits(M_VS + 4)
                evac(M_VW, v_w[:, :, :], two)
                splits(M_VW + 4)
                for c in range(4):
                    evac(M_Q[c], qT[:, 2 * c:2 * c + 2, :], two)
                    splits(M_Q[c] + 4)
                act.wait_ge(s_mm, M_GT + 1)
                act.activation(gate[:, :, :], mid_of(M_GT)[:, 0:96].rearrange("p (t n) -> p t n", t=2), ACT.Exp, scale=-1.0)\
                   .then_inc(s_mid, 1)
                splits(M_GT + 4)
                splits(M_CW[1][1] + 1)
                act.wait_ge(s_mm, M_CW[1][1] + 1)
                for j in range(2):
                    for nt in range(2):
                        act.activation(hid[:, j, nt, :], ps[2 * j + nt][:, 0:60], ACT.Gelu_apprx_tanh,
                                       bias=vec[:, C_B1 + 2 * j + nt:C_B1 + 2 * j + nt + 1]).then_inc(s_hid, 1)
                def exps(h):
                    hb = h % 2
                    act.wait_ge(s_nb, h + 1)
                    for qt in range(2):
                        for br in range(3):
                            c = 3 * qt + br
                            p_ = pp[:, hb, part(qt, br)]
                            ins = act.activation(p_, p_, ACT.Exp, bias=nb[:, hb, c:c + 1], scale=HD ** -0.5,
                                                 accum_out=den[:, hb, c:c + 1] if br else None)
                    ins.then_inc(s_exp, 1)

                exps(0)
                exps(1)
                for h in range(NH):
                    act.wait_ge(s_T, h + 1)
                    if h >= 2:
                        act.wait_ge(s_O, h - 1)
                    act.activation(pts[:, h % 2, 0:384], ps[3][:, 0:384], ACT.Copy).then_inc(s_Tev, 1)
                    act.activation(pts[0:NCP, h % 2, 384:512], ps[3][0:NCP, 384:512], ACT.Copy).then_inc(s_Tev, 1)
                    if h % 2 == 0 and h:
                        act.wait_ge(s_O, h)
                        act.activation(h32[:, h // 2 - 1, :], ps[5 + (h // 2 - 1) % 2][:, 0:T], ACT.Copy).then_inc(s_oev, 1)
                    if h + 2 < NH:
                        exps(h + 2)
                    ada_row(B1G + h // 8, h % 8)
                    if h >= 12:
                        splits(M_BO[0] + min(h - 11, 3))
                act.wait_ge(s_O, NH)
                act.activation(h32[:, 7, :], ps[6][:, 0:T], ACT.Copy).then_inc(s_oev, 1)
                linear_y_squares(5, M_BO)
                act.wait_ge(s_mod, B1G + 1)
                y_gains(G_N5, 3)
                guess(5)

            if has("ffn1"):
                boundary(5, 3, 4, (B1G, 8), B2SH, M_BO[3] + 1)
                splits(M_FF[1] + 3)
                if has("gla"):
                    act.dma_start(ctx_tm[:, :, :], I["ctx_2"][0].rearrange("(t p) d -> p t d", p=P)).then_inc(s_ctx, 16)
                ffn(1)
                squares(7, from_y, y_done(1, M_FF[1] + 32))
                y_gains(G_N7, 4)
                guess(7)

            if has("gla"):
                act.wait_ge(s_wz, 1)
                act.dma_start(wab[0:16, 0:256], I["w_af_2"][0]).then_inc(s_wab, 16)
                act.dma_start(wab[16:32, 256:512], I["w_ab_2"][0]).then_inc(s_wab, 16)
                act.dma_start(wab[32:33, 0:256], I["b_af_2"]).then_inc(s_wab, 16)
                act.dma_start(wab[32:33, 256:512], I["b_ab_2"]).then_inc(s_wab, 16)
                ada_rows(B2G, 0, 4)
                squares(8, from_x, lambda b: act.wait_ge(s_x, 16 + b + 1))
                guess(8)
                squares(9, lambda b: cx[:, 2 * b:2 * b + 2, :], lambda b: act.wait_ge(s_cx, b + 1))
                ada_rows(B2G, 4)
                shift(5, (B2SH, 0), hh, M_FF[1] + 32)
                guess(9)
                shift(6, (10, 0), gh)
                splits(M_K2 + 3)
                two = lambda b: b[:, :].rearrange("p (k t) -> p k t", k=2)

                def evac2(m, which, dst, func=ACT.Copy, scale=1.0, view=two):
                    if which == 0:
                        act.wait_ge(s_mm, m + 1)
                    u = pl.um[m] + which
                    act.activation(dst, view(ps[4 + u % MID]), func, scale=scale).then_inc(s_mid, 1)

                evac2(M_K2, 0, qk[:, 2:4, :])
                evac2(M_K2, 1, kctx[:, :, :])
                splits(M_K2 + 4)
                for j in range(2):
                    evac2(M_V2[j], 0, vx[:, :, 256 * j:256 * j + 256])
                    evac2(M_V2[j], 1, vctx[:, :, 256 * j:256 * j + 256])
                    splits(M_V2[j] + 4)
                evac2(M_AL, 0, alx[0:32, :], view=lambda b: b[0:32, 0:T])
                evac2(M_AL, 1, alc[0:32, :], view=lambda b: b[0:32, 0:T])
                splits(M_AL + 4)
                evac2(M_Q2, 0, qk[:, 0:2, :], scale=0.125)
                splits(M_Q2 + 4)
                act.wait_ge(s_gp, 1)
                lt = [wc[:, 0, :], wc[:, 1, :], bx[:, 0:2, :].rearrange("p k t -> p (k t)"),
                      bx[:, 2:4, :].rearrange("p k t -> p (k t)")]
                for b in range(4):
                    ins = act.activation(lt[b], ps[b][:, :], ACT.Abs)
                link(ins)
                for b in range(4):
                    ins = act.activation(lt[b], lt[b], ACT.Exp, scale=-1.0)
                link(ins)
                for b in range(4):
                    act.activation(lt[b], lt[b], ACT.Ln, bias=one1[:, 0:1], scale=1.0).then_inc(s_la, 1)
                for j in range(2):
                    evac2(M_OG[j], 0, og[:, 2 * j:2 * j + 2, :], func=ACT.Silu)
                    splits(M_OG[j] + 4)
                act.wait_ge(s_cum, 1)
                act.wait_ge(s_g, 2)
                for tt in range(2):
                    act.activation(wc[:, tt, :], ps[tt][:, :], ACT.Exp, scale=1.0 / 16).then_inc(s_wc, 1)
                for j in range(2):
                    evac2(M_SC[j], 0, sct[:, 2 * j:2 * j + 2, :])
                    splits(M_SC[j] + 4)
                act.wait_ge(s_st, 1)
                act.activation(st[:, :, :, :], ps[2][:, :].rearrange("p (a b c) -> p a b c", a=2, b=2), ACT.Copy).then_inc(s_ste, 1)
                for j in range(2):
                    evac2(M_SX[j], 0, ct[:, 2 * j:2 * j + 2, :])
                    splits(min(M_SX[j] + 4, M_SB[1] + 1))
                for j in range(2):
                    evac2(M_SB[j], 0, sbt[:, 2 * j:2 * j + 2, :])
                act.wait_ge(s_B, 1)
                act.activation(qi[:, 0:2, :], bx[:, 0:2, :], ACT.Exp, scale=1.0 / 16)
                for j in range(2):
                    ins = act.activation(qi[:, 2 + j, :], bx[:, 2 + j, :], ACT.Exp, bias=tot[:, j:j + 1], scale=-1.0 / 16)
                ins.then_inc(s_qe, 1)
                for l in range(8):
                    act.wait_ge(s_D, l + 1)
                    act.activation(eb[:, l % 2, :, :], eb[:, l % 2, :, :], ACT.Exp, scale=1.0 / 16).then_inc(s_Ex, 1)
                    if l:
                        ada_row(B2SC, l - 1)
                ada_row(B2SC, 7)
                splits(M_WO[0] + 3)
                act.wait_ge(s_o4, 1)
                for b in range(2):
                    ins = act.activation(o2[:, 2 * b:2 * b + 2, :], two(ps[2 + b]), ACT.Square)
                ins.then_inc(s_o2, 1)
                for b in range(2):
                    act.wait_ge(s_v2, 2 + b)
                    act.activation(r4[:, 2 * b:2 * b + 2, :], r4[:, 2 * b:2 * b + 2, :], ACT.Sqrt, bias=zero_col).then_inc(s_r2, 1)
                linear_y_squares(10, M_WO)
                y_gains(G_N10, 5)
                guess(10)

            if has("ffn2"):
                boundary(10, 5, 7, (B2G, 8), None, M_WO[3] + 1)
                splits(M_UP + 2)

                def conv_epi(c, i=0):
                    m = M_UP + (3 * c - 1 if c else 0)
                    act.wait_ge(s_mm, m + 1 + 6 * i)
                    if c:
                        act.wait_ge(s_tap, 8 * c + 16 * i)
                        act.wait_ge(s_sil, c + 2 * i)
                    bank = ps[4 + c % 2]
                    act.activation(ut[:, :, :], bank[:, :].rearrange("p (k t) -> p k t", t=T), ACT.Copy)
                    for k in range(2):
                        b_, w_ = C_BCF + 2 * c + k, C_WCF + 22 * 4 + 2 * c + k
                        ins = act.activation(cvt[:, k, :], bank[:, T * k:T * k + T], ACT.Identity,
                                             bias=vec[:, bass.ds(b_ + 4 * i, 1)], scale=vec[:, bass.ds(w_ + 4 * i, 1)])
                    ins.then_inc(s_ue, 1)
                    hi(M_UP + 3 * c + 2, i)
                    if c < CF - 1:
                        hi(M_UP + 3 * c + 3, i)
                    act.wait_ge(s_tap, 8 * c + 8 + 16 * i)
                    if c:
                        act.wait_ge(s_fa, c + 2 * i)
                    act.activation(sl[:, :, :], cvt[:, :, :], ACT.Silu).then_inc(s_sil, 1)
                    if c < CF - 1:
                        hi(M_UP + 3 * c + 4, i)
                    act.wait_ge(s_fa, c + 1 + 2 * i)
                    act.activation(chi[:, c % 2, :], fa[:, :, :].rearrange("p k t -> p (k t)"), ACT.Copy).then_inc(s_chi, 1)

                conv_epi(0)
                with act.Fori(0, 4) as i:
                    for j in range(2):
                        conv_epi(1 + j, i)
                conv_epi(9)
                conv_epi(10)
                split_next[0] = NM
                squares(12, from_y, y_done(2, M_UP + 33))
                y_gains(G_N12, 6)
                guess(12)

        @block.vector
        def _(dve):
            chain = [0]

            def link(ins):
                ins.then_inc(d_ch, 1)
                chain[0] += 1
                dve.wait_ge(d_ch, chain[0])

            split_next = [0]

            def lo(m, i=0):
                dve.wait_ge(s_hi, m + 1 + 6 * i)
                w = pl.width[m]
                dve.tensor_tensor(wlo[:, m % SPL, 0:w], raw[:, pl.nm[m] % RAW, 0:w], whi[:, m % SPL, 0:w],
                                  ALU.subtract).then_inc(s_lo, 1)

            def splits(upto_m):
                while split_next[0] < min(upto_m, NM):
                    lo(split_next[0])
                    split_next[0] += 1

            def refine(k):
                dve.wait_ge(s_stat, k + 1)
                link(dve.tensor_scalar(vv[:, :], stat, EPS, None, ALU.add))
                dve.reciprocal(r0[:, :], vv[:, :]).then_inc(s_v, 1)
                dve.wait_ge(s_r0, k + 1)
                link(dve.tensor_tensor(n1[:, :], r0[:, :], r0[:, :], ALU.mult))
                link(dve.scalar_tensor_tensor(out=n1[:, :], in0=n1[:, :], scalar=-0.5, in1=vv[:, :], op0=ALU.mult, op1=ALU.mult))
                dve.scalar_tensor_tensor(out=rs[:, :], in0=n1[:, :], scalar=1.5, in1=r0[:, :], op0=ALU.add, op1=ALU.mult)\
                   .then_inc(s_rs, 1)
                dve.wait_ge(s_rs, k + 1)

            def mods(b):
                dve.wait_ge(s_col, 8 * b + 8)
                link(dve.tensor_tensor(mod[:, b, :], sums(b), vec[:, BIAS[b]:BIAS[b] + 16], ALU.add))
                if b == B2SH:
                    link(dve.tensor_tensor(mod[:, 10, :], sums(b, 1), vec[:, BIAS[b]:BIAS[b] + 16], ALU.add))
                for c, kind, m, g in COEFS[b]:
                    if kind == "A":
                        ins = dve.scalar_tensor_tensor(out=coef[:, c, :], in0=m, scalar=1.0, in1=vec[:, g:g + 8],
                                                       op0=ALU.add, op1=ALU.mult)
                    else:
                        ins = dve.tensor_tensor(coef[:, c, :], m, vec[:, g:g + 8], ALU.mult)
                    if c != COEFS[b][-1][0]:
                        link(ins)
                ins.then_inc(s_mod, 1)
                dve.wait_ge(s_mod, b + 1)

            def make_h(o, c, cols_b, dl=hl, dh=hh, src=x):
                def lo_of(kt):
                    dve.wait_ge(s_hh, 8 * o + kt + 1)
                    b, c0 = cols_b
                    dve.scalar_tensor_tensor(out=dl[:, kt, :], in0=tt_[:, kt, :], scalar=mod[:, b, c0 + kt:c0 + kt + 1],
                                             in1=dh[:, kt, :], op0=ALU.add, op1=ALU.subtract).then_inc(s_h, 1)

                if o:
                    dve.wait_ge(s_h, 8 * o)
                for kt in range(KT):
                    dve.scalar_tensor_tensor(out=tt_[:, kt, :], in0=src[:, kt, :], scalar=coef[:, c, kt:kt + 1], in1=rs[:, :],
                                             op0=ALU.mult, op1=ALU.mult).then_inc(s_t, 1)
                    dve.wait_ge(s_t, 8 * o + kt + 1)
                    if kt >= 2:
                        lo_of(kt - 2)
                lo_of(6)
                lo_of(7)

            def update_x(nx):
                rs2 = rs[:, :].rearrange("p (a t) -> p a t", a=1).broadcast_to([P, 2, T])
                for b in range(4):
                    dve.wait_ge(s_yfree, 4 * (nx - 1) + b + 1)
                    q = slice(2 * b, 2 * b + 2)
                    link(dve.tensor_tensor(tt_[:, q, :], tt_[:, q, :], rs2, ALU.mult))
                    dve.tensor_tensor(x[:, q, :], x[:, q, :], tt_[:, q, :], ALU.add).then_inc(s_x, 1)

            for i in range(6):
                dve.wait_ge(s_vT, i + 1)
                dve.tensor_copy(vec[:, V0[i]:V0[i + 1]], ps[7][:, 0:NV[i]] if i % 2 == 0 else ps[6][:, 0:NV[i]])\
                   .then_inc(s_vec, 1)
                if i == 0:
                    for b in range(4):
                        dve.wait_ge(s_xT, b + 1)
                        dve.tensor_copy(x[:, 2 * b:2 * b + 2, :], ps[b][:, :].rearrange("p (k t) -> p k t", t=T)).then_inc(s_x, 1)
                    link(dve.tensor_tensor(sel[:, :], ident[:, 0:2], ident[:, 32:34], ALU.add))
                    link(dve.tensor_tensor(sel[:, :], sel[:, :], ident[:, 64:66], ALU.add))
                    dve.tensor_tensor(sel[:, :], sel[:, :], ident[:, 96:98], ALU.add).then_inc(s_sel, 1)
                    dve.wait_ge(s_cpad0, 1)
                    dve.wait_ge(s_sg, 1)
                    dve.tensor_copy(cpad[:, 0, :, 0], csil[:, 0:8]).then_inc(s_cp, 1)
                    dve.tensor_copy(cpad[:, 1, :, 0], csil[:, 8:16]).then_inc(s_cp, 1)
                    dve.tensor_copy(cpad[:, 1, :, 1], csil[:, 16:24]).then_inc(s_cp, 1)
            dve.wait_ge(s_vec, 6)
            dve.wait_ge(s_x, 4)
            if has("gmlp"):
                for b in range(2):
                    dve.wait_ge(s_wsT, b + 1)
                    dve.tensor_copy(wT[:, 4 * b:4 * b + 4, :], ps[b][:, :].rearrange("p (g t) -> p g t", g=4)).then_inc(s_wTc, 1)
            refine(0)
            splits(3)
            mods(B0SH)
            make_h(0, A_N0, (B0SH, 0))
            if has("gmlp"):
                for j in range(8):
                    splits(min(j + 4, 8))
                    if j == 5:
                        dve.wait_ge(s_mid, pl.um[M_V[3]] + 1)
                        dve.wait_ge(s_gm, 64)
                        for tt in range(2):
                            for f in range(2):
                                link(dve.bn_stats(bst[:, tt, f, :], v_tm[:, tt, 512 * f:512 * f + 512]))
                        link(dve.bn_aggr(mv[:, 0, :], bst[:, 0, :, :]))
                        link(dve.bn_aggr(mv[:, 1, :], bst[:, 1, :, :]))
                        link(dve.tensor_scalar(lr[:, 2, :], mv[:, :, 1], EPS, None, ALU.add))
                        dve.reciprocal(lr[:, 1, :], lr[:, 2, :]).then_inc(s_v2, 1)
                        dve.wait_ge(s_r2, 1)
                link(dve.tensor_tensor(lr[:, 3, :], lr[:, 1, :], lr[:, 1, :], ALU.mult))
                link(dve.scalar_tensor_tensor(out=lr[:, 3, :], in0=lr[:, 3, :], scalar=-0.5, in1=lr[:, 2, :], op0=ALU.mult, op1=ALU.mult))
                link(dve.scalar_tensor_tensor(out=lr[:, 2, :], in0=lr[:, 3, :], scalar=1.5, in1=lr[:, 1, :], op0=ALU.add, op1=ALU.mult))
                for tt in range(2):
                    link(dve.tensor_scalar(v_tm[:, tt, :], v_tm[:, tt, :], mv[:, tt, 0:1], lr[:, 2, tt:tt + 1], ALU.subtract, ALU.mult))
                for tt in range(2):
                    link(dve.tensor_tensor(v_tm[:, tt, :], v_tm[:, tt, :], lng[:, :], ALU.mult))
                    dve.tensor_tensor(v_tm[:, tt, :], v_tm[:, tt, :], lnb[:, :], ALU.add).then_inc(s_vn, 1)
                mods(B0G)
                dve.wait_ge(s_h, 8)
                dve.wait_ge(s_mid, pl.um[M_U[3]] + 1)
                dve.wait_ge(s_mm, M_U[3] + 1)
                for b in range(4):
                    dve.wait_ge(s_mix, b + 1)
                    bias = bs_b[:, 2 * b:2 * b + 2, :].rearrange("p g (a t) -> p g a t", a=1).broadcast_to([P, 2, 2, P])
                    link(dve.tensor_tensor(tt_[:, 2 * b:2 * b + 2, :].rearrange("p g (a t) -> p g a t", a=2),
                                           ps[b][:, :].rearrange("p (g a t) -> p g a t", g=2, a=2), bias, ALU.add))
                    link(dve.tensor_tensor(h32[:, 2 * b:2 * b + 2, :], tt_[:, 2 * b:2 * b + 2, :], u_fm[:, 2 * b:2 * b + 2, :], ALU.mult))
                    link(dve.tensor_copy(hh[:, 2 * b:2 * b + 2, :], h32[:, 2 * b:2 * b + 2, :]))
                    dve.tensor_tensor(hl[:, 2 * b:2 * b + 2, :], h32[:, 2 * b:2 * b + 2, :], hh[:, 2 * b:2 * b + 2, :], ALU.subtract)\
                       .then_inc(s_oa, 1)
                mods(B0SC)
                dve.wait_ge(s_oa, 4)
                splits(M_AO[3] + 1)
                refine(1)
                update_x(1)

            def boundary(k, nx, o, c, cols_b, b1):
                refine(k + 1)
                dve.wait_ge(s_x, 4 * nx + 4)
                make_h(o, c, cols_b)
                if b1 is not None:
                    mods(b1)

            def ffn(f):
                m0, c0 = M_FF[f], 16 * f
                mid0 = pl.um[m0]

                def epi(c, i=0, first=False):
                    dve.wait_ge(s_mid, mid0 + c + 1 + 3 * i)
                    if c >= 3:
                        dve.wait_ge(s_mm, m0 + 2 * (c - 3) + 3 + 6 * i)
                    dve.tensor_tensor(fhi[:, c % 3, :], fr[:, :], fr[:, :], ALU.mult).then_inc(s_fh, 1)
                    dve.wait_ge(s_fh, c0 + c + 1 + 3 * i)
                    dve.wait_ge(s_fsq, c0 + c + 1 + 3 * i)
                    dve.tensor_tensor(flo[:, c % 3, :], fm[:, :], fhi[:, c % 3, :], ALU.subtract).then_inc(s_fact, 1)

                epi(0)
                splits(m0 + 4)
                for c in range(1, 4):
                    epi(c)
                    splits(m0 + 2 * c + 4)
                with dve.Fori(0, 3) as i:
                    for j in range(3):
                        c = 4 + j
                        epi(c, i)
                        lo(m0 + 2 * c + 2, i)
                        lo(m0 + 2 * c + 3, i)
                split_next[0] = m0 + 28
                for c in range(13, 16):
                    epi(c)
                    splits(min(m0 + 2 * c + 4, m0 + 32))

            if has("ffn0"):
                boundary(1, 1, 1, A_N2, (B0G, 8), B1SH)
                splits(M_FF[0] + 3)
                ffn(0)
                refine(3)
                update_x(2)

            if has("attn"):
                refine(4)
                dve.wait_ge(s_x, 12)
                mods(BKV)
                make_h(2, A_KV, (BKV, 0), gl, gh)
                make_h(3, A_N4, (B1SH, 0))
                splits(M_VW + 1)

                def compress(j):
                    dve.wait_ge(s_bsh[j], 64)
                    if j:
                        dve.wait_ge(s_mm, M_CW[0][1] + 1)
                    for half in range(2):
                        src = bsh[j][:, :, 16 * half:16 * half + 240].rearrange("p g (c i two) -> p i g c two", c=NC, two=2)[:, :, :, :, 0]
                        pos = vec[:, C_POS + 16 * j + 8 * half:C_POS + 16 * j + 8 * half + 8]
                        pos = pos.rearrange("p (i a b) -> p i a b", a=1, b=1).broadcast_to([P, 8, NG, NC])
                        link(dve.tensor_tensor(blk[:, 8 * half:8 * half + 8, :, :], src, pos, ALU.add))
                    b60 = blk[:, :, :, :].rearrange("p i g c -> p i (g c)")
                    link(dve.tensor_copy(bhi[:, :, :], b60))
                    dve.tensor_tensor(blo[:, :, :], b60, bhi[:, :, :], ALU.subtract).then_inc(s_blk, 1)
                    dve.wait_ge(s_blk, j + 1)

                splits(M_Q[1] + 1)
                compress(0)
                splits(M_CW[0][1] + 1)
                dve.wait_ge(s_mid, pl.um[M_GT] + 1)
                link(dve.tensor_scalar(gate[:, :, :], gate[:, :, :], 1.0, None, ALU.add))
                dve.reciprocal(gate[:, :, :], gate[:, :, :]).then_inc(s_gt, 1)
                splits(M_CW[1][0] + 1)
                compress(1)
                splits(M_CW[1][1] + 1)
                dve.wait_ge(s_gt, 1)
                dve.wait_ge(s_aw, 96)
                dve.wait_ge(s_w2, 1)
                link(dve.memset(kc[:, :, NC:NCP], 0.0))
                dve.tensor_scalar(kc[:, :, 0:NC], ps[0][:, 0:60].rearrange("p (g c) -> p g c", g=NG), b2k[:, 0:1], None, ALU.add)\
                   .then_inc(s_kv, 1)
                bias = b2v[0:NC, :].rearrange("p (a n) -> p a n", a=1).broadcast_to([NC, NG, HD])
                dve.tensor_tensor(vcs[0:NC, :, :], ps[1][0:NC, 0:256].rearrange("p (g n) -> p g n", g=NG), bias, ALU.add)\
                   .then_inc(s_kv, 1)
                dve.wait_ge(s_kv, 2)
                dve.wait_ge(s_asm, 3)

                def scores_out(h):
                    hb = h % 2
                    dve.wait_ge(s_S, h + 1)
                    if h >= 2:
                        dve.wait_ge(s_T, h - 1)
                    for qt in range(2):
                        for br in range(3):
                            mask = cmm[:, qt, :] if br == 0 else cmask[:, P * (1 - qt):T]
                            c = 3 * qt + br
                            ins = dve.tensor_tensor_reduce(pp[:, hb, part(qt, br)], score_psum(qt, br), mask, 1.0, -3e38,
                                                           ALU.add, ALU.max, mx[:, hb, c:c + 1])
                    ins.then_inc(s_Sev, 1)
                    dve.wait_ge(s_Sev, h + 1)
                    dve.tensor_scalar(nb[:, hb, :], mx[:, hb, :], -HD ** -0.5, None, ALU.mult).then_inc(s_nb, 1)

                def gated(h):
                    hb = h % 2
                    dve.wait_ge(s_exp, h + 1)
                    for qt in range(2):
                        p_ = pp[:, hb, part(qt, 0)]
                        link(dve.tensor_tensor_reduce(p_, p_, cm01[:, qt, :], 1.0, 0.0, ALU.mult, ALU.add,
                                                      den[:, hb, 3 * qt:3 * qt + 1]))
                    link(dve.tensor_scalar(rec[:, hb, :], den[:, hb, :], 1e-30, None, ALU.max))
                    link(dve.reciprocal(rec[:, hb, :], rec[:, hb, :]))
                    link(dve.tensor_tensor(cf[:, hb, :].rearrange("p (t b) -> p t b", t=2),
                                           rec[:, hb, :].rearrange("p (t b) -> p t b", t=2), gate[:, :, 3 * h:3 * h + 3], ALU.mult))
                    for qt in range(2):
                        for br in range(3):
                            c = 3 * qt + br
                            p_ = pp[:, hb, part(qt, br)]
                            ins = dve.tensor_scalar(p_, p_, cf[:, hb, c:c + 1], None, ALU.mult)
                    ins.then_inc(s_p, 1)
                    dve.wait_ge(s_p, h + 1)

                scores_out(0)
                scores_out(1)
                gated(0)
                for h in range(NH):
                    if h + 1 < NH:
                        gated(h + 1)
                    dve.wait_ge(s_T, h + 1)
                    if h >= 2:
                        dve.wait_ge(s_O, h - 1)
                    dve.tensor_copy(pts[:, h % 2, 512:896], ps[4][:, 0:384]).then_inc(s_TevD, 1)
                    dve.tensor_copy(pts[0:NCP, h % 2, 896:1024], ps[4][0:NCP, 384:512]).then_inc(s_TevD, 1)
                    if h % 2 == 0 and h:
                        k = h // 2 - 1
                        dve.wait_ge(s_oev, k + 1)
                        link(dve.tensor_copy(hh[:, k, :], h32[:, k, :]))
                        dve.tensor_tensor(hl[:, k, :], h32[:, k, :], hh[:, k, :], ALU.subtract).then_inc(s_oh, 1)
                    if h + 2 < NH:
                        scores_out(h + 2)
                    if h >= 12:
                        splits(M_BO[0] + min(h - 11, 3))
                dve.wait_ge(s_oev, 8)
                link(dve.tensor_copy(hh[:, 7, :], h32[:, 7, :]))
                dve.tensor_tensor(hl[:, 7, :], h32[:, 7, :], hh[:, 7, :], ALU.subtract).then_inc(s_oh, 1)
                dve.wait_ge(s_oh, 8)
                dve.wait_ge(s_col, 8 * B1SC + 8)
                mods(B1G)
                mods(B1SC)
                splits(M_BO[3] + 1)
                refine(5)
                update_x(3)

            if has("ffn1"):
                boundary(5, 3, 4, A_N6, (B1G, 8), B2SH)
                splits(M_FF[1] + 3)
                ffn(1)
                refine(7)
                update_x(4)

            if has("gla"):
                for b in range(4):
                    dve.wait_ge(s_cT, b + 1)
                    dve.tensor_copy(cx[:, 2 * b:2 * b + 2, :], ps[b][:, :].rearrange("p (k t) -> p k t", t=T)).then_inc(s_cx, 1)
                refine(8)
                dve.wait_ge(s_x, 20)
                make_h(5, A_N8, (B2SH, 0))
                dve.wait_ge(s_cx, 4)
                refine(9)
                make_h(6, A_N9, (10, 0), gl, gh, cx)
                mods(B2G)
                splits(M_Q2 + 4)
                lt = [wc[:, 0, :], wc[:, 1, :], bx[:, 0:2, :].rearrange("p k t -> p (k t)"),
                      bx[:, 2:4, :].rearrange("p k t -> p (k t)")]
                gt = [gc[:, 0, :], gc[:, 1, :], gx[:, 0:2, :].rearrange("p k t -> p (k t)"),
                      gx[:, 2:4, :].rearrange("p k t -> p (k t)")]
                for b in range(4):
                    dve.wait_ge(s_la, b + 1)
                    dve.scalar_tensor_tensor(out=gt[b], in0=ps[b][:, :], scalar=0.0, in1=lt[b], op0=ALU.min, op1=ALU.subtract)                       .then_inc(s_g, 1)
                splits(M_OG[0] + 4)
                dve.wait_ge(s_g, 4)
                link(dve.memset(bx[:, 2:4, 0:1], 0.0))
                for j in range(4):
                    n = T if j < 2 else T - 1
                    ins = dve.tensor_tensor_scan(bx[:, j, T - n:T], one1[:, 0:n], gx[:, j, 0:n], 0.0, ALU.mult, ALU.add)
                link(ins)
                link(dve.tensor_tensor(tot[:, :], bx[:, 2:4, T - 1], gx[:, 2:4, T - 1], ALU.add))
                dve.tensor_scalar(tot[:, :], tot[:, :], 1.0 / 16, None, ALU.mult).then_inc(s_B, 1)
                splits(M_OG[1] + 4)
                for tt in range(2):
                    dve.wait_ge(s_wc, tt + 1)
                    w_ = wc[:, tt, :].rearrange("p (f n) -> p f n", f=2)
                    ins = dve.tensor_tensor(w_, w_, kctx[:, tt:tt + 1, :].broadcast_to([P, 2, T]), ALU.mult)
                ins.then_inc(s_kd, 1)
                for j in range(2):
                    splits(M_SC[j] + 4)
                splits(M_SB[1] + 1)
                for j in range(2):
                    dve.wait_ge(s_mid, pl.um[M_SX[j]] + 1)
                    ins = dve.tensor_tensor(ct[:, 2 * j:2 * j + 2, :], ct[:, 2 * j:2 * j + 2, :], sct[:, 2 * j:2 * j + 2, :], ALU.mult)
                link(ins)
                row = lambda a, k: a[:, k, :].rearrange("p (r w) -> p r w", w=64)
                tap = lambda w, k: vec[:, C_WSC + 4 * w + k:C_WSC + 4 * w + k + 1]
                for k in range(4):
                    ins = dve.tensor_scalar(sct[:, k, :], ct[:, k, :], tap(1, k), vec[:, C_BSC + k:C_BSC + k + 1], ALU.mult, ALU.add)
                link(ins)
                for w, to, frm in ((0, slice(1, 64), slice(0, 63)), (2, slice(0, 63), slice(1, 64))):
                    for k in range(4):
                        ins = dve.scalar_tensor_tensor(out=row(sct, k)[:, :, to], in0=row(ct, k)[:, :, frm], scalar=tap(w, k),
                                                       in1=row(sct, k)[:, :, to], op0=ALU.mult, op1=ALU.add)
                    link(ins)
                dve.wait_ge(s_mid, pl.um[M_SB[1]] + 1)
                link(dve.tensor_tensor(sct[:, :, :], sct[:, :, :], sbt[:, :, :], ALU.mult))
                dve.wait_ge(s_mm, M_SB[1] + 1)
                link(dve.tensor_copy(hh[:, 4:8, :], sct[:, :, :]))
                dve.tensor_tensor(hl[:, 4:8, :], sct[:, :, :], hh[:, 4:8, :], ALU.subtract).then_inc(s_cv, 1)
                dve.wait_ge(s_qe, 1)
                q_ = qk[:, 0:2, :].rearrange("p (a k) t -> p a k t", a=1).broadcast_to([P, 2, 2, T])
                qi_ = qi[:, :, :].rearrange("p (a k) t -> p a k t", a=2)
                dve.tensor_tensor(qi_, qi_, q_, ALU.mult).then_inc(s_qi, 1)

                def operands(l):
                    dve.wait_ge(s_Ex, l + 1)
                    dve.tensor_tensor(eb[:, l % 2, :, :], eb[:, l % 2, :, :], qk[:, :, :], ALU.mult).then_inc(s_E, 1)

                def fill(n):
                    dve.wait_ge(s_lev, n + 1)
                    for par in range(2):
                        src = ps[2 * (n % 2) + par][:, :].rearrange("p (c i) -> p c i", i=P)
                        dst = (a_x if n == 1 else a_d)[:, par, :, :, :].rearrange("p t g i -> p (t g) i")
                        if n < 2:
                            ins = dve.tensor_copy(dst, src)
                        else:
                            mask = lmask[:, n - 2:n - 1, :].broadcast_to([P, 4, P])
                            ins = dve.copy_predicated(dst, mask, src)
                    ins.then_inc(s_A, 1)
                    dve.wait_ge(s_A, n + 1)

                dve.wait_ge(s_gm3, 9)
                fill(0)
                operands(0)
                for l in range(8):
                    if l < 7:
                        operands(l + 1)
                    fill(l + 1)
                mods(B2SC)
                splits(M_WO[0] + 3)
                dve.wait_ge(s_ms4, 1)
                for b in range(2):
                    q = slice(2 * b, 2 * b + 2)
                    link(dve.tensor_scalar(v4[:, q, :], ps[b][:, :].rearrange("p (k t) -> p k t", k=2), D / P, EPS, ALU.mult, ALU.add))
                    dve.reciprocal(r4[:, q, :], v4[:, q, :]).then_inc(s_v2, 1)
                dve.wait_ge(s_r2, 3)
                link(dve.tensor_tensor(n4[:, :, :], r4[:, :, :], r4[:, :, :], ALU.mult))
                link(dve.scalar_tensor_tensor(out=n4[:, :, :], in0=n4[:, :, :], scalar=-0.5, in1=v4[:, :, :], op0=ALU.mult, op1=ALU.mult))
                link(dve.scalar_tensor_tensor(out=r4[:, :, :], in0=n4[:, :, :], scalar=1.5, in1=r4[:, :, :], op0=ALU.add, op1=ALU.mult))
                for b in range(2):
                    ins = dve.scalar_tensor_tensor(out=o4[:, b:4:2, :], in0=ps[2 + b][:, :].rearrange("p (k t) -> p k t", k=2),
                                                   scalar=vec[:, C_GH:C_GH + 1], in1=r4[:, 2 * b:2 * b + 2, :], op0=ALU.mult, op1=ALU.mult)
                link(ins)
                link(dve.tensor_tensor(o4[:, :, :], o4[:, :, :], og[:, :, :], ALU.mult))
                link(dve.tensor_copy(hh[:, 0:4, :], o4[:, :, :]))
                dve.tensor_tensor(hl[:, 0:4, :], o4[:, :, :], hh[:, 0:4, :], ALU.subtract).then_inc(s_gs, 1)
                splits(M_WO[3] + 1)
                refine(10)
                dve.wait_ge(s_gs, 1)
                update_x(5)

            if has("ffn2"):
                boundary(10, 5, 7, A_N11, (B2G, 8), None)
                splits(M_UP + 2)
                TAPS = [(dr, dc) for dr in (-1, 0, 1) for dc in (-1, 0, 1) if (dr, dc) != (0, 0)]
                HROW, WROW = T // 64, 64

                def conv_epi(c, i=0):
                    dve.wait_ge(s_ue, c + 1 + 2 * i)
                    for n, (dr, dc) in enumerate(TAPS):
                        to = (slice(max(0, -dr), HROW - max(0, dr)), slice(max(0, -dc), WROW - max(0, dc)))
                        frm = (slice(max(0, dr), HROW - max(0, -dr)), slice(max(0, dc), WROW - max(0, -dc)))
                        for k in range(2):
                            grid = lambda a: a[:, k, :].rearrange("p (r w) -> p r w", w=WROW)
                            w_ = C_WCF + 22 * (3 * (dr + 1) + dc + 1) + 2 * c + k
                            y = grid(cvt)[:, to[0], to[1]]
                            ins = dve.scalar_tensor_tensor(out=y, in0=grid(ut)[:, frm[0], frm[1]],
                                                           scalar=vec[:, bass.ds(w_ + 4 * i, 1)], in1=y,
                                                           op0=ALU.mult, op1=ALU.add)
                        ins.then_inc(s_tap, 1)
                        dve.wait_ge(s_tap, 8 * c + n + 1 + 16 * i)
                        if n == 3:
                            lo(M_UP + 3 * c + 2, i)
                    if c < CF - 1:
                        lo(M_UP + 3 * c + 3, i)
                    dve.wait_ge(s_mm, M_UP + (3 * c if c else 1) + 1 + 6 * i)
                    dve.wait_ge(s_sil, c + 1 + 2 * i)
                    if c:
                        dve.wait_ge(s_cact, c + 2 * i)
                    dve.tensor_tensor(fa[:, :, :], sl[:, :, :], ps[6 + c % 2][:, :].rearrange("p (k t) -> p k t", t=T), ALU.mult)                       .then_inc(s_fa, 1)
                    if c < CF - 1:
                        lo(M_UP + 3 * c + 4, i)
                    dve.wait_ge(s_fa, c + 1 + 2 * i)
                    dve.wait_ge(s_chi, c + 1 + 2 * i)
                    dve.tensor_tensor(clo[:, c % 2, :], fa[:, :, :].rearrange("p k t -> p (k t)"), chi[:, c % 2, :], ALU.subtract)                       .then_inc(s_cact, 1)

                conv_epi(0)
                with dve.Fori(0, 4) as i:
                    for j in range(2):
                        conv_epi(1 + j, i)
                conv_epi(9)
                conv_epi(10)
                split_next[0] = NM
                refine(12)
                update_x(6)

            dve.wait_ge(s_x, 4 * N_UPD + 4)
            dve.wait_ge(s_yfree, 4 * N_UPD)
            for b in range(4):
                dve.wait_ge(s_oT, b + 1)
                dve.tensor_copy(y_tm[:, b // 2, 512 * (b % 2):512 * (b % 2) + 512], ps[b][:, :]).then_inc(s_oc, 1)

        @block.tensor
        def _(pe):
            def ada_chunk(a):
                c, u = (0 if a < 8 * B2SH else 1), pl.ua[a]
                full(pe, pl.na[a])
                if pl.before(u):
                    pe.wait_ge(s_mid, pl.before(u))
                w = raw[:, pl.na[a] % RAW, :].rearrange("p (k n) -> p k n", n=256)
                for kt in range(KT):
                    g = kt % 4
                    mm = pe.matmul(ps[pl.bank[u]][32 * g:32 * g + 32, 0:256], cpad[:, c, kt, :], w[:, kt, :],
                                   start=kt < 4, stop=kt >= 4)
                mm.then_inc(s_ada, 1)

            def ada_col(a):
                b = a // 8
                if a % 8 == 0:
                    if pl.ua[a]:
                        pe.wait_ge(s_mid, pl.ua[a])
                    if b and b != B1SC:
                        pe.wait_ge(s_mod, b)
                pe.wait_ge(s_mid, pl.ua[a] + 1)
                bank, at_ = SUMS[b]
                for j in range(2):
                    c = at_ + 4 * (a % 8) + 2 * j
                    mm = pe.matmul(ps[bank][:, c:c + 2], stage[:, a % 4, P * j:P * j + P], sel[:, :], start=True, stop=True)
                mm.then_inc(s_col, 1)

            def ada_part(b, j0=0, j1=8):
                for a in range(8 * b + j0, 8 * b + j1):
                    ada_chunk(a)
                    if a > 8 * b + j0:
                        ada_col(a - 1)
                ada_col(8 * b + j1 - 1)

            def mean_square(k):
                if k:
                    pe.wait_ge(s_rs, k)
                for kt in range(KT):
                    if kt % 2 == 0:
                        pe.wait_ge(s_sq, 4 * k + kt // 2 + 1)
                    mm = pe.matmul(stat, onesm[:, :], sq[:, kt, :], start=kt == 0, stop=kt == KT - 1)
                mm.then_inc(s_stat, 1)

            def w_of(m, kts=KT):
                w = pl.width[m] // kts
                v = slice(0, pl.width[m])
                return (whi[:, m % SPL, v].rearrange("p (k n) -> p k n", n=w),
                        wlo[:, m % SPL, v].rearrange("p (k n) -> p k n", n=w))

            def feature_major(m, dst, ah, al, i=0, kts=KT, o=None):
                wh, wl = w_of(m, kts)
                for nt in range(wh.shape[2] // P):
                    for kt in range(kts):
                        if o is not None and nt == 0:
                            pe.wait_ge(s_h, 8 * o + kt + 1)
                        n = slice(nt * P, nt * P + P)
                        pe.matmul(dst(nt), wh[:, kt, n], ah[:, kt, :], start=kt == 0, stop=False)
                        pe.matmul(dst(nt), wh[:, kt, n], al[:, kt, :], start=False, stop=False)
                        mm = pe.matmul(dst(nt), wl[:, kt, n], ah[:, kt, :], start=False, stop=kt == kts - 1)
                return mm

            def token_major(m, dst, ah, al, o=None):
                wh, wl = w_of(m)
                for tt in range(2):
                    for kt in range(KT):
                        if o is not None and tt == 0:
                            pe.wait_ge(s_h, 8 * o + kt + 1)
                        t = slice(tt * P, tt * P + P)
                        pe.matmul(dst(tt), ah[:, kt, t], wh[:, kt, :], start=kt == 0, stop=False)
                        pe.matmul(dst(tt), ah[:, kt, t], wl[:, kt, :], start=False, stop=False)
                        mm = pe.matmul(dst(tt), al[:, kt, t], wh[:, kt, :], start=False, stop=kt == KT - 1)
                return mm

            def split_ready(m, i=0):
                pe.wait_ge(s_lo, m + 1 + 6 * i)

            def mid_free(u):
                if pl.before(u):
                    pe.wait_ge(s_mid, pl.before(u))

            def linear_mid(m, ah, al, tm=False, i=0, o=None):
                u = pl.um[m]
                split_ready(m, i)
                mid_free(u)
                w = pl.width[m] // KT
                if tm:
                    mm = token_major(m, lambda tt: ps[4 + u % MID][:, w * tt:w * tt + w], ah, al, o)
                else:
                    mm = feature_major(m, lambda nt: ps[4 + u % MID][:, T * nt:T * nt + T], ah, al, o=o)
                mm.then_inc(s_mm, 1)

            def linear_y(m, j, ah, al):
                split_ready(m)
                feature_major(m, lambda nt: ps[j][:, T * nt:T * nt + T], ah, al).then_inc(s_mm, 1)

            def open_y():
                for b in range(4):
                    pe.matmul(ps[b][:, :], zb[:, 0:P], zb[:, :], start=True, stop=True)

            def rows_onto_y(m, ah, al, last=False):
                wh, wl = w_of(m, 2)
                for nt in range(KT):
                    for k in range(2):
                        t = slice(T * k, T * k + T)
                        y = ps[nt // 2][:, T * (nt % 2):T * (nt % 2) + T]
                        n = slice(nt * P, nt * P + P)
                        pe.matmul(y, wh[:, k, n], ah[:, t], start=False, stop=False, skip_group_check=True)
                        pe.matmul(y, wh[:, k, n], al[:, t], start=False, stop=False, skip_group_check=True)
                        mm = pe.matmul(y, wl[:, k, n], ah[:, t], start=False, stop=False, skip_group_check=True)
                    if last and nt in (1, 3, 5):
                        mm.then_inc(s_yb, 1)
                return mm

            def ffn(f, o):
                m0, c0 = M_FF[f], 16 * f
                u0 = pl.um[m0]

                def ff_in(c, m, i=0, o=None):
                    split_ready(m, i)
                    if c == 0:
                        mid_free(u0)
                    else:
                        pe.wait_ge(s_mid, u0 + c - MID + 1 + 3 * i)
                    bank = ps[4 + (u0 + c) % MID]
                    feature_major(m, lambda nt: bank[:, T * nt:T * nt + T], hh, hl, o=o).then_inc(s_mm, 1)

                def ff_out(c, m, i=0):
                    split_ready(m, i)
                    pe.wait_ge(s_fact, c0 + c + 1 + 3 * i)
                    rows_onto_y(m, fhi[:, c % 3, :], flo[:, c % 3, :], last=c == 15).then_inc(s_mm, 1)

                ff_in(0, m0, o=o)
                pe.wait_ge(s_mod, (B1SH if f == 0 else B2SH) + 1)
                pe.wait_ge(s_mid, u0)
                open_y()
                with pe.Fori(0, 5) as i:
                    for j in range(3):
                        ff_in(j + 1, m0 + 1 + 2 * j, i)
                        ff_out(j, m0 + 2 + 2 * j, i)
                ff_out(15, m0 + 31)

            def boundary(k, b1):
                mean_square(k)
                if b1 is not None:
                    ada_part(b1, 0, 5)
                mean_square(k + 1)
                if b1 is not None:
                    ada_part(b1, 5)

            pe.wait_ge(s_const, 5)
            pe.wait_ge(s_vrow, 16 * 20)
            for i in range(6):
                if i >= 2:
                    pe.wait_ge(s_vec, i - 1)
                dst = ps[7] if i % 2 == 0 else ps[6]
                pe.transpose(dst[:, 0:NV[i]], vrow[0:NV[i], i, :], ident[0:NV[i], 0:NV[i]]).then_inc(s_vT, 1)
                if i == 0:
                    pe.wait_ge(s_x0, 16)
                    for b in range(4):
                        for q in range(4):
                            kt, tt = 2 * b + q // 2, q % 2
                            mm = pe.transpose(ps[b][:, q * P:q * P + P], x_tm[:, tt, kt * P:kt * P + P], ident[:, :])
                        mm.then_inc(s_xT, 1)
            if has("gmlp"):
                pe.wait_ge(s_gm, 64)
                pe.wait_ge(s_x, 4)
                for b in range(2):
                    for q in range(4):
                        mm = pe.transpose(ps[b][:, q * P:q * P + P], ws[:, 4 * b + q, :], ident[:, :])
                    mm.then_inc(s_wsT, 1)
            pe.wait_ge(s_vec, 6)
            mean_square(0)
            pe.wait_ge(s_cp, 3)
            pe.wait_ge(s_sel, 1)
            ada_part(B0SH)
            if has("gmlp"):
                for j in range(4):
                    linear_mid(M_V[j], hh, hl, tm=True, o=0 if j == 0 else None)
                for j in range(4):
                    linear_mid(M_U[j], hh, hl)
                ada_part(B0G)
                pe.wait_ge(s_wT, 1)
                pe.wait_ge(s_vn, 2)
                pe.wait_ge(s_wTc, 2)
                for b in range(4):
                    for g in (2 * b, 2 * b + 1):
                        for tt in range(2):
                            c0 = (g % 2) * T + tt * P
                            mm = pe.matmul(ps[b][:, c0:c0 + P], v_tm[:, tt, g * P:g * P + P], wT[:, g, :], start=True, stop=True)
                    mm.then_inc(s_mix, 1)
                ada_part(B0SC)
                pe.wait_ge(s_oa, 4)
                for j in range(4):
                    linear_y(M_AO[j], j, hh, hl)
                if has("ffn0"):
                    boundary(1, B1SH)
                else:
                    mean_square(1)
            if has("ffn0"):
                pe.wait_ge(s_yfree, 4)
                ffn(0, 1)
                mean_square(3)

            if has("attn"):
                ada_part(BKV, 0, 5)
                mean_square(4)
                ada_part(BKV, 5)
                for m in (M_KC, M_VC, M_KS, M_KW):
                    linear_mid(m, gh, gl, o=2 if m == M_KC else None)
                for m in (M_VS, M_VW):
                    linear_mid(m, gh, gl, tm=True)
                for j in range(4):
                    linear_mid(M_Q[j], hh, hl, o=3 if j == 0 else None)
                linear_mid(M_GT, hh, hl, tm=True)
                for j in range(2):
                    pe.wait_ge(s_blk, j + 1)
                    for c in range(2):
                        m = M_CW[j][c]
                        split_ready(m)
                        wh, wl = w_of(m)
                        for nt in range(2):
                            n = slice(P * nt, P * nt + P)
                            dst = ps[2 * j + nt][:, 0:60]
                            for i in range(8):
                                ah, al = bhi[:, 8 * c + i, :], blo[:, 8 * c + i, :]
                                pe.matmul(dst, wh[:, i, n], ah, start=c == 0 and i == 0, stop=False)
                                pe.matmul(dst, wh[:, i, n], al, start=False, stop=False)
                                mm = pe.matmul(dst, wl[:, i, n], ah, start=False, stop=c == 1 and i == 7)
                        mm.then_inc(s_mm, 1)
                pe.wait_ge(s_hid, 4)
                pe.wait_ge(s_aw, 96)
                for nt in range(2):
                    pe.matmul(ps[0][:, 0:60], w2k[:, nt, :], hid[:, 0, nt, :], start=nt == 0, stop=nt == 1)
                for g in range(NG):
                    for nt in range(2):
                        mm = pe.matmul(ps[1][0:NC, HD * g:HD * g + HD], hid[:, 1, nt, NC * g:NC * g + NC], w2v[:, nt, :],
                                       start=nt == 0, stop=nt == 1)
                mm.then_inc(s_w2, 1)
                pe.wait_ge(s_kv, 2)
                pe.wait_ge(s_kcp, 128)
                pe.wait_ge(s_mid, pl.ua[8 * B1G])

                def scores(h):
                    if h:
                        pe.wait_ge(s_Sev, h)
                    b, g = slice(64 * (h % 2), 64 * (h % 2) + 64), h // 4
                    for qt in range(2):
                        q = qT[b, h // 2, P * qt:P * qt + P]
                        nk = P * (qt + 1)
                        pe.matmul(ps[qt][:, 0:NCP + nk], q, kc[b, g, 0:NCP + nk], start=True, stop=True)
                        mm = pe.matmul(score_psum(qt, 2), q, kw[b, g, 0:nk], start=True, stop=True)
                    mm.then_inc(s_S, 1)

                def turn(h):
                    hb = h % 2
                    pe.wait_ge(s_p, h + 1)
                    if h:
                        pe.wait_ge(s_Tev, 2 * h)
                        pe.wait_ge(s_TevD, 2 * h)
                    for br in (1, 2):
                        bank = ps[2 + br]
                        for qt in range(2):
                            at_ = part(qt, br).start
                            for kt in range(qt + 1):
                                pe.transpose(bank[:, (kt * T + (qt - kt) * P):(kt * T + (qt - kt) * P) + P],
                                             pp[:, hb, at_ + P * kt:at_ + P * kt + P], ident[:, :])
                        mm = pe.transpose(bank[0:NCP, 384:512], pp[:, hb, part(br - 1, 0)], ident[:, :])
                    mm.then_inc(s_T, 1)

                def values(h):
                    hb, g = h % 2, h // 4
                    if h % 2 == 0 and h >= 4:
                        pe.wait_ge(s_oev, h // 2 - 1)
                    pe.wait_ge(s_Tev, 2 * h + 2)
                    pe.wait_ge(s_TevD, 2 * h + 2)
                    o = ps[5 + (h // 2) % 2][64 * (h % 2):64 * (h % 2) + 64, :]
                    n = slice(HD * g, HD * g + HD)
                    pe.matmul(o[:, 0:T], v_s[:, 0, n], pts[:, hb, 0:T], start=True, stop=False)
                    pe.matmul(o[:, P:T], v_s[:, 1, n], pts[:, hb, T:T + P], start=False, stop=False)
                    pe.matmul(o[:, P:T], v_w[:, 1, n], pts[:, hb, 512 + T:512 + T + P], start=False, stop=False)
                    for qt in range(2):
                        pe.matmul(o[:, P * qt:P * qt + P], vcs[0:NC, g, :], pts[0:NC, hb, 512 * qt + 384:512 * qt + 512],
                                  start=False, stop=False)
                    pe.matmul(o[:, 0:T], v_w[:, 0, n], pts[:, hb, 512:512 + T], start=False, stop=True).then_inc(s_O, 1)

                pe.wait_ge(s_rs, 5)
                scores(0)
                scores(1)
                for h in range(NH):
                    turn(h)
                    if h + 2 < NH:
                        scores(h + 2)
                    ada_chunk(8 * B1G + h)
                    values(h)
                    ada_col(8 * B1G + h)
                pe.wait_ge(s_oh, 8)
                pe.wait_ge(s_mod, B1SC + 1)
                for j in range(4):
                    linear_y(M_BO[j], j, hh, hl)
                if not has("ffn1"):
                    mean_square(5)

            if has("ffn1"):
                boundary(5, B2SH)
                pe.wait_ge(s_yfree, 12)
                ffn(1, 4)
                mean_square(7)

            if has("gla"):
                ada_part(B2G, 0, 2)
                pe.wait_ge(s_ctx, 16)
                for b in range(4):
                    pe.wait_ge(s_yfree, 16 - 3 + b)
                    for q in range(4):
                        kt, tt = 2 * b + q // 2, q % 2
                        mm = pe.transpose(ps[b][:, q * P:q * P + P], ctx_tm[:, tt, kt * P:kt * P + P], ident[:, :])
                    mm.then_inc(s_cT, 1)
                ada_part(B2G, 2, 4)
                mean_square(8)
                mean_square(9)
                ada_part(B2G, 4)

                def linear_two(m, tm):
                    split_ready(m)
                    w = pl.width[m] // KT
                    for i, (ah, al_, t_) in enumerate(((hh, hl, tm[0]), (gh, gl, tm[1]))):
                        u = pl.um[m] + i
                        o = 5 + i if m == M_K2 else None
                        mid_free(u)
                        if t_:
                            mm = token_major(m, lambda tt: ps[4 + u % MID][:, w * tt:w * tt + w], ah, al_, o)
                        else:
                            mm = feature_major(m, lambda nt: ps[4 + u % MID][:, T * nt:T * nt + T], ah, al_, o=o)
                    mm.then_inc(s_mm, 1)

                linear_two(M_K2, (False, True))
                pe.wait_ge(s_mod, B2G + 1)
                for j in range(2):
                    linear_two(M_V2[j], (True, True))
                linear_two(M_AL, (False, False))
                linear_mid(M_Q2, hh, hl)
                pe.wait_ge(s_mid, pl.um[M_AL] + 2)
                pe.wait_ge(s_wab, 64)
                pe.wait_ge(s_gm3, 2)
                pe.wait_ge(s_cx, 4)
                for tt in range(2):
                    pe.matmul(ps[tt][:, :], alc[:, P * tt:P * tt + P], wab[:, :], start=True, stop=True)
                for j in range(4):
                    mm = pe.matmul(ps[2 + j // 2][:, T * (j % 2):T * (j % 2) + T], wab[:, P * j:P * j + P], alx[:, :], start=True, stop=True)
                mm.then_inc(s_gp, 1)
                for j in range(2):
                    linear_mid(M_OG[j], hh, hl)
                pe.wait_ge(s_gm3, 4)
                pe.wait_ge(s_g, 2)
                ones = one1[:, 0:P]
                pe.matmul(ps[0][:, 0:T], trif[:, :], gc[:, 0, 0:T], start=True, stop=False)
                pe.matmul(ps[0][:, 0:T], ones, gc[:, 1, 0:T], start=False, stop=True)
                pe.matmul(ps[1][:, 0:T], trif[:, :], gc[:, 1, 0:T], start=True, stop=True)
                pe.matmul(ps[0][:, T:512], trib[:, :], gc[:, 0, T:512], start=True, stop=True)
                pe.matmul(ps[1][:, T:512], trib[:, :], gc[:, 1, T:512], start=True, stop=False)
                pe.matmul(ps[1][:, T:512], ones, gc[:, 0, T:512], start=False, stop=True).then_inc(s_cum, 1)
                for j in range(2):
                    linear_mid(M_SC[j], hh, hl)
                pe.wait_ge(s_kd, 1)
                pe.wait_ge(s_g, 4)
                for f in range(2):
                    for h in range(GHD):
                        dst = ps[2][64 * (h % 2):64 * (h % 2) + 64, 256 * f + P * (h // 2):256 * f + P * (h // 2) + P]
                        for tt in range(2):
                            mm = pe.matmul(dst, wc[:, tt, 256 * f + 64 * h:256 * f + 64 * h + 64], vctx[:, tt, P * h:P * h + P],
                                           start=tt == 0, stop=tt == 1)
                mm.then_inc(s_st, 1)
                for j in range(2):
                    linear_mid(M_SX[j], hh, hl)
                for j in range(2):
                    linear_mid(M_SB[j], hh, hl)

                def level(n):
                    if n == 0:
                        pe.wait_ge(s_ste, 1)
                        pe.wait_ge(s_mid, pl.um[M_Q2] + 1)
                        op = qk[:, :, :]
                    else:
                        pe.wait_ge(s_E, n)
                        op = eb[:, (n - 1) % 2, :, :]
                    if n >= 2:
                        pe.wait_ge(s_A, n - 1)
                    for jt in range(2):
                        it = 1 - jt if n == 1 else jt
                        for h in range(GHD):
                            b = slice(64 * (h % 2), 64 * (h % 2) + 64)
                            c = 2 * jt + h // 2
                            mm = pe.matmul(ps[2 * (n % 2) + h % 2][:, P * c:P * c + P], op[b, 2 + h // 2, P * jt:P * jt + P],
                                           op[b, h // 2, P * it:P * it + P], start=True, stop=True)
                    mm.then_inc(s_lev, 1)

                level(0)
                for n in range(1, 9):
                    level(n)
                    ada_chunk(8 * B2SC + n - 1)
                    if n > 1:
                        ada_col(8 * B2SC + n - 2)
                ada_col(8 * B2SC + 7)
                pe.wait_ge(s_qi, 1)
                pe.wait_ge(s_A, 9)
                for h in range(GHD):
                    b = slice(64 * (h % 2), 64 * (h % 2) + 64)
                    o = ps[2 + h % 2][:, T * (h // 2):T * (h // 2) + T]
                    for f in range(2):
                        pe.matmul(o, st[b, f, h // 2, :], qi[b, 2 * f + h // 2, :], start=f == 0, stop=False)
                    for it in range(2):
                        for jt in range(2):
                            a_ = (a_d if it == jt else a_x)[:, h % 2, jt, h // 2, :]
                            mm = pe.matmul(o[:, P * it:P * it + P], vx[:, jt, P * h:P * h + P], a_, start=False, stop=it + jt == 2)
                mm.then_inc(s_o4, 1)
                pe.wait_ge(s_o2, 1)
                for b in range(2):
                    mm = pe.matmul(ps[b][:, :], onesm[:, :], o2[:, 2 * b:2 * b + 2, :].rearrange("p k t -> p (k t)"), start=True, stop=True)
                mm.then_inc(s_ms4, 1)
                pe.wait_ge(s_cv, 1)
                pe.wait_ge(s_gs, 1)
                for j in range(4):
                    linear_y(M_WO[j], j, hh, hl)
                if not has("ffn2"):
                    mean_square(10)

            if has("ffn2"):
                boundary(10, None)
                pe.wait_ge(s_yfree, 20)
                pe.wait_ge(s_mid, pl.ua[8 * B2SC + 7] + 1)
                pe.wait_ge(s_mod, B2SC + 1)

                def up(m, bank, i=0, o=None):
                    split_ready(m, i)
                    feature_major(m, lambda nt: ps[bank][:, T * nt:T * nt + T], hh, hl, o=o).then_inc(s_mm, 1)

                def conv_body(c, i=0):
                    if c:
                        pe.wait_ge(s_ue, c + 2 * i)
                    up(M_UP + 3 * c + 2, 4 + (c + 1) % 2, i)
                    if c:
                        pe.wait_ge(s_fa, c + 2 * i)
                    up(M_UP + 3 * c + 3, 6 + (c + 1) % 2, i)
                    down(c, M_UP + 3 * c + 4, i)

                def down(c, m, i=0):
                    split_ready(m, i)
                    pe.wait_ge(s_cact, c + 1 + 2 * i)
                    rows_onto_y(m, chi[:, c % 2, :], clo[:, c % 2, :], last=c == CF - 1).then_inc(s_mm, 1)

                up(M_UP, 4, o=7)
                up(M_UP + 1, 6)
                open_y()
                conv_body(0)
                with pe.Fori(0, 4) as i:
                    for j in range(2):
                        conv_body(1 + j, i)
                conv_body(9)
                down(10, M_UP + 32)
                mean_square(12)

            pe.wait_ge(s_x, 4 * N_UPD + 4)
            pe.wait_ge(s_yfree, 4 * N_UPD) if N_UPD else None
            pe.wait_ge(s_wTc, 2) if has("gmlp") else None
            for b in range(4):
                for q in range(4):
                    kt = 4 * (b % 2) + q
                    mm = pe.transpose(ps[b][:, q * P:q * P + P], x[:, kt, (b // 2) * P:(b // 2) * P + P], ident[:, :])
                mm.then_inc(s_oT, 1)

        @block.gpsimd
        def _(pool):
            chain = [0]

            def link(ins):
                ins.then_inc(g_ch, 1)
                chain[0] += 1
                pool.wait_ge(g_ch, chain[0])

            link(pool.memset(ident[:, :], 0.0))
            pool.affine_select(out=ident[:, :], in_=ident[:, :], compare_op=ALU.not_equal, fill=1.0, base=0,
                               pattern=[[-1, P]], channel_multiplier=1).then_inc(s_const, 1)
            pool.memset(onesm[:, :], 1.0 / D).then_inc(s_const, 1)
            pool.memset(zb[:, :], 0.0).then_inc(s_const, 1)
            pool.memset(one1[:, :], 1.0).then_inc(s_const, 1)
            pool.memset(zero1[:, :], 0.0).then_inc(s_const, 1)
            pool.memset(cpad[:, :, :, :], 0.0).then_inc(s_cpad0, 1)
            if has("gmlp"):
                pool.wait_ge(s_wTc, 2)
                pool.affine_select(out=wT[:, :, :], in_=wT[:, :, :], compare_op=ALU.is_ge, fill=0.0, base=0,
                                   pattern=[[0, 8], [1, P]], channel_multiplier=-1).then_inc(s_wT, 1)

            if has("attn"):
                pool.wait_ge(s_mm, M_FF[0] + 32)
                link(pool.memset(cmask[:, :], 0.0))
                pool.affine_select(out=cmask[:, :], in_=cmask[:, :], compare_op=ALU.is_ge, fill=NEG, base=P,
                                   pattern=[[-1, T]], channel_multiplier=1).then_inc(s_asm, 1)
                for m_, keep, fill in ((cmm, 0.0, NEG), (cm01, 1.0, 0.0)):
                    link(pool.memset(m_[:, :, :], keep))
                    pool.affine_select(out=m_[:, :, :], in_=m_[:, :, :], compare_op=ALU.is_ge, fill=fill, base=-31,
                                       pattern=[[P, 2], [-16, NCP]], channel_multiplier=1).then_inc(s_asm, 1)

            if has("gla"):
                pool.wait_ge(s_mm, M_FF[1] + 32)
                pool.memset(wab[:, :], 0.0).then_inc(s_wz, 1)
                pool.wait_ge(s_wz, 1)
                for n, a in enumerate((alx, alc)):
                    pool.memset(a[32:33, :], 1.0).then_inc(s_gm3, 1)
                    pool.wait_ge(s_gm3, n + 1)
                for tri, cm in ((trif, 1), (trib, -1)):
                    link(pool.memset(tri[:, :], 1.0))
                    pool.affine_select(out=tri[:, :], in_=tri[:, :], compare_op=ALU.is_ge, fill=0.0, base=-1,
                                       pattern=[[-cm, P]], channel_multiplier=cm).then_inc(s_gm3, 1)
                link(pool.memset(lmask[:, :, :], 1.0))
                for n in range(7):
                    s = 64 >> n
                    v = lmask[:, n, :].rearrange("p (b a e) -> p b a e", a=2, e=s)
                    link(pool.affine_select(out=v, in_=v, compare_op=ALU.is_ge, fill=0.0, base=-s,
                                            pattern=[[-2 * s, P // (2 * s)], [s, 2], [0, s]], channel_multiplier=1))
                    ins = pool.affine_select(out=v, in_=v, compare_op=ALU.is_ge, fill=0.0, base=2 * s - 1,
                                             pattern=[[2 * s, P // (2 * s)], [-s, 2], [0, s]], channel_multiplier=-1)
                    if n < 6:
                        link(ins)
                ins.then_inc(s_gm3, 5)
                pool.wait_ge(s_B, 1)
                for l in range(8):
                    s = 128 >> l
                    if l >= 2:
                        pool.wait_ge(s_lev, l)
                    blocks = lambda a: a.rearrange("p k (b e) -> p k b e", e=2 * s)
                    fw, bw = blocks(bx[:, 0:2, :]), blocks(bx[:, 2:4, :])
                    eq, ek = blocks(eb[:, l % 2, 0:2, :]), blocks(eb[:, l % 2, 2:4, :])
                    shape = [P, 2, T // (2 * s), s]
                    fm_, bm = fw[:, :, :, s - 1:s].broadcast_to(shape), bw[:, :, :, s:s + 1].broadcast_to(shape)
                    left, right = slice(0, s), slice(s, 2 * s)
                    pool.tensor_tensor(eq[:, :, :, right], fw[:, :, :, right], fm_, ALU.subtract)
                    pool.tensor_tensor(ek[:, :, :, left], fm_, fw[:, :, :, left], ALU.subtract)
                    pool.tensor_tensor(eq[:, :, :, left], bm, bw[:, :, :, left], ALU.subtract)
                    pool.tensor_tensor(ek[:, :, :, right], bw[:, :, :, right], bm, ALU.subtract).then_inc(s_D, 1)


_INS = ["x", "c", "ada_w", "ada_b", "norm_g", "a_w_in", "a_ln_g", "a_ln_b", "a_w_s", "a_b_s", "a_w_out", "kv_ada_w",
        "kv_ada_b", "kv_norm_g", "kv_w", "cmp_pos", "cmp_w1", "cmp_b1", "cmp_w2", "cmp_b2", "b_w_in", "b_w_out",
        "ff_w_in", "ff_w_out", "c_2", "ctx_2", "c_ctx_2", "w_ada_2", "b_ada_2", "g_pre_mix_2", "g_post_mix_2",
        "g_pre_ffn_2", "g_post_ffn_2", "w_in_2", "w_af_2", "b_af_2", "w_ab_2", "b_ab_2", "g_head_2", "w_sc_2",
        "b_sc_2", "w_out_2", "w_up_2", "w_cf_2", "b_cf_2", "w_down_2"]
_OUTS = [((1, 256, 1024), "float32")]


def kernel(**inputs):
    import numpy as _np
    import concourse.bacc as _bacc
    from concourse import mybir as _mybir
    from concourse.bass_utils import run_bass_kernel_spmd as _run

    nc = _bacc.Bacc("TRN2", target_bir_lowering=False, num_devices=1)
    arrays, args = {}, {}
    for name in _INS:
        a = _np.ascontiguousarray(inputs[name])
        arrays[f"in_{name}_dram"] = a
        args[name] = nc.dram_tensor(f"in_{name}_dram", a.shape, _mybir.dt.from_np(a.dtype), kind="ExternalInput").ap()
    shape, dtype = _OUTS[0]
    res = nc.dram_tensor("out_0_dram", shape, _mybir.dt.from_np(_np.dtype(dtype)), kind="ExternalOutput").ap()
    build(nc, args, res)
    r = _run(nc, [arrays], core_ids=[0])
    return r.results[0]["out_0_dram"]
```

```python
import concourse.bass as bass
from concourse import mybir

F32 = mybir.dt.float32
F32R = mybir.dt.float32r
BF16 = mybir.dt.bfloat16
I8 = mybir.dt.int8
ALU = mybir.AluOpType
ACT = mybir.ActivationFunctionType
AX = mybir.AxisListType

P = 128
T = 256
D = 1024
KT = D // P
EPS = 1e-6
NEG = -1e30
CH = 2048
WARM_KT, WARM_UPDATE, WARM_ADA, WARM_H, WARM_CTX, WARM_LEVEL = 1, 16, 2, 20, 12, 3
RAW = 6
SPL = 3
MID = 3

STAGES = ["x", "gmlp", "ffn0", "attn", "ffn1", "gla", "ffn2"]


class Plan:

    def __init__(self):
        self.src, self.kind, self.order = [], [], []
        self.nm, self.na, self.um, self.ua = [], [], [], []
        self.width = []
        self.u = 0
        self.bank = []

    def m(self, src, mids=1, width=CH):
        self.nm.append(len(self.src))
        self.um.append(self.u)
        self.bank += [4 + (self.u + i) % MID for i in range(mids)]
        self.u += mids
        self.kind.append("M")
        self.order.append(len(self.nm) - 1)
        self.width.append(width)
        self.src.append(src)
        return len(self.nm) - 1

    def a(self, src, bank):
        self.na.append(len(self.src))
        if len(self.na) % 2:
            self.bank.append(bank)
            self.u += 1
        self.ua.append(self.u - 1)
        self.kind.append("A")
        self.order.append(len(self.na) - 1)
        self.src.append(src)

    def before(self, u):
        return max([v + 1 for v in range(u) if self.bank[v] == self.bank[u]], default=0)


def cols(w, c0, n=256):
    return w.rearrange("(k p) n -> p k n", p=P)[:, :, c0:c0 + n]


def rows(w, r0, n=2):
    return w.rearrange("(k p) n -> p k n", p=P)[:, r0:r0 + n, :]


def build(nc, I, out, upto="ffn2"):
    stage_n = STAGES.index(upto)

    def has(s):
        return stage_n >= STAGES.index(s)

    pl = Plan()
    ada = {0: I["ada_w"][0], 1: I["ada_w"][1], 2: I["w_ada_2"][0], "kv": I["kv_ada_w"]}
    BATCH = [(0, 0), (0, 1), (0, 2), (1, 0), ("kv", 0), (1, 1), (1, 2), (2, 0), (2, 1), (2, 2)]
    B0SH, B0G, B0SC, B1SH, BKV, B1G, B1SC, B2SH, B2G, B2SC = range(10)

    SUMS = {}

    def ada_batch(b, more=0):
        w, third = BATCH[b]
        if b in (B1G, B1SC):
            SUMS[b] = (2, T + 32 * (b - B1G))
            banks = [7, 7]
        else:
            SUMS[b] = (4 + (pl.u + 4 + more + 2) % MID, 0)
            banks = [k for k in (4, 5, 6) if k != SUMS[b][0]]
        for j in range(8):
            half, c0 = j % 2, 2048 * third + 512 * (j // 2)
            pl.a(ada[w].rearrange("(k p) n -> p k n", p=P)[:, 4 * half:4 * half + 4, c0:c0 + 512], banks[j // 2 % 2])

    ada_batch(B0SH)
    if has("gmlp"):
        M_V = [pl.m(cols(I["a_w_in"][0], 1024 + 256 * j)) for j in range(4)]
        M_U = [pl.m(cols(I["a_w_in"][0], 256 * j)) for j in range(4)]
        ada_batch(B0G, 4)
        ada_batch(B0SC)
        M_AO = [pl.m(cols(I["a_w_out"][0], 256 * j), 0) for j in range(4)]
    M_FF = {}
    if has("ffn0"):
        ada_batch(B1SH)

    def ffn_chunks(f):
        m0 = pl.m(cols(I["ff_w_in"][f], 0))
        for c in range(15):
            pl.m(cols(I["ff_w_in"][f], 256 * (c + 1)))
            pl.m(rows(I["ff_w_out"][f], 2 * c), 0)
        pl.m(rows(I["ff_w_out"][f], 30), 0)
        M_FF[f] = m0

    if has("ffn0"):
        ffn_chunks(0)
    if has("attn"):
        ada_batch(BKV)
        M_KC, M_VC, M_KS, M_KW, M_VS, M_VW = [pl.m(cols(I["kv_w"], 256 * j)) for j in (0, 1, 2, 4, 3, 5)]
        M_Q = [pl.m(cols(I["b_w_in"][0], 256 * c)) for c in range(4)]
        M_GT = pl.m(cols(I["b_w_in"][0], 1024, 48), 1, 384)
        M_CW = [[pl.m(rows(I["cmp_w1"][j], 8 * c, 8), 0) for c in range(2)] for j in range(2)]
        ada_batch(B1G)
        ada_batch(B1SC)
        M_BO = [pl.m(cols(I["b_w_out"][0], 256 * j), 0) for j in range(4)]
    if has("ffn1"):
        ada_batch(B2SH)
        ffn_chunks(1)
    if has("gla"):
        ada_batch(B2G)
        w2 = I["w_in_2"][0]
        M_K2 = pl.m(cols(w2, 0), 2)
        M_V2 = [pl.m(cols(w2, 256 + 256 * j), 2) for j in range(2)]
        M_AL = pl.m(cols(w2, 768, 128), 2, 1024)
        M_Q2 = pl.m(cols(w2, 800))
        M_OG = [pl.m(cols(w2, 1056 + 256 * j)) for j in range(2)]
        M_SC = [pl.m(cols(w2, 2080 + 256 * j)) for j in range(2)]
        M_SX = [pl.m(cols(w2, 2592 + 256 * j)) for j in range(2)]
        M_SB = [pl.m(cols(w2, 1568 + 256 * j)) for j in range(2)]
        ada_batch(B2SC)
        M_WO = [pl.m(cols(I["w_out_2"][0], 256 * j), 0) for j in range(4)]
        spare = [k for k in (4, 5, 6) if k != SUMS[B2SC][0]]
        O_BANKS, MS_BANKS = [7, spare[0]], [spare[1], SUMS[B2SC][0]]
    if has("ffn2"):
        wup, wdn = I["w_up_2"][0], I["w_down_2"][0]
        M_UP = pl.m(cols(wup, 0), 0)
        pl.m(cols(wup, 2816), 0)
        for c in range(10):
            pl.m(cols(wup, 256 * (c + 1)), 0)
            pl.m(cols(wup, 2816 + 256 * (c + 1)), 0)
            pl.m(rows(wdn, 2 * c), 0)
        pl.m(rows(wdn, 20), 0)
    NM, NN = len(pl.nm), len(pl.src)
    POOL_SPLITS = []
    if has("ffn0"):
        POOL_SPLITS.append(M_FF[0])
    if has("attn"):
        POOL_SPLITS.append(M_KC)
    if has("ffn1"):
        POOL_SPLITS.append(M_FF[1])
    if has("gla"):
        POOL_SPLITS.append(M_K2)
    if has("ffn2"):
        POOL_SPLITS.append(M_UP)

    at = [16512]

    def take(nbytes):
        o = at[0]
        at[0] += (nbytes + 31) // 32 * 32
        return o

    def sb(name, shape, dt=F32, off=None):
        size = 1
        for s in shape[1:]:
            size *= s
        size *= {F32: 4, F32R: 4, BF16: 2, I8: 1}[dt]
        return nc.alloc_sbuf_tensor_at(name, shape, dt, offset=take(size) if off is None else off)

    raw = sb("raw", [P, RAW, CH])
    whi = sb("whi", [P, SPL, CH], F32R)
    wlo = sb("wlo", [P, SPL, CH], F32R)
    x = sb("x", [P, KT, T])
    hh = sb("hh", [P, KT, T], F32R)
    hl = sb("hl", [P, KT, T], F32R)
    oK = take(16384)
    gh = sb("gh", [P, KT, T], F32R, oK)
    gl = sb("gl", [P, KT, T], F32R, oK + 8192)
    oS = take(24576)
    sq = sb("sq", [P, KT, T], F32, oS)
    tt_ = sb("tt_", [P, KT, T], F32, oS + 8192)
    h32 = sb("h32", [P, KT, T], F32, oS + 16384)
    ident = sb("ident", [P, P])
    onesm = sb("onesm", [P, P])
    one1 = sb("one1", [P, 256])
    eps = sb("eps", [P, 1])
    zero1 = sb("zero1", [P, 1])
    zb = sb("zb", [P, 512], BF16)
    NV = [96, 107, 99, 99, 112, 48]
    V0 = [sum(NV[:i]) for i in range(7)]
    vec = sb("vec", [P, V0[6]])
    mod = sb("mod", [P, 11, 16])
    coef = sb("coef", [P, 14, KT])
    csil = sb("csil", [P, 24])
    cpad = sb("cpad", [P, 2, KT, 32])
    stage = sb("stage", [P, 2, 512])
    sel = sb("sel", [P, 2])
    vv = sb("vv", [P, T])
    r0 = sb("r0", [P, T])
    n1 = sb("n1", [P, T])
    rs = sb("rs", [P, T])
    oP = at[0]
    LIMIT = 229368

    def region(base, end):
        pos = [base]

        def f(name, shape, dt=F32):
            size = 1
            for s in shape[1:]:
                size *= s
            size *= {F32: 4, F32R: 4, BF16: 2, I8: 1}[dt]
            o = pos[0]
            pos[0] += (size + 31) // 32 * 32
            assert pos[0] <= end, (name, pos[0], end)
            return nc.alloc_sbuf_tensor_at(name, shape, dt, offset=o)

        return f

    r = region(oP, LIMIT)
    wT = r("wT", [P, 8, P])
    bs_b = r("bs_b", [P, 8, P])
    lng = r("lng", [P, D])
    lnb = r("lnb", [P, D])
    ws = r("ws", [P, 8, P])
    bst = r("bst", [P, 2, 2, 6])
    mv = r("mv", [P, 2, 2])
    lr = r("lr", [P, 4, 2])
    rK = region(oK, oK + 16384)
    v_tm = rK("v_tm", [P, 2, D])
    u_fm = rK("u_fm", [P, KT, T])
    x_tm = sb("x_tm", [P, 2, D], F32, oS + 8192)
    vrow = sb("vrow", [P, 6, P], F32, oS + 16384)
    r = region(oP, LIMIT)
    fr = r("fr", [P, 512])
    fm = r("fm", [P, 512])
    fhi = r("fhi", [P, 3, 512], F32R)
    flo = r("flo", [P, 3, 512], F32R)
    y_tm = sb("y_tm", [P, 2, D], F32, oS)

    NC, NCP, HD, NG, NH = 15, 16, 64, 4, 16
    r = region(oP, LIMIT)
    kc = r("kc", [P, NG, NCP + T])
    kw = r("kw", [P, NG, T])
    v_s = r("v_s", [P, 2, NG * HD])
    v_w = r("v_w", [P, 2, NG * HD])
    ks_fm = r("ks_fm", [P, 2, T])
    kw_fm = r("kw_fm", [P, 2, T])
    cmask = r("cmask", [P, T])
    cmm = r("cmm", [P, 2, NCP])
    cm01 = r("cm01", [P, 2, NCP])
    gate = r("gate", [P, 2, 48])
    hid = r("hid", [P, 2, 2, 60])
    ht = r("ht", [NG * NC, 2, T])
    w2k = r("w2k", [P, 2, P])
    w2v = r("w2v", [P, 2, HD])
    b2k = r("b2k", [P, 1])
    b2v = r("b2v", [NCP, HD])
    vcs = r("vcs", [NCP, NG, HD])
    mx = r("mx", [P, 2, 6])
    nb = r("nb", [P, 2, 6])
    den = r("den", [P, 2, 6])
    rec = r("rec", [P, 2, 6])
    cf = r("cf", [P, 2, 6])
    qT = sb("qT", [P, KT, T], F32, oK)
    pp = sb("pp", [P, 2, 800], F32, oK + 8192)
    bsh = [sb(f"bsh{j}", [P, NG, T], F32, oS + 8192 + 4096 * j) for j in range(2)]
    pts = sb("pts", [P, 2, 1024], F32, oS + 8192)
    rS = region(oS + 16384, oS + 24576)
    blk = rS("blk", [P, 16, NG, NC])
    kc_fm = rS("kc_fm", [P, 2, T])
    vc_fm = rS("vc_fm", [P, 2, T])
    rS = region(oS, oS + 8192)
    WIN = NG * NC
    bw = rS("bw", [P, 2 * 16 * WIN + P - WIN], F32R)
    bhi, blo = (bw[:, 16 * WIN * i:16 * WIN * i + 16 * WIN].rearrange("p (i w) -> p i w", w=WIN) for i in range(2))

    GHD = 4
    r = region(oP, LIMIT)
    qk = r("qk", [P, 4, T])
    kctx = r("kctx", [P, 2, T])
    o_v = oP + 6144
    vx = r("vx", [P, 2, 512])
    vctx = r("vctx", [P, 2, 512])
    cx = sb("cx", [P, KT, T], F32, o_v)
    alx = r("alx", [33, T])
    alc = r("alc", [33, T])
    wab = r("wab", [33, 512])
    st = r("st", [P, 2, 2, P])
    trif = r("trif", [P, P])
    trib = r("trib", [P, P])
    lmask = r("lmask", [P, 7, P], I8)
    tot = r("tot", [P, 2])
    ctx_tm = sb("ctx_tm", [P, 2, D], F32, oK)
    rK = region(oK, oK + 16384)
    gc = rK("gc", [P, 2, 512])
    wc = rK("wc", [P, 2, 512])
    gx = rK("gx", [P, 4, T])
    bx = rK("bx", [P, 4, T])
    a_x = sb("a_x", [P, 2, 2, 2, P], F32, oK)
    a_d = sb("a_d", [P, 2, 2, 2, P], F32, oK + 4096)
    qi = sb("qi", [P, 4, T], F32, oK + 8192)
    r4 = sb("r4", [P, 4, T], F32, oK + 4096)
    v4 = sb("v4", [P, 4, T], F32, oK + 8192)
    n4 = sb("n4", [P, 4, T], F32, oK + 12288)
    rS = region(oS, oS + 24576)
    og = rS("og", [P, 4, T])
    sbt = rS("sbt", [P, 4, T])
    ct = rS("ct", [P, 4, T])
    sct = rS("sct", [P, 4, T])
    eb = rS("eb", [P, 2, 4, T])
    o2 = sb("o2", [P, 4, T], F32, oS + 16384)
    o4 = sb("o4", [P, 4, T], F32, oS + 20480)

    CF = I["w_down_2"].shape[1] // 256
    r = region(oP, LIMIT)
    ut = r("ut", [P, 2, T])
    cvt = r("cvt", [P, 2, T])
    sl = r("sl", [P, 2, T])
    fa = r("fa", [P, 2, T])
    chi = r("chi", [P, 2, 512], F32R)
    clo = r("clo", [P, 2, 512], F32R)

    ps = [nc.alloc_psum_tensor(f"bank{i}", [P, 512], F32) for i in range(8)]
    stat = ps[7][:, 0:256]

    def sums(b, c=0):
        bank, at_ = SUMS[b]
        return ps[bank][:, at_:at_ + 32].rearrange("p (n c) -> p n c", c=2)[:, :, c]


    sems = {}

    def sem(name):
        if name not in sems:
            sems[name] = nc.alloc_semaphore(name)
        return sems[name]

    raw_full = [sem(f"raw_full{i}") for i in range(RAW)]
    s_hi, s_lo, s_mm = sem("hi_ready"), sem("lo_ready"), sem("chunk_multiplied")
    s_ada = sem("ada_multiplied")
    s_mid = sem("mid_evacuated")

    def vc(tile, row):
        return V0[tile] + row

    C_NORM = [[vc(0, 24 + 8 * (4 * l + i)) for i in range(4)] for l in range(2)]
    C_KVN = vc(0, 88)
    C_PREMIX, C_POSTMIX, C_PREFFN, C_POSTFFN = (vc(1, 8 * i) for i in range(4))
    C_BSC, C_WSC, C_BCF, C_B1, C_GH, C_POS = vc(1, 32), vc(1, 36), vc(1, 48), vc(1, 70), vc(1, 74), vc(1, 75)
    C_WCF = V0[2]
    C_ADAB = V0[4]
    BIAS = [C_ADAB + {0: 0, 1: 48, "kv": 96, 2: 112}[w] + 16 * t for w, t in BATCH]

    (A_N0, G_N1, A_N2, G_N3, A_KV, A_N4, G_N5, A_N6, G_N7, A_N8, A_N9, G_N10, A_N11, G_N12) = range(14)
    SH = lambda b: mod[:, b, 0:8]
    SC = lambda b: mod[:, b, 8:16]
    COEFS = {
        B0SH: [(A_N0, "A", SC(B0SH), C_NORM[0][0])],
        B0G: [(G_N1, "G", SH(B0G), C_NORM[0][1])],
        B0SC: [(A_N2, "A", SH(B0SC), C_NORM[0][2]), (G_N3, "G", SC(B0SC), C_NORM[0][3])],
        B1SH: [(A_N4, "A", SC(B1SH), C_NORM[1][0])],
        BKV: [(A_KV, "A", SC(BKV), C_KVN)],
        B1G: [(G_N5, "G", SH(B1G), C_NORM[1][1])],
        B1SC: [(A_N6, "A", SH(B1SC), C_NORM[1][2]), (G_N7, "G", SC(B1SC), C_NORM[1][3])],
        B2SH: [(A_N8, "A", SC(B2SH), C_PREMIX), (A_N9, "A", SC(10), C_PREMIX)],
        B2G: [(G_N10, "G", SH(B2G), C_POSTMIX)],
        B2SC: [(A_N11, "A", SH(B2SC), C_PREFFN), (G_N12, "G", SC(B2SC), C_POSTFFN)],
    }

    s_crow = sem("conditions_loaded")
    s_vrow, s_x0, s_gm = sem("vec_rows_loaded"), sem("x_loaded"), sem("gmlp_rows_loaded")
    s_const, s_cpad0 = sem("constants_ready"), sem("cpad_zeroed")
    s_vT, s_vec = sem("vec_transposed"), sem("vec_ready")
    s_sg, s_cp = sem("c_silu"), sem("c_padded")
    s_xT, s_x = sem("x_transposed"), sem("x_ready")
    s_col, s_mod, s_sel = sem("ada_columns_summed"), sem("mod_ready"), sem("row_selector_ready")
    s_v, s_r0, s_v2, s_r2 = sem("variance_ready"), sem("rsqrt_guess"), sem("other_variance_ready"), sem("other_rsqrt_guess")
    s_sq, s_stat, s_rs = sem("squares"), sem("mean_square"), sem("rsqrt_ready")
    s_t, s_hh, s_h = sem("normed"), sem("h_hi_ready"), sem("h_ready")
    s_yb = sem("y_bank_complete")
    s_yfree = sem("y_banks_free")
    s_vn = sem("v_normed")
    s_wsT, s_wTc, s_wT = sem("ws_transposed"), sem("ws_copied"), sem("ws_masked")
    s_mix, s_oa = sem("mixed"), sem("gmlp_out_split")
    s_fsq, s_fh, s_fact = sem("ffn_squared"), sem("ffn_hi"), sem("ffn_act_ready")
    s_oT, s_oc, s_out = sem("out_transposed"), sem("out_copied"), sem("out_stored")
    s_ht, s_htT = sem("cmp_hidden_rows"), sem("cmp_hidden_transposed")
    s_bsh = [sem("k_cmp_shifted"), sem("v_cmp_shifted")]
    s_kcp, s_asm, s_aw = sem("keys_doubled"), sem("attention_masks_ready"), sem("cmp_weights_loaded")
    s_blk, s_hid, s_w2, s_kv = sem("cmp_blocks_split"), sem("cmp_hidden"), sem("cmp_second"), sem("keys_values_ready")
    s_gt = sem("gates_ready")
    s_S, s_Sev, s_nb, s_exp, s_p = sem("scores"), sem("scores_evacuated"), sem("max_ready"), sem("exp_done"), sem("probs_ready")
    s_T, s_Tev, s_TevD, s_O, s_oev, s_oh = (sem("probs_transposed"), sem("sel_probs_copied"), sem("win_probs_copied"),
                                            sem("heads_done"), sem("pairs_evacuated"), sem("pairs_split"))
    s_ctx, s_cT, s_cx = sem("ctx_loaded"), sem("ctx_transposed"), sem("ctx_ready")
    s_wz, s_wab, s_al, s_gm3 = sem("gate_weights_zeroed"), sem("gate_weights_loaded"), sem("gate_rows_ready"), sem("gla_masks_ready")
    s_gp, s_la, s_g = sem("gates_multiplied"), sem("gates_logged"), sem("log_decays_ready")
    s_cum, s_wc, s_kd, s_st, s_ste = (sem("decays_summed"), sem("decays_to_end"), sem("ctx_keys_decayed"),
                                      sem("states_multiplied"), sem("states_ready"))
    s_qev, s_vev, s_B, s_qe, s_qi = (sem("q_k_ready"), sem("v_ready"), sem("decays_cumulated"), sem("state_decays"),
                                     sem("q_for_states"))
    s_D, s_Ex, s_E, s_lev, s_A = (sem("level_differences"), sem("level_decays"), sem("level_operands"),
                                  sem("level_multiplied"), sem("attention_filled"))
    s_og, s_sc, s_sx, s_sb, s_cv = sem("out_gate"), sem("sc_ready"), sem("sx_ready"), sem("sb_ready"), sem("conv_split")
    s_l4 = sem("gla_mean_squares_logged")
    s_o4, s_o2, s_ms4, s_gs = sem("gla_heads_done"), sem("gla_squares"), sem("gla_mean_squares"), sem("gla_out_split")
    s_ue, s_tap, s_sil, s_fa, s_chi, s_cact = (sem("conv_input_ready"), sem("taps_added"), sem("conv_silu"),
                                               sem("conv_gated"), sem("conv_hi"), sem("conv_act_ready"))
    d_ch, a_ch, g_ch = sem("vector_chain"), sem("scalar_chain"), sem("gpsimd_chain")

    N_UPD = [0, 1, 2, 3, 4, 5, 6][stage_n]
    def part(qt, br):
        nk = P * (qt + 1)
        at0 = 0 if qt == 0 else NCP + 2 * P
        lo_, n = [(0, NCP), (NCP, nk), (NCP + nk, nk)][br]
        return slice(at0 + lo_, at0 + lo_ + n)

    def score_psum(qt, br):
        nk = P * (qt + 1)
        if qt == 0:
            return ps[0][:, part(0, br)]
        return ps[2][:, 0:T] if br == 2 else ps[1][:, [slice(0, NCP), slice(NCP, NCP + T)][br]]

    block = nc.Block()
    with block:

        def full(eng, n, i=0, per=1):
            eng.wait_ge(raw_full[n % RAW], 16 * (n // RAW + 1) + 16 * i)

        v8 = lambda a: a.rearrange("(r p) -> r p", p=P)

        @block.sync
        def _(sp):
            x_rows = I["x"][0].rearrange("(t p) d -> p t d", p=P)

            def load(n, i=0, src=None, freed=None):
                if freed is None and n >= RAW:
                    k = pl.order[n - RAW]
                    if pl.kind[n - RAW] == "M":
                        sp.wait_ge(s_lo, k + 1)
                    else:
                        sp.wait_ge(s_ada, k + 1)
                elif freed is not None:
                    sp.wait_ge(s_lo, freed)
                s = pl.src[n] if src is None else src
                k, w = s.shape[1], s.shape[2]
                sp.dma_start(raw[:, n % RAW, 0:k * w].rearrange("p (k n) -> p k n", n=w), s)\
                  .then_inc(raw_full[n % RAW], 16)

            def ffn_loads(f):
                m0 = M_FF[f]
                n0 = pl.nm[m0]
                for n in range(n0, n0 + 7):
                    load(n)
                win = I["ff_w_in"][f].rearrange("(k p) n -> p k n", p=P)
                wout = I["ff_w_out"][f].rearrange("(k p) n -> p k n", p=P)
                with sp.Fori(1, 5) as i:
                    for j in range(3):
                        load(n0 + 1 + 2 * j, src=win[:, :, bass.ds(768 * i + 256 * (j + 1), 256)],
                             freed=m0 + 1 + 2 * j - 6 + 6 * i + 1)
                        load(n0 + 2 + 2 * j, src=wout[:, bass.ds(6 * i + 2 * j, 2), :],
                             freed=m0 + 2 + 2 * j - 6 + 6 * i + 1)
                load(n0 + 31)
                return n0 + 32

            def conv_loads():
                n0 = pl.nm[M_UP]
                for n in range(n0, n0 + 8):
                    load(n)
                wup_ = wup.rearrange("(k p) n -> p k n", p=P)
                wdn_ = wdn.rearrange("(k p) n -> p k n", p=P)
                ff2 = 256 * CF
                with sp.Fori(0, 4) as i:
                    for j in range(2):
                        c = 2 + j
                        for k, src in enumerate((wup_[:, :, bass.ds(512 * i + 256 * (c + 1), 256)],
                                                 wup_[:, :, bass.ds(512 * i + ff2 + 256 * (c + 1), 256)],
                                                 wdn_[:, bass.ds(4 * i + 2 * c, 2), :])):
                            m = 3 * c + 2 + k
                            load(n0 + m, src=src, freed=M_UP + m - 6 + 1 + 6 * i)
                load(n0 + 32)
                return n0 + 33

            for row, src in ((0, v8(I["c"][0])), (8, v8(I["c_2"][0])), (16, v8(I["c_ctx_2"])),
                             (24, I["norm_g"].rearrange("l i (r p) -> (l i r) p", p=P)), (88, v8(I["kv_norm_g"]))):
                sp.dma_start(vrow[row:row + src.shape[0], 0, :], src).then_inc(s_crow, 16)
            sp.dma_start(x_tm[:, :, :], x_rows).then_inc(s_x0, 16)
            n = 0
            while n < NN:
                if n == 10:
                    sp.dma_start(ws[:, :, :], I["a_w_s"][0].rearrange("g t s -> t g s")).then_inc(s_gm, 16)
                    sp.dma_start(bs_b[:, :, :], I["a_b_s"][0:1].broadcast_to([P, 8, P])).then_inc(s_gm, 16)
                    sp.dma_start(lng[:, :], I["a_ln_g"][0:1].broadcast_to([P, D])).then_inc(s_gm, 16)
                    sp.dma_start(lnb[:, :], I["a_ln_b"][0:1].broadcast_to([P, D])).then_inc(s_gm, 16)
                if pl.kind[n] == "M" and pl.order[n] in M_FF.values():
                    f = [k for k in M_FF if M_FF[k] == pl.order[n]][0]
                    n = ffn_loads(f)
                elif has("ffn2") and n == pl.nm[M_UP]:
                    n = conv_loads()
                else:
                    load(n)
                    n += 1
            for b in range(4):
                c = slice(256 * b, 256 * b + 256)
                sp.wait_ge(s_oc, b + 1)
                sp.dma_start(out[0].rearrange("(t p) d -> p t d", p=P)[:, :, c], y_tm[:, :, c]).then_inc(s_out, 16)
            sp.wait_ge(s_out, 64)

        @block.scalar
        def _(act):
            chain = [0]

            def link(ins):
                ins.then_inc(a_ch, 1)
                chain[0] += 1
                act.wait_ge(a_ch, chain[0])

            def load_rows(tile, row, src):
                n = src.shape[0]
                act.dma_start(vrow[row:row + n, tile, :], src).then_inc(s_vrow, 16)

            act.wait_ge(s_vec, 1)
            act.activation(csil[:, :], vec[:, 0:24], ACT.Silu).then_inc(s_sg, 1)
            load_rows(4, 0, I["ada_b"].rearrange("l (r p) -> (l r) p", p=P))
            load_rows(4, 96, v8(I["kv_ada_b"]))
            load_rows(1, 0, v8(I["g_pre_mix_2"][0]))
            load_rows(1, 8, v8(I["g_post_mix_2"][0]))
            load_rows(1, 16, v8(I["g_pre_ffn_2"][0]))
            load_rows(1, 24, v8(I["g_post_ffn_2"][0]))
            load_rows(1, 32, v8(I["b_sc_2"][0]))
            load_rows(1, 36, I["w_sc_2"][0].rearrange("w (r p) -> (w r) p", p=P))
            load_rows(1, 48, v8(I["b_cf_2"][0]))
            load_rows(1, 70, I["cmp_b1"].rearrange("j (r p) -> (j r) p", p=P))
            load_rows(1, 74, I["g_head_2"])
            load_rows(1, 75, I["cmp_pos"].rearrange("j (r a) d -> (j r) (a d)", a=2))
            wcf = I["w_cf_2"][0].rearrange("a b (r p) -> (a b r) p", p=P)
            load_rows(2, 0, wcf[0:99, :])
            load_rows(3, 0, wcf[99:198, :])
            load_rows(5, 0, v8(I["b_ada_2"][0]))

            split_next = [0]

            def hi(m, i=0):
                full(act, pl.nm[m], i)
                if m >= SPL:
                    act.wait_ge(s_mm, m - SPL + 1 + 6 * i)
                w = pl.width[m]
                act.activation(whi[:, m % SPL, 0:w], raw[:, pl.nm[m] % RAW, 0:w], ACT.Copy).then_inc(s_hi, 1)

            def splits(upto_m):
                while split_next[0] < min(upto_m, NM):
                    hi(split_next[0])
                    split_next[0] += 1

            def ada_row(b, j):
                c = 4 * b + j
                act.wait_ge(s_ada, 2 * c + 2)
                if c >= 2:
                    act.wait_ge(s_col, c - 1)
                act.activation(stage[:, c % 2, :], ps[pl.bank[pl.ua[2 * c]]][:, :], ACT.Copy).then_inc(s_mid, 1)

            def ada_rows(b, j0=0, j1=4):
                for j in range(j0, j1):
                    ada_row(b, j)

            def squares(k, src, wait):
                for b in range(4):
                    wait(b)
                    if k and b == 0:
                        act.wait_ge(s_stat, k)
                    act.activation(sq[:, 2 * b:2 * b + 2, :], src(b), ACT.Square).then_inc(s_sq, 1)

            def guess(k):
                act.wait_ge(s_v, k + 1)
                act.activation(r0[:, :], r0[:, :], ACT.Sqrt, bias=zero_col).then_inc(s_r0, 1)

            def y_gains(c, nx):
                if nx > 1:
                    act.wait_ge(s_x, 4 * nx)
                for kt in range(KT):
                    ins = act.activation(tt_[:, kt, :], ps[kt // 2][:, (kt % 2) * T:(kt % 2) * T + T], ACT.Identity,
                                         scale=coef[:, c, kt:kt + 1], bias=zero_col)
                    if kt % 2:
                        ins.then_inc(s_yfree, 1)

            def shift(o, b, dh=hh, free=0):
                if free:
                    act.wait_ge(s_mm, free)
                for kt in range(KT):
                    act.wait_ge(s_t, 8 * o + kt + 1)
                    act.activation(dh[:, kt, :], tt_[:, kt, :], ACT.Identity, bias=mod[:, b[0], b[1] + kt:b[1] + kt + 1])\
                       .then_inc(s_hh, 1)

            def linear_y_squares(k, ms, more=0):
                def wait(b):
                    splits(min(ms[b] + 3, ms[3] + 1 + more))
                    act.wait_ge(s_mm, ms[b] + 1)
                squares(k, from_y, wait)

            zero_col = zero1[:, 0:1]

            def y_done(n, chunks):
                return lambda b: act.wait_ge(s_yb, 3 * n + b + 1) if b < 3 else act.wait_ge(s_mm, chunks)

            act.wait_ge(s_const, 5)
            from_x = lambda b: x[:, 2 * b:2 * b + 2, :]
            from_y = lambda b: ps[b][:, :].rearrange("p (k t) -> p k t", t=T)

            squares(0, from_x, lambda b: act.wait_ge(s_x, b + 1))
            ada_rows(B0SH, 0, 1)
            guess(0)
            ada_rows(B0SH, 1)
            splits(1)
            act.wait_ge(s_mod, 1)
            shift(0, (B0SH, 0))
            splits(3)
            if has("gmlp"):
                for j in range(4):
                    m = M_V[j]
                    act.wait_ge(s_mm, m + 1)
                    act.activation(v_tm[:, :, 256 * j:256 * j + 256], ps[4 + pl.um[m] % MID][:, :].rearrange("p (t n) -> p t n", t=2),
                                   ACT.Gelu_apprx_tanh).then_inc(s_mid, 1)
                    splits(m + 4)
                for j in range(4):
                    m = M_U[j]
                    act.wait_ge(s_mm, m + 1)
                    act.activation(u_fm[:, 2 * j:2 * j + 2, :], ps[4 + pl.um[m] % MID][:, :].rearrange("p (k t) -> p k t", t=T),
                                   ACT.Gelu_apprx_tanh).then_inc(s_mid, 1)
                    splits(min(m + 4, M_AO[0]))
                act.wait_ge(s_v2, 1)
                act.activation(lr[:, 1, :], lr[:, 1, :], ACT.Sqrt, bias=zero_col).then_inc(s_r2, 1)
                ada_rows(B0G)
                ada_rows(B0SC)
                splits(M_AO[3])
                linear_y_squares(1, M_AO)
                y_gains(G_N1, 1)
                guess(1)
            def boundary(k, nx, o, cols_b, b1, free, m):
                if b1 is not None:
                    ada_rows(b1, 0, 2)
                squares(k + 1, from_x, lambda b: act.wait_ge(s_x, 4 * nx + b + 1))
                splits(m + 2)
                guess(k + 1)
                if b1 is not None:
                    ada_rows(b1, 2)
                shift(o, cols_b, hh, free)

            def ffn(f):
                m0, c0 = M_FF[f], 16 * f
                u0 = pl.um[m0]

                def epi(c, m, i=0):
                    u = u0 + c
                    act.wait_ge(s_mm, m + 1 + 6 * i)
                    if c0 + c > 0:
                        act.wait_ge(s_fh, c0 + c + 3 * i)
                        act.wait_ge(s_fsq, c0 + c + 3 * i)
                    act.activation(fr[:, :], ps[4 + u % MID][:, :], ACT.Relu).then_inc(s_mid, 1)
                    act.wait_ge(s_mid, pl.um[m0] + c + 1 + 3 * i)
                    if c0 + c > 0:
                        act.wait_ge(s_fact, c0 + c + 3 * i)
                    act.activation(fm[:, :], fr[:, :], ACT.Square).then_inc(s_fsq, 1)

                epi(0, m0)
                splits(m0 + 4)
                with act.Fori(0, 4) as i:
                    for j in range(3):
                        c = 1 + j
                        epi(c, m0 + 2 * c - 1, i)
                        hi(m0 + 2 * c + 2, i)
                        hi(m0 + 2 * c + 3, i)
                split_next[0] = m0 + 28
                for c in range(13, 16):
                    epi(c, m0 + 2 * c - 1)
                    splits(min(m0 + 2 * c + 4, m0 + 32))

            if has("ffn0"):
                boundary(1, 1, 1, (B0G, 8), B1SH, M_AO[3] + 1, M_FF[0])
                splits(M_FF[0] + 3)
                ffn(0)
                squares(3, from_y, y_done(0, M_FF[0] + 32))
                y_gains(G_N3, 2)
                guess(3)

            if has("attn"):
                ada_rows(BKV, 0, 2)
                act.dma_start(w2k[:, :, 0:HD], I["cmp_w2"][0].rearrange("(k p) n -> p k n", p=P)).then_inc(s_aw, 16)
                act.dma_start(w2k[:, :, HD:P], I["cmp_w2"][0].rearrange("(k p) n -> p k n", p=P)).then_inc(s_aw, 16)
                act.dma_start(w2v[:, :, :], I["cmp_w2"][1].rearrange("(k p) n -> p k n", p=P)).then_inc(s_aw, 16)
                act.dma_start(b2k[0:HD, :], I["cmp_b2"][0].rearrange("(p a) -> p a", a=1)).then_inc(s_aw, 16)
                act.dma_start(b2k[HD:P, :], I["cmp_b2"][0].rearrange("(p a) -> p a", a=1)).then_inc(s_aw, 16)
                act.dma_start(b2v[:, :], I["cmp_b2"][1:2].broadcast_to([NCP, HD])).then_inc(s_aw, 16)
                squares(4, from_x, lambda b: act.wait_ge(s_x, 8 + b + 1))
                splits(M_KC + 2)
                guess(4)
                ada_rows(BKV, 2)
                shift(2, (BKV, 0), gh)
                splits(M_KC + 3)
                shift(3, (B1SH, 0), hh, M_FF[0] + 32)
                splits(M_KC + 3)

                def mid_of(m):
                    return ps[4 + pl.um[m] % MID]

                def evac(m, dst, view):
                    act.wait_ge(s_mm, m + 1)
                    act.activation(dst, view(mid_of(m)), ACT.Copy).then_inc(s_mid, 1)

                two = lambda b: b[:, :].rearrange("p (k t) -> p k t", k=2)
                act.wait_ge(s_h, 32)
                for j, (m, fm_) in enumerate(((M_KC, kc_fm), (M_VC, vc_fm))):
                    evac(m, fm_[:, :, :], two)
                    act.wait_ge(s_mid, pl.um[m] + 1)
                    for half in range(2):
                        for par in range(2):
                            act.dma_start(bsh[j][64 * half:64 * half + 64, par:4:2, 0:T - half],
                                          fm_[64 * par:64 * par + 64, :, half:T]).then_inc(s_bsh[j], 16)
                    splits(m + 4)
                for m, fm_, to in ((M_KS, ks_fm, kc[:, :, NCP:NCP + T]), (M_KW, kw_fm, kw[:, :, :])):
                    evac(m, fm_[:, :, :], two)
                    act.wait_ge(s_mid, pl.um[m] + 1)
                    for half in range(2):
                        for par in range(2):
                            act.dma_start(to[64 * half:64 * half + 64, par:4:2, :], fm_[64 * par:64 * par + 64, :, :])\
                               .then_inc(s_kcp, 16)
                    splits(m + 4)
                evac(M_VS, v_s[:, :, :], two)
                splits(M_VS + 4)
                evac(M_VW, v_w[:, :, :], two)
                splits(M_VW + 4)
                for c in range(4):
                    evac(M_Q[c], qT[:, 2 * c:2 * c + 2, :], two)
                    splits(M_Q[c] + 4)
                act.wait_ge(s_mm, M_GT + 1)
                act.activation(gate[:, :, :], mid_of(M_GT)[:, 0:96].rearrange("p (t n) -> p t n", t=2), ACT.Exp, scale=-1.0)\
                   .then_inc(s_mid, 1)
                splits(M_GT + 4)
                splits(M_CW[1][1] + 1)
                for j in range(2):
                    act.wait_ge(s_mm, M_CW[j][1] + 1)
                    act.activation(ht[:, j, :], ps[j][0:WIN, 0:T], ACT.Copy).then_inc(s_ht, 1)
                for j in range(2):
                    act.wait_ge(s_htT, j + 1)
                    for nt in range(2):
                        act.activation(hid[:, j, nt, :], ps[2 + j][:, WIN * nt:WIN * nt + WIN], ACT.Gelu_apprx_tanh,
                                       bias=vec[:, C_B1 + 2 * j + nt:C_B1 + 2 * j + nt + 1]).then_inc(s_hid, 1)
                def exps(h):
                    hb = h % 2
                    act.wait_ge(s_nb, h + 1)
                    for qt in range(2):
                        for br in range(3):
                            c = 3 * qt + br
                            p_ = pp[:, hb, part(qt, br)]
                            ins = act.activation(p_, p_, ACT.Exp, bias=nb[:, hb, c:c + 1], scale=HD ** -0.5,
                                                 accum_out=den[:, hb, c:c + 1] if br else None)
                    ins.then_inc(s_exp, 1)

                exps(0)
                exps(1)
                for h in range(NH):
                    act.wait_ge(s_T, h + 1)
                    if h >= 2:
                        act.wait_ge(s_O, h - 1)
                    act.activation(pts[:, h % 2, 0:384], ps[3][:, 0:384], ACT.Copy).then_inc(s_Tev, 1)
                    act.activation(pts[0:NCP, h % 2, 384:512], ps[3][0:NCP, 384:512], ACT.Copy).then_inc(s_Tev, 1)
                    if h % 2 == 0 and h:
                        act.wait_ge(s_O, h)
                        act.activation(h32[:, h // 2 - 1, :], ps[5 + (h // 2 - 1) % 2][:, 0:T], ACT.Copy).then_inc(s_oev, 1)
                    if h % 2:
                        ada_row(B1G + h // 8, h % 8 // 2)
                    if h >= 12:
                        splits(M_BO[0] + min(h - 11, 3))
                    if h + 2 < NH:
                        exps(h + 2)
                act.wait_ge(s_O, NH)
                act.activation(h32[:, 7, :], ps[6][:, 0:T], ACT.Copy).then_inc(s_oev, 1)
                linear_y_squares(5, M_BO)
                act.wait_ge(s_mod, B1G + 1)
                y_gains(G_N5, 3)
                guess(5)

            if has("ffn1"):
                boundary(5, 3, 4, (B1G, 8), B2SH, M_BO[3] + 1, M_FF[1])
                splits(M_FF[1] + 3)
                if has("gla"):
                    act.dma_start(ctx_tm[:, :, :], I["ctx_2"][0].rearrange("(t p) d -> p t d", p=P)).then_inc(s_ctx, 16)
                ffn(1)
                squares(7, from_y, y_done(1, M_FF[1] + 32))
                y_gains(G_N7, 4)
                guess(7)

            if has("gla"):
                act.wait_ge(s_wz, 1)
                act.dma_start(wab[0:16, 0:256], I["w_af_2"][0]).then_inc(s_wab, 16)
                act.dma_start(wab[16:32, 256:512], I["w_ab_2"][0]).then_inc(s_wab, 16)
                act.dma_start(wab[32:33, 0:256], I["b_af_2"]).then_inc(s_wab, 16)
                act.dma_start(wab[32:33, 256:512], I["b_ab_2"]).then_inc(s_wab, 16)
                ada_rows(B2G, 0, 2)
                squares(8, from_x, lambda b: act.wait_ge(s_x, 16 + b + 1))
                splits(M_K2 + 2)
                guess(8)
                squares(9, lambda b: cx[:, 2 * b:2 * b + 2, :], lambda b: act.wait_ge(s_cx, b + 1))
                ada_rows(B2G, 2)
                shift(5, (B2SH, 0), hh, M_FF[1] + 32)
                guess(9)
                shift(6, (10, 0), gh)
                splits(M_K2 + 3)
                two = lambda b: b[:, :].rearrange("p (k t) -> p k t", k=2)

                def evac2(m, which, dst, func=ACT.Copy, scale=1.0, view=two):
                    if which == 0:
                        act.wait_ge(s_mm, m + 1)
                    u = pl.um[m] + which
                    act.activation(dst, view(ps[4 + u % MID]), func, scale=scale).then_inc(s_mid, 1)

                evac2(M_K2, 0, qk[:, 2:4, :])
                evac2(M_K2, 1, kctx[:, :, :])
                splits(M_K2 + 4)
                for j in range(2):
                    evac2(M_V2[j], 0, vx[:, :, 256 * j:256 * j + 256])
                    evac2(M_V2[j], 1, vctx[:, :, 256 * j:256 * j + 256])
                    splits(M_V2[j] + 4)
                evac2(M_AL, 0, alx[0:32, :], view=lambda b: b[0:32, 0:T])
                evac2(M_AL, 1, alc[0:32, :], view=lambda b: b[0:32, 0:T])
                splits(M_AL + 4)
                evac2(M_Q2, 0, qk[:, 0:2, :], scale=0.125)
                splits(M_Q2 + 4)
                act.wait_ge(s_gp, 1)
                lt = [wc[:, 0, :], wc[:, 1, :], bx[:, 0:2, :].rearrange("p k t -> p (k t)"),
                      bx[:, 2:4, :].rearrange("p k t -> p (k t)")]
                for b in range(4):
                    ins = act.activation(lt[b], ps[b][:, :], ACT.Abs)
                link(ins)
                for b in range(4):
                    ins = act.activation(lt[b], lt[b], ACT.Exp, scale=-1.0)
                link(ins)
                for b in range(4):
                    act.activation(lt[b], lt[b], ACT.Ln, bias=one1[:, 0:1], scale=1.0).then_inc(s_la, 1)
                for j in range(2):
                    evac2(M_OG[j], 0, og[:, 2 * j:2 * j + 2, :], func=ACT.Silu)
                    splits(M_OG[j] + 4)
                act.wait_ge(s_cum, 1)
                act.wait_ge(s_g, 2)
                for tt in range(2):
                    act.activation(wc[:, tt, :], ps[tt][:, :], ACT.Exp, scale=1.0 / 16).then_inc(s_wc, 1)
                for j in range(2):
                    evac2(M_SC[j], 0, sct[:, 2 * j:2 * j + 2, :])
                    splits(M_SC[j] + 4)
                act.wait_ge(s_st, 1)
                act.activation(st[:, :, :, :], ps[2][:, :].rearrange("p (a b c) -> p a b c", a=2, b=2), ACT.Copy).then_inc(s_ste, 1)
                for j in range(2):
                    evac2(M_SX[j], 0, ct[:, 2 * j:2 * j + 2, :])
                    splits(min(M_SX[j] + 4, M_SB[1] + 1))
                for j in range(2):
                    evac2(M_SB[j], 0, sbt[:, 2 * j:2 * j + 2, :])
                act.wait_ge(s_B, 1)
                act.activation(qi[:, 0:2, :], bx[:, 0:2, :], ACT.Exp, scale=1.0 / 16)
                for j in range(2):
                    ins = act.activation(qi[:, 2 + j, :], bx[:, 2 + j, :], ACT.Exp, bias=tot[:, j:j + 1], scale=-1.0 / 16)
                ins.then_inc(s_qe, 1)
                for l in range(8):
                    act.wait_ge(s_D, l + 1)
                    act.activation(eb[:, l % 2, :, :], eb[:, l % 2, :, :], ACT.Exp, scale=1.0 / 16).then_inc(s_Ex, 1)
                    if l in (2, 4, 6):
                        ada_row(B2SC, l // 2 - 1)
                ada_row(B2SC, 3)
                splits(M_WO[0] + 3)
                act.wait_ge(s_o4, 1)
                for b in range(2):
                    ins = act.activation(o2[:, 2 * b:2 * b + 2, :], two(ps[O_BANKS[b]]), ACT.Square)
                ins.then_inc(s_o2, 1)
                act.wait_ge(s_ms4, 1)
                for b in range(2):
                    act.activation(n4[:, 2 * b:2 * b + 2, :], two(ps[MS_BANKS[b]]), ACT.Ln, bias=eps[:, 0:1], scale=D / P)\
                       .then_inc(s_l4, 1)
                act.wait_ge(s_l4, 2)
                act.activation(r4[:, :, :], n4[:, :, :], ACT.Exp, scale=-0.5).then_inc(s_r2, 1)
                linear_y_squares(10, M_WO, 2 if has("ffn2") else 0)
                y_gains(G_N10, 5)
                guess(10)

            if has("ffn2"):
                boundary(10, 5, 7, (B2G, 8), None, M_WO[3] + 1, M_UP)
                splits(M_UP + 2)

                def conv_epi(c, i=0):
                    m = M_UP + (3 * c - 1 if c else 0)
                    act.wait_ge(s_mm, m + 1 + 6 * i)
                    if c:
                        act.wait_ge(s_tap, 8 * c + 16 * i)
                        act.wait_ge(s_sil, c + 2 * i)
                    bank = ps[4 + c % 2]
                    act.activation(ut[:, :, :], bank[:, :].rearrange("p (k t) -> p k t", t=T), ACT.Copy)
                    for k in range(2):
                        b_, w_ = C_BCF + 2 * c + k, C_WCF + 22 * 4 + 2 * c + k
                        ins = act.activation(cvt[:, k, :], bank[:, T * k:T * k + T], ACT.Identity,
                                             bias=vec[:, bass.ds(b_ + 4 * i, 1)], scale=vec[:, bass.ds(w_ + 4 * i, 1)])
                    ins.then_inc(s_ue, 1)
                    hi(M_UP + 3 * c + 2, i)
                    if c < CF - 1:
                        hi(M_UP + 3 * c + 3, i)
                    act.wait_ge(s_tap, 8 * c + 8 + 16 * i)
                    if c:
                        act.wait_ge(s_fa, c + 2 * i)
                    act.activation(sl[:, :, :], cvt[:, :, :], ACT.Silu).then_inc(s_sil, 1)
                    if c < CF - 1:
                        hi(M_UP + 3 * c + 4, i)
                    act.wait_ge(s_fa, c + 1 + 2 * i)
                    act.activation(chi[:, c % 2, :], fa[:, :, :].rearrange("p k t -> p (k t)"), ACT.Copy).then_inc(s_chi, 1)

                conv_epi(0)
                with act.Fori(0, 4) as i:
                    for j in range(2):
                        conv_epi(1 + j, i)
                conv_epi(9)
                conv_epi(10)
                split_next[0] = NM
                squares(12, from_y, y_done(2, M_UP + 33))
                y_gains(G_N12, 6)
                guess(12)

            act.wait_ge(s_stat, [1, 2, 4, 6, 8, 11, 13][stage_n])
            for b in range(4):
                act.wait_ge(s_oT, b + 1)
                act.activation(y_tm[:, :, 256 * b:256 * b + 256], ps[b][:, :].rearrange("p (t n) -> p t n", t=2), ACT.Copy)\
                   .then_inc(s_oc, 1)

        @block.vector
        def _(dve):
            chain = [0]

            def link(ins):
                ins.then_inc(d_ch, 1)
                chain[0] += 1
                dve.wait_ge(d_ch, chain[0])

            split_next = [0]

            def lo(m, i=0):
                dve.wait_ge(s_hi, m + 1 + 6 * i)
                w = pl.width[m]
                dve.tensor_tensor(wlo[:, m % SPL, 0:w], raw[:, pl.nm[m] % RAW, 0:w], whi[:, m % SPL, 0:w],
                                  ALU.subtract).then_inc(s_lo, 1)

            def splits(upto_m):
                while split_next[0] < min(upto_m, NM):
                    if split_next[0] - 2 in POOL_SPLITS:
                        dve.wait_ge(s_lo, split_next[0])
                    lo(split_next[0])
                    split_next[0] += 1

            def left_to_pool(m):
                split_next[0] = m + 2

            def refine(k):
                dve.wait_ge(s_stat, k + 1)
                link(dve.tensor_scalar(vv[:, :], stat, EPS, None, ALU.add))
                dve.reciprocal(r0[:, :], vv[:, :]).then_inc(s_v, 1)
                dve.wait_ge(s_r0, k + 1)
                link(dve.tensor_tensor(n1[:, :], r0[:, :], r0[:, :], ALU.mult))
                link(dve.scalar_tensor_tensor(out=n1[:, :], in0=n1[:, :], scalar=-0.5, in1=vv[:, :], op0=ALU.mult, op1=ALU.mult))
                dve.scalar_tensor_tensor(out=rs[:, :], in0=n1[:, :], scalar=1.5, in1=r0[:, :], op0=ALU.add, op1=ALU.mult)\
                   .then_inc(s_rs, 1)
                dve.wait_ge(s_rs, k + 1)

            def mods(b):
                dve.wait_ge(s_col, 4 * b + 4)
                link(dve.tensor_tensor(mod[:, b, :], sums(b), vec[:, BIAS[b]:BIAS[b] + 16], ALU.add))
                if b == B2SH:
                    link(dve.tensor_tensor(mod[:, 10, :], sums(b, 1), vec[:, BIAS[b]:BIAS[b] + 16], ALU.add))
                for c, kind, m, g in COEFS[b]:
                    if kind == "A":
                        ins = dve.scalar_tensor_tensor(out=coef[:, c, :], in0=m, scalar=1.0, in1=vec[:, g:g + 8],
                                                       op0=ALU.add, op1=ALU.mult)
                    else:
                        ins = dve.tensor_tensor(coef[:, c, :], m, vec[:, g:g + 8], ALU.mult)
                    if c != COEFS[b][-1][0]:
                        link(ins)
                ins.then_inc(s_mod, 1)
                dve.wait_ge(s_mod, b + 1)

            def make_h(o, c, cols_b, dl=hl, dh=hh, src=x):
                def lo_of(kt):
                    dve.wait_ge(s_hh, 8 * o + kt + 1)
                    b, c0 = cols_b
                    dve.scalar_tensor_tensor(out=dl[:, kt, :], in0=tt_[:, kt, :], scalar=mod[:, b, c0 + kt:c0 + kt + 1],
                                             in1=dh[:, kt, :], op0=ALU.add, op1=ALU.subtract).then_inc(s_h, 1)

                if o:
                    dve.wait_ge(s_h, 8 * o)
                for kt in range(KT):
                    dve.scalar_tensor_tensor(out=tt_[:, kt, :], in0=src[:, kt, :], scalar=coef[:, c, kt:kt + 1], in1=rs[:, :],
                                             op0=ALU.mult, op1=ALU.mult).then_inc(s_t, 1)
                    dve.wait_ge(s_t, 8 * o + kt + 1)
                    if kt >= 2:
                        lo_of(kt - 2)
                lo_of(6)
                lo_of(7)

            def update_x(nx):
                rs2 = rs[:, :].rearrange("p (a t) -> p a t", a=1).broadcast_to([P, 2, T])
                for b in range(4):
                    dve.wait_ge(s_yfree, 4 * (nx - 1) + b + 1)
                    q = slice(2 * b, 2 * b + 2)
                    link(dve.tensor_tensor(tt_[:, q, :], tt_[:, q, :], rs2, ALU.mult))
                    dve.tensor_tensor(x[:, q, :], x[:, q, :], tt_[:, q, :], ALU.add).then_inc(s_x, 1)

            def vectors(i, bank):
                dve.wait_ge(s_vT, i + 1)
                dve.tensor_copy(vec[:, V0[i]:V0[i + 1]], ps[bank][:, 0:NV[i]]).then_inc(s_vec, 1)

            vectors(0, 7)
            dve.wait_ge(s_const, 5)
            link(dve.tensor_tensor(sel[:, :], ident[:, 0:2], ident[:, 32:34], ALU.add))
            link(dve.tensor_tensor(sel[:, :], sel[:, :], ident[:, 64:66], ALU.add))
            dve.tensor_tensor(sel[:, :], sel[:, :], ident[:, 96:98], ALU.add).then_inc(s_sel, 1)
            dve.wait_ge(s_cpad0, 1)
            dve.wait_ge(s_sg, 1)
            dve.tensor_copy(cpad[:, 0, :, 0], csil[:, 0:8]).then_inc(s_cp, 1)
            dve.tensor_copy(cpad[:, 1, :, 0], csil[:, 8:16]).then_inc(s_cp, 1)
            dve.tensor_copy(cpad[:, 1, :, 1], csil[:, 16:24]).then_inc(s_cp, 1)
            for b in range(4):
                dve.wait_ge(s_xT, b + 1)
                dve.tensor_copy(x[:, 2 * b:2 * b + 2, :], ps[b][:, :].rearrange("p (k t) -> p k t", t=T)).then_inc(s_x, 1)
            refine(0)
            for i in range(1, 6):
                vectors(i, 2 + i % 2)
            dve.wait_ge(s_vec, 6)
            mods(B0SH)
            splits(1)
            make_h(0, A_N0, (B0SH, 0))
            splits(3)
            if has("gmlp"):
                for j in range(8):
                    splits(min(j + 4, 8))
                    if j == 3:
                        for b in range(2):
                            dve.wait_ge(s_wsT, b + 1)
                            dve.tensor_copy(wT[:, 4 * b:4 * b + 4, :], ps[b][:, :].rearrange("p (g t) -> p g t", g=4)).then_inc(s_wTc, 1)
                    if j == 5:
                        dve.wait_ge(s_mid, pl.um[M_V[3]] + 1)
                        dve.wait_ge(s_gm, 64)
                        for tt in range(2):
                            for f in range(2):
                                link(dve.bn_stats(bst[:, tt, f, :], v_tm[:, tt, 512 * f:512 * f + 512]))
                        link(dve.bn_aggr(mv[:, 0, :], bst[:, 0, :, :]))
                        link(dve.bn_aggr(mv[:, 1, :], bst[:, 1, :, :]))
                        link(dve.tensor_scalar(lr[:, 2, :], mv[:, :, 1], EPS, None, ALU.add))
                        dve.reciprocal(lr[:, 1, :], lr[:, 2, :]).then_inc(s_v2, 1)
                        dve.wait_ge(s_r2, 1)
                link(dve.tensor_tensor(lr[:, 3, :], lr[:, 1, :], lr[:, 1, :], ALU.mult))
                link(dve.scalar_tensor_tensor(out=lr[:, 3, :], in0=lr[:, 3, :], scalar=-0.5, in1=lr[:, 2, :], op0=ALU.mult, op1=ALU.mult))
                link(dve.scalar_tensor_tensor(out=lr[:, 2, :], in0=lr[:, 3, :], scalar=1.5, in1=lr[:, 1, :], op0=ALU.add, op1=ALU.mult))
                for tt in range(2):
                    link(dve.tensor_scalar(v_tm[:, tt, :], v_tm[:, tt, :], mv[:, tt, 0:1], lr[:, 2, tt:tt + 1], ALU.subtract, ALU.mult))
                for tt in range(2):
                    link(dve.tensor_tensor(v_tm[:, tt, :], v_tm[:, tt, :], lng[:, :], ALU.mult))
                    dve.tensor_tensor(v_tm[:, tt, :], v_tm[:, tt, :], lnb[:, :], ALU.add).then_inc(s_vn, 1)
                mods(B0G)
                dve.wait_ge(s_h, 8)
                dve.wait_ge(s_mid, pl.um[M_U[3]] + 1)
                dve.wait_ge(s_mm, M_U[3] + 1)
                for b in range(4):
                    dve.wait_ge(s_mix, b + 1)
                    bias = bs_b[:, 2 * b:2 * b + 2, :].rearrange("p g (a t) -> p g a t", a=1).broadcast_to([P, 2, 2, P])
                    link(dve.tensor_tensor(tt_[:, 2 * b:2 * b + 2, :].rearrange("p g (a t) -> p g a t", a=2),
                                           ps[b][:, :].rearrange("p (g a t) -> p g a t", g=2, a=2), bias, ALU.add))
                    link(dve.tensor_tensor(h32[:, 2 * b:2 * b + 2, :], tt_[:, 2 * b:2 * b + 2, :], u_fm[:, 2 * b:2 * b + 2, :], ALU.mult))
                    link(dve.tensor_copy(hh[:, 2 * b:2 * b + 2, :], h32[:, 2 * b:2 * b + 2, :]))
                    dve.tensor_tensor(hl[:, 2 * b:2 * b + 2, :], h32[:, 2 * b:2 * b + 2, :], hh[:, 2 * b:2 * b + 2, :], ALU.subtract)\
                       .then_inc(s_oa, 1)
                mods(B0SC)
                dve.wait_ge(s_oa, 4)
                splits(M_AO[3] + 1)
                refine(1)
                update_x(1)

            def boundary(k, nx, o, c, cols_b, b1, m):
                left_to_pool(m)
                refine(k + 1)
                dve.wait_ge(s_x, 4 * nx + 4)
                make_h(o, c, cols_b)
                if b1 is not None:
                    mods(b1)

            def ffn(f):
                m0, c0 = M_FF[f], 16 * f
                mid0 = pl.um[m0]

                def epi(c, i=0, first=False):
                    dve.wait_ge(s_mid, mid0 + c + 1 + 3 * i)
                    if c >= 3:
                        dve.wait_ge(s_mm, m0 + 2 * (c - 3) + 3 + 6 * i)
                    dve.tensor_tensor(fhi[:, c % 3, :], fr[:, :], fr[:, :], ALU.mult).then_inc(s_fh, 1)
                    dve.wait_ge(s_fh, c0 + c + 1 + 3 * i)
                    dve.wait_ge(s_fsq, c0 + c + 1 + 3 * i)
                    dve.tensor_tensor(flo[:, c % 3, :], fm[:, :], fhi[:, c % 3, :], ALU.subtract).then_inc(s_fact, 1)

                epi(0)
                splits(m0 + 4)
                for c in range(1, 4):
                    epi(c)
                    splits(m0 + 2 * c + 4)
                with dve.Fori(0, 3) as i:
                    for j in range(3):
                        c = 4 + j
                        epi(c, i)
                        lo(m0 + 2 * c + 2, i)
                        lo(m0 + 2 * c + 3, i)
                split_next[0] = m0 + 28
                for c in range(13, 16):
                    epi(c)
                    splits(min(m0 + 2 * c + 4, m0 + 32))

            if has("ffn0"):
                boundary(1, 1, 1, A_N2, (B0G, 8), B1SH, M_FF[0])
                splits(M_FF[0] + 3)
                ffn(0)
                refine(3)
                update_x(2)

            if has("attn"):
                left_to_pool(M_KC)
                refine(4)
                dve.wait_ge(s_x, 12)
                mods(BKV)
                make_h(2, A_KV, (BKV, 0), gl, gh)
                splits(M_KC + 3)
                make_h(3, A_N4, (B1SH, 0))
                splits(M_VW + 1)

                def compress(j):
                    dve.wait_ge(s_bsh[j], 64)
                    if j:
                        dve.wait_ge(s_mm, M_CW[0][1] + 1)
                    for half in range(2):
                        src = bsh[j][:, :, 16 * half:16 * half + 240].rearrange("p g (c i two) -> p i g c two", c=NC, two=2)[:, :, :, :, 0]
                        pos = vec[:, C_POS + 16 * j + 8 * half:C_POS + 16 * j + 8 * half + 8]
                        pos = pos.rearrange("p (i a b) -> p i a b", a=1, b=1).broadcast_to([P, 8, NG, NC])
                        link(dve.tensor_tensor(blk[:, 8 * half:8 * half + 8, :, :], src, pos, ALU.add))
                    b60 = blk[:, :, :, :].rearrange("p i g c -> p i (g c)")
                    link(dve.tensor_copy(bhi, b60))
                    if j == 0:
                        dve.tensor_copy(bw[:, 32 * WIN:32 * WIN + P - WIN], one1[:, 0:P - WIN])
                    dve.tensor_tensor(blo, b60, bhi, ALU.subtract).then_inc(s_blk, 1)
                    dve.wait_ge(s_blk, j + 1)

                splits(M_Q[1] + 1)
                compress(0)
                splits(M_CW[0][1] + 1)
                dve.wait_ge(s_mid, pl.um[M_GT] + 1)
                link(dve.tensor_scalar(gate[:, :, :], gate[:, :, :], 1.0, None, ALU.add))
                dve.reciprocal(gate[:, :, :], gate[:, :, :]).then_inc(s_gt, 1)
                splits(M_CW[1][0] + 1)
                compress(1)
                splits(M_CW[1][1] + 1)
                dve.wait_ge(s_gt, 1)
                dve.wait_ge(s_aw, 96)
                dve.wait_ge(s_w2, 1)
                link(dve.memset(kc[:, :, NC:NCP], 0.0))
                dve.tensor_scalar(kc[:, :, 0:NC], ps[0][:, 0:60].rearrange("p (g c) -> p g c", g=NG), b2k[:, 0:1], None, ALU.add)\
                   .then_inc(s_kv, 1)
                bias = b2v[0:NC, :].rearrange("p (a n) -> p a n", a=1).broadcast_to([NC, NG, HD])
                dve.tensor_tensor(vcs[0:NC, :, :], ps[1][0:NC, 0:256].rearrange("p (g n) -> p g n", g=NG), bias, ALU.add)\
                   .then_inc(s_kv, 1)
                dve.wait_ge(s_kv, 2)
                dve.wait_ge(s_asm, 3)

                def scores_out(h):
                    hb = h % 2
                    dve.wait_ge(s_S, h + 1)
                    if h >= 2:
                        dve.wait_ge(s_T, h - 1)
                    for qt in range(2):
                        for br in range(3):
                            mask = cmm[:, qt, :] if br == 0 else cmask[:, P * (1 - qt):T]
                            c = 3 * qt + br
                            ins = dve.tensor_tensor_reduce(pp[:, hb, part(qt, br)], score_psum(qt, br), mask, 1.0, -3e38,
                                                           ALU.add, ALU.max, mx[:, hb, c:c + 1])
                    ins.then_inc(s_Sev, 1)
                    dve.wait_ge(s_Sev, h + 1)
                    dve.tensor_scalar(nb[:, hb, :], mx[:, hb, :], -HD ** -0.5, None, ALU.mult).then_inc(s_nb, 1)

                def gated(h):
                    hb = h % 2
                    dve.wait_ge(s_exp, h + 1)
                    for qt in range(2):
                        p_ = pp[:, hb, part(qt, 0)]
                        ins = dve.tensor_tensor_reduce(p_, p_, cm01[:, qt, :], 1.0, 1e-30, ALU.mult, ALU.add,
                                                       den[:, hb, 3 * qt:3 * qt + 1])
                    link(ins)
                    link(dve.reciprocal(rec[:, hb, :], den[:, hb, :]))
                    link(dve.tensor_tensor(cf[:, hb, :].rearrange("p (t b) -> p t b", t=2),
                                           rec[:, hb, :].rearrange("p (t b) -> p t b", t=2), gate[:, :, 3 * h:3 * h + 3], ALU.mult))
                    for qt in range(2):
                        for br in range(3):
                            c = 3 * qt + br
                            p_ = pp[:, hb, part(qt, br)]
                            ins = dve.tensor_scalar(p_, p_, cf[:, hb, c:c + 1], None, ALU.mult)
                    ins.then_inc(s_p, 1)
                    dve.wait_ge(s_p, h + 1)

                scores_out(0)
                scores_out(1)
                gated(0)
                for h in range(NH):
                    dve.wait_ge(s_T, h + 1)
                    if h >= 2:
                        dve.wait_ge(s_O, h - 1)
                    dve.tensor_copy(pts[:, h % 2, 512:896], ps[4][:, 0:384]).then_inc(s_TevD, 1)
                    dve.tensor_copy(pts[0:NCP, h % 2, 896:1024], ps[4][0:NCP, 384:512]).then_inc(s_TevD, 1)
                    if h + 2 < NH:
                        scores_out(h + 2)
                    if h + 1 < NH:
                        gated(h + 1)
                    if h % 2 == 0 and h:
                        k = h // 2 - 1
                        dve.wait_ge(s_oev, k + 1)
                        link(dve.tensor_copy(hh[:, k, :], h32[:, k, :]))
                        dve.tensor_tensor(hl[:, k, :], h32[:, k, :], hh[:, k, :], ALU.subtract).then_inc(s_oh, 1)
                    if h >= 13:
                        splits(M_BO[0] + min(h - 12, 3))
                dve.wait_ge(s_oev, 8)
                link(dve.tensor_copy(hh[:, 7, :], h32[:, 7, :]))
                dve.tensor_tensor(hl[:, 7, :], h32[:, 7, :], hh[:, 7, :], ALU.subtract).then_inc(s_oh, 1)
                dve.wait_ge(s_oh, 8)
                dve.wait_ge(s_col, 4 * B1SC + 4)
                mods(B1G)
                mods(B1SC)
                splits(M_BO[3] + 1)
                refine(5)
                update_x(3)

            if has("ffn1"):
                boundary(5, 3, 4, A_N6, (B1G, 8), B2SH, M_FF[1])
                splits(M_FF[1] + 3)
                ffn(1)
                refine(7)
                update_x(4)

            if has("gla"):
                for b in range(4):
                    dve.wait_ge(s_cT, b + 1)
                    dve.tensor_copy(cx[:, 2 * b:2 * b + 2, :], ps[b][:, :].rearrange("p (k t) -> p k t", t=T)).then_inc(s_cx, 1)
                left_to_pool(M_K2)
                refine(8)
                dve.wait_ge(s_x, 20)
                make_h(5, A_N8, (B2SH, 0))
                dve.wait_ge(s_cx, 4)
                refine(9)
                make_h(6, A_N9, (10, 0), gl, gh, cx)
                mods(B2G)
                splits(M_Q2 + 4)
                lt = [wc[:, 0, :], wc[:, 1, :], bx[:, 0:2, :].rearrange("p k t -> p (k t)"),
                      bx[:, 2:4, :].rearrange("p k t -> p (k t)")]
                gt = [gc[:, 0, :], gc[:, 1, :], gx[:, 0:2, :].rearrange("p k t -> p (k t)"),
                      gx[:, 2:4, :].rearrange("p k t -> p (k t)")]
                for b in range(4):
                    dve.wait_ge(s_la, b + 1)
                    dve.scalar_tensor_tensor(out=gt[b], in0=ps[b][:, :], scalar=0.0, in1=lt[b], op0=ALU.min, op1=ALU.subtract)                       .then_inc(s_g, 1)
                splits(M_OG[0] + 4)
                dve.wait_ge(s_g, 4)
                link(dve.memset(bx[:, 2:4, 0:1], 0.0))
                for j in range(4):
                    n = T if j < 2 else T - 1
                    ins = dve.tensor_tensor_scan(bx[:, j, T - n:T], one1[:, 0:n], gx[:, j, 0:n], 0.0, ALU.mult, ALU.add)
                link(ins)
                link(dve.tensor_tensor(tot[:, :], bx[:, 2:4, T - 1], gx[:, 2:4, T - 1], ALU.add))
                dve.tensor_scalar(tot[:, :], tot[:, :], 1.0 / 16, None, ALU.mult).then_inc(s_B, 1)
                splits(M_OG[1] + 4)
                for tt in range(2):
                    dve.wait_ge(s_wc, tt + 1)
                    w_ = wc[:, tt, :].rearrange("p (f n) -> p f n", f=2)
                    ins = dve.tensor_tensor(w_, w_, kctx[:, tt:tt + 1, :].broadcast_to([P, 2, T]), ALU.mult)
                ins.then_inc(s_kd, 1)
                for j in range(2):
                    splits(M_SC[j] + 4)
                splits(M_SB[1] + 1)
                for j in range(2):
                    dve.wait_ge(s_mid, pl.um[M_SX[j]] + 1)
                    ins = dve.tensor_tensor(ct[:, 2 * j:2 * j + 2, :], ct[:, 2 * j:2 * j + 2, :], sct[:, 2 * j:2 * j + 2, :], ALU.mult)
                link(ins)
                row = lambda a, k: a[:, k, :].rearrange("p (r w) -> p r w", w=64)
                tap = lambda w, k: vec[:, C_WSC + 4 * w + k:C_WSC + 4 * w + k + 1]
                for k in range(4):
                    ins = dve.tensor_scalar(sct[:, k, :], ct[:, k, :], tap(1, k), vec[:, C_BSC + k:C_BSC + k + 1], ALU.mult, ALU.add)
                link(ins)
                for w, to, frm in ((0, slice(1, 64), slice(0, 63)), (2, slice(0, 63), slice(1, 64))):
                    for k in range(4):
                        ins = dve.scalar_tensor_tensor(out=row(sct, k)[:, :, to], in0=row(ct, k)[:, :, frm], scalar=tap(w, k),
                                                       in1=row(sct, k)[:, :, to], op0=ALU.mult, op1=ALU.add)
                    link(ins)

                def operands(l):
                    dve.wait_ge(s_Ex, l + 1)
                    dve.tensor_tensor(eb[:, l % 2, :, :], eb[:, l % 2, :, :], qk[:, :, :], ALU.mult).then_inc(s_E, 1)

                def fill(n):
                    dve.wait_ge(s_lev, n + 1)
                    for par in range(2):
                        src = ps[2 * (n % 2) + par][:, :].rearrange("p (c i) -> p c i", i=P)
                        dst = (a_x if n == 1 else a_d)[:, par, :, :, :].rearrange("p t g i -> p (t g) i")
                        if n < 2:
                            ins = dve.tensor_copy(dst, src)
                        else:
                            mask = lmask[:, n - 2:n - 1, :].broadcast_to([P, 4, P])
                            ins = dve.copy_predicated(dst, mask, src)
                    ins.then_inc(s_A, 1)
                    dve.wait_ge(s_A, n + 1)

                dve.wait_ge(s_gm3, 9)
                fill(0)
                operands(0)
                for l in range(8):
                    if l < 7:
                        operands(l + 1)
                    fill(l + 1)
                    if l == 0:
                        dve.wait_ge(s_mid, pl.um[M_SB[1]] + 1)
                        link(dve.tensor_tensor(sct[:, :, :], sct[:, :, :], sbt[:, :, :], ALU.mult))
                    if l == 1:
                        dve.wait_ge(s_mm, M_SB[1] + 1)
                        link(dve.tensor_copy(hh[:, 4:8, :], sct[:, :, :]))
                    if l == 2:
                        dve.tensor_tensor(hl[:, 4:8, :], sct[:, :, :], hh[:, 4:8, :], ALU.subtract).then_inc(s_cv, 1)
                    if l == 3:
                        dve.wait_ge(s_qe, 1)
                        q_ = qk[:, 0:2, :].rearrange("p (a k) t -> p a k t", a=1).broadcast_to([P, 2, 2, T])
                        qi_ = qi[:, :, :].rearrange("p (a k) t -> p a k t", a=2)
                        dve.tensor_tensor(qi_, qi_, q_, ALU.mult).then_inc(s_qi, 1)
                mods(B2SC)
                splits(M_WO[0] + 3)
                for b in range(2):
                    q = slice(2 * b, 2 * b + 2)
                    dve.wait_ge(s_l4, b + 1)
                    link(dve.tensor_scalar(v4[:, q, :], ps[MS_BANKS[b]][:, :].rearrange("p (k t) -> p k t", k=2), D / P, EPS, ALU.mult, ALU.add))
                dve.wait_ge(s_r2, 2)
                link(dve.tensor_tensor(n4[:, :, :], r4[:, :, :], r4[:, :, :], ALU.mult))
                link(dve.scalar_tensor_tensor(out=n4[:, :, :], in0=n4[:, :, :], scalar=-0.5, in1=v4[:, :, :], op0=ALU.mult, op1=ALU.mult))
                link(dve.scalar_tensor_tensor(out=r4[:, :, :], in0=n4[:, :, :], scalar=1.5, in1=r4[:, :, :], op0=ALU.add, op1=ALU.mult))
                for b in range(2):
                    ins = dve.scalar_tensor_tensor(out=o4[:, b:4:2, :], in0=ps[O_BANKS[b]][:, :].rearrange("p (k t) -> p k t", k=2),
                                                   scalar=vec[:, C_GH:C_GH + 1], in1=r4[:, 2 * b:2 * b + 2, :], op0=ALU.mult, op1=ALU.mult)
                link(ins)
                link(dve.tensor_tensor(o4[:, :, :], o4[:, :, :], og[:, :, :], ALU.mult))
                link(dve.tensor_copy(hh[:, 0:4, :], o4[:, :, :]))
                dve.tensor_tensor(hl[:, 0:4, :], o4[:, :, :], hh[:, 0:4, :], ALU.subtract).then_inc(s_gs, 1)
                splits(M_WO[3] + 1)
                refine(10)
                dve.wait_ge(s_gs, 1)
                update_x(5)

            if has("ffn2"):
                boundary(10, 5, 7, A_N11, (B2G, 8), None, M_UP)
                TAPS = [(dr, dc) for dr in (-1, 0, 1) for dc in (-1, 0, 1) if (dr, dc) != (0, 0)]
                HROW, WROW = T // 64, 64

                def conv_epi(c, i=0):
                    dve.wait_ge(s_ue, c + 1 + 2 * i)
                    for n, (dr, dc) in enumerate(TAPS):
                        to = (slice(max(0, -dr), HROW - max(0, dr)), slice(max(0, -dc), WROW - max(0, dc)))
                        frm = (slice(max(0, dr), HROW - max(0, -dr)), slice(max(0, dc), WROW - max(0, -dc)))
                        for k in range(2):
                            grid = lambda a: a[:, k, :].rearrange("p (r w) -> p r w", w=WROW)
                            w_ = C_WCF + 22 * (3 * (dr + 1) + dc + 1) + 2 * c + k
                            y = grid(cvt)[:, to[0], to[1]]
                            ins = dve.scalar_tensor_tensor(out=y, in0=grid(ut)[:, frm[0], frm[1]],
                                                           scalar=vec[:, bass.ds(w_ + 4 * i, 1)], in1=y,
                                                           op0=ALU.mult, op1=ALU.add)
                        ins.then_inc(s_tap, 1)
                        dve.wait_ge(s_tap, 8 * c + n + 1 + 16 * i)
                        if n == 3:
                            lo(M_UP + 3 * c + 2, i)
                    if c < CF - 1:
                        lo(M_UP + 3 * c + 3, i)
                    dve.wait_ge(s_mm, M_UP + (3 * c if c else 1) + 1 + 6 * i)
                    dve.wait_ge(s_sil, c + 1 + 2 * i)
                    if c:
                        dve.wait_ge(s_cact, c + 2 * i)
                    dve.tensor_tensor(fa[:, :, :], sl[:, :, :], ps[6 + c % 2][:, :].rearrange("p (k t) -> p k t", t=T), ALU.mult)                       .then_inc(s_fa, 1)
                    if c < CF - 1:
                        lo(M_UP + 3 * c + 4, i)
                    dve.wait_ge(s_fa, c + 1 + 2 * i)
                    dve.wait_ge(s_chi, c + 1 + 2 * i)
                    dve.tensor_tensor(clo[:, c % 2, :], fa[:, :, :].rearrange("p k t -> p (k t)"), chi[:, c % 2, :], ALU.subtract)                       .then_inc(s_cact, 1)

                dve.wait_ge(s_lo, M_UP + 2)
                conv_epi(0)
                with dve.Fori(0, 4) as i:
                    for j in range(2):
                        conv_epi(1 + j, i)
                conv_epi(9)
                conv_epi(10)
                split_next[0] = NM
                refine(12)
                update_x(6)

        @block.tensor
        def _(pe):
            def ada_chunk(a):
                c, u, half = (0 if a < 8 * B2SH else 1), pl.ua[a], a % 2
                full(pe, pl.na[a])
                if not half and pl.before(u):
                    pe.wait_ge(s_mid, pl.before(u))
                w = raw[:, pl.na[a] % RAW, :].rearrange("p (k n) -> p k n", n=512)
                for g in range(4):
                    mm = pe.matmul(ps[pl.bank[u]][32 * g:32 * g + 32, :], cpad[:, c, 4 * half + g, :], w[:, g, :],
                                   start=half == 0, stop=half == 1)
                mm.then_inc(s_ada, 1)

            def ada_col(b, j):
                c = 4 * b + j
                u = pl.ua[2 * c]
                if j == 0:
                    if u:
                        pe.wait_ge(s_mid, u)
                    if b and b != B1SC:
                        pe.wait_ge(s_mod, b)
                pe.wait_ge(s_mid, u + 1)
                bank, at_ = SUMS[b]
                for n in range(4):
                    k = at_ + 2 * (4 * j + n)
                    mm = pe.matmul(ps[bank][:, k:k + 2], stage[:, c % 2, P * n:P * n + P], sel[:, :], start=True, stop=True)
                mm.then_inc(s_col, 1)

            def ada_part(b, j0=0, j1=4):
                for j in range(j0, j1):
                    ada_chunk(8 * b + 2 * j)
                    ada_chunk(8 * b + 2 * j + 1)
                    if j > j0:
                        ada_col(b, j - 1)
                ada_col(b, j1 - 1)

            def keep_warm(n, bank=3):
                for _ in range(n):
                    pe.matmul(ps[bank][:, :], zb[:, 0:P], zb[:, :], start=True, stop=True)

            def mean_square(k, idle=0):
                if k:
                    pe.wait_ge(s_rs, k)
                keep_warm(idle, 7)
                for kt in range(KT):
                    if kt % 2 == 0:
                        pe.wait_ge(s_sq, 4 * k + kt // 2 + 1)
                    mm = pe.matmul(stat, onesm[:, :], sq[:, kt, :], start=kt == 0, stop=kt == KT - 1)
                mm.then_inc(s_stat, 1)

            def w_of(m, kts=KT):
                w = pl.width[m] // kts
                v = slice(0, pl.width[m])
                return (whi[:, m % SPL, v].rearrange("p (k n) -> p k n", n=w),
                        wlo[:, m % SPL, v].rearrange("p (k n) -> p k n", n=w))

            def feature_major(m, dst, ah, al, i=0, kts=KT, o=None):
                wh, wl = w_of(m, kts)
                for nt in range(wh.shape[2] // P):
                    for kt in range(kts):
                        if o is not None and nt == 0:
                            pe.wait_ge(s_h, 8 * o + kt + 1)
                            keep_warm(WARM_KT)
                        n = slice(nt * P, nt * P + P)
                        pe.matmul(dst(nt), wh[:, kt, n], ah[:, kt, :], start=kt == 0, stop=False)
                        pe.matmul(dst(nt), wh[:, kt, n], al[:, kt, :], start=False, stop=False)
                        mm = pe.matmul(dst(nt), wl[:, kt, n], ah[:, kt, :], start=False, stop=kt == kts - 1)
                return mm

            def token_major(m, dst, ah, al, o=None):
                wh, wl = w_of(m)
                for tt in range(2):
                    for kt in range(KT):
                        if o is not None and tt == 0:
                            pe.wait_ge(s_h, 8 * o + kt + 1)
                            keep_warm(WARM_KT)
                        t = slice(tt * P, tt * P + P)
                        pe.matmul(dst(tt), ah[:, kt, t], wh[:, kt, :], start=kt == 0, stop=False)
                        pe.matmul(dst(tt), ah[:, kt, t], wl[:, kt, :], start=False, stop=False)
                        mm = pe.matmul(dst(tt), al[:, kt, t], wh[:, kt, :], start=False, stop=kt == KT - 1)
                return mm

            def split_ready(m, i=0):
                pe.wait_ge(s_lo, m + 1 + 6 * i)

            def mid_free(u):
                if pl.before(u):
                    pe.wait_ge(s_mid, pl.before(u))

            def linear_mid(m, ah, al, tm=False, i=0, o=None):
                u = pl.um[m]
                split_ready(m, i)
                mid_free(u)
                w = pl.width[m] // KT
                if tm:
                    mm = token_major(m, lambda tt: ps[4 + u % MID][:, w * tt:w * tt + w], ah, al, o)
                else:
                    mm = feature_major(m, lambda nt: ps[4 + u % MID][:, T * nt:T * nt + T], ah, al, o=o)
                mm.then_inc(s_mm, 1)

            def linear_y(m, j, ah, al):
                split_ready(m)
                feature_major(m, lambda nt: ps[j][:, T * nt:T * nt + T], ah, al).then_inc(s_mm, 1)

            def open_y():
                for b in range(4):
                    pe.matmul(ps[b][:, :], zb[:, 0:P], zb[:, :], start=True, stop=True)

            def rows_onto_y(m, ah, al, last=False):
                wh, wl = w_of(m, 2)
                for nt in range(KT):
                    for k in range(2):
                        t = slice(T * k, T * k + T)
                        y = ps[nt // 2][:, T * (nt % 2):T * (nt % 2) + T]
                        n = slice(nt * P, nt * P + P)
                        pe.matmul(y, wh[:, k, n], ah[:, t], start=False, stop=False, skip_group_check=True)
                        pe.matmul(y, wh[:, k, n], al[:, t], start=False, stop=False, skip_group_check=True)
                        mm = pe.matmul(y, wl[:, k, n], ah[:, t], start=False, stop=False, skip_group_check=True)
                    if last and nt in (1, 3, 5):
                        mm.then_inc(s_yb, 1)
                return mm

            def ffn(f, o):
                m0, c0 = M_FF[f], 16 * f
                u0 = pl.um[m0]

                def ff_in(c, m, i=0, o=None):
                    split_ready(m, i)
                    if c == 0:
                        mid_free(u0)
                    else:
                        pe.wait_ge(s_mid, u0 + c - MID + 1 + 3 * i)
                    bank = ps[4 + (u0 + c) % MID]
                    feature_major(m, lambda nt: bank[:, T * nt:T * nt + T], hh, hl, o=o).then_inc(s_mm, 1)

                def ff_out(c, m, i=0):
                    split_ready(m, i)
                    pe.wait_ge(s_fact, c0 + c + 1 + 3 * i)
                    rows_onto_y(m, fhi[:, c % 3, :], flo[:, c % 3, :], last=c == 15).then_inc(s_mm, 1)

                ff_in(0, m0, o=o)
                pe.wait_ge(s_mod, (B1SH if f == 0 else B2SH) + 1)
                pe.wait_ge(s_mid, u0)
                open_y()
                with pe.Fori(0, 5) as i:
                    for j in range(3):
                        ff_in(j + 1, m0 + 1 + 2 * j, i)
                        ff_out(j, m0 + 2 + 2 * j, i)
                ff_out(15, m0 + 31)

            N_Y = {1: 4, 3: 8, 5: 12, 7: 16, 10: 20}

            def boundary(k, b1):
                mean_square(k)
                if b1 is not None:
                    ada_part(b1, 0, 2)
                    mean_square(k + 1)
                    ada_part(b1, 2)
                else:
                    mean_square(k + 1, WARM_UPDATE)
                pe.wait_ge(s_yfree, N_Y[k])
                keep_warm(WARM_ADA if b1 is not None else WARM_H)

            def vectors(i, bank):
                pe.transpose(ps[bank][:, 0:NV[i]], vrow[0:NV[i], i, :], ident[0:NV[i], 0:NV[i]]).then_inc(s_vT, 1)

            pe.wait_ge(s_const, 5)
            pe.wait_ge(s_crow, 16 * 5)
            vectors(0, 7)
            pe.wait_ge(s_x0, 16)
            for b in range(4):
                for q in range(4):
                    kt, tt = 2 * b + q // 2, q % 2
                    mm = pe.transpose(ps[b][:, q * P:q * P + P], x_tm[:, tt, kt * P:kt * P + P], ident[:, :])
                mm.then_inc(s_xT, 1)
            pe.wait_ge(s_cp, 3)
            pe.wait_ge(s_sel, 1)
            pe.wait_ge(s_vec, 1)
            ada_part(B0SH, 0, 1)
            mean_square(0)
            ada_part(B0SH, 1, 3)
            pe.wait_ge(s_vrow, 16 * 15)
            pe.wait_ge(s_x, 4)
            for i in range(1, 6):
                if i >= 3:
                    pe.wait_ge(s_vec, i - 1)
                vectors(i, 2 + i % 2)
            ada_part(B0SH, 3)
            if has("gmlp"):
                for j in range(4):
                    linear_mid(M_V[j], hh, hl, tm=True, o=0 if j == 0 else None)
                pe.wait_ge(s_gm, 64)
                pe.wait_ge(s_x, 4)
                for b in range(2):
                    for q in range(4):
                        mm = pe.transpose(ps[b][:, q * P:q * P + P], ws[:, 4 * b + q, :], ident[:, :])
                    mm.then_inc(s_wsT, 1)
                for j in range(4):
                    linear_mid(M_U[j], hh, hl)
                ada_part(B0G)
                pe.wait_ge(s_wT, 1)
                pe.wait_ge(s_vn, 2)
                pe.wait_ge(s_wTc, 2)
                for b in range(4):
                    for g in (2 * b, 2 * b + 1):
                        for tt in range(2):
                            c0 = (g % 2) * T + tt * P
                            mm = pe.matmul(ps[b][:, c0:c0 + P], v_tm[:, tt, g * P:g * P + P], wT[:, g, :], start=True, stop=True)
                    mm.then_inc(s_mix, 1)
                ada_part(B0SC)
                pe.wait_ge(s_oa, 4)
                for j in range(4):
                    linear_y(M_AO[j], j, hh, hl)
                if has("ffn0"):
                    boundary(1, B1SH)
                else:
                    mean_square(1)
            if has("ffn0"):
                pe.wait_ge(s_yfree, 4)
                ffn(0, 1)
                mean_square(3)

            if has("attn"):
                ada_part(BKV, 0, 2)
                mean_square(4)
                ada_part(BKV, 2)
                pe.wait_ge(s_yfree, 8)
                keep_warm(WARM_ADA)
                for m in (M_KC, M_VC, M_KS, M_KW):
                    linear_mid(m, gh, gl, o=2 if m == M_KC else None)
                for m in (M_VS, M_VW):
                    linear_mid(m, gh, gl, tm=True)
                for j in range(4):
                    linear_mid(M_Q[j], hh, hl, o=3 if j == 0 else None)
                linear_mid(M_GT, hh, hl, tm=True)
                for j in range(2):
                    pe.wait_ge(s_blk, j + 1)
                    for c in range(2):
                        m = M_CW[j][c]
                        split_ready(m)
                        wh, wl = w_of(m)
                        for i in range(8):
                            k = (8 * c + i) * WIN
                            ah, al = bw[:, k:k + P], bw[:, 16 * WIN + k:16 * WIN + k + P]
                            pe.matmul(ps[j][:, 0:T], ah, wh[:, i, :], start=c == 0 and i == 0, stop=False)
                            pe.matmul(ps[j][:, 0:T], ah, wl[:, i, :], start=False, stop=False)
                            mm = pe.matmul(ps[j][:, 0:T], al, wh[:, i, :], start=False, stop=c == 1 and i == 7)
                        mm.then_inc(s_mm, 1)
                for j in range(2):
                    pe.wait_ge(s_ht, j + 1)
                    for nt in range(2):
                        mm = pe.transpose(ps[2 + j][:, WIN * nt:WIN * nt + WIN], ht[:, j, P * nt:P * nt + P], ident[0:WIN, 0:WIN])
                    mm.then_inc(s_htT, 1)
                pe.wait_ge(s_hid, 4)
                pe.wait_ge(s_aw, 96)
                for nt in range(2):
                    pe.matmul(ps[0][:, 0:60], w2k[:, nt, :], hid[:, 0, nt, :], start=nt == 0, stop=nt == 1)
                for g in range(NG):
                    for nt in range(2):
                        mm = pe.matmul(ps[1][0:NC, HD * g:HD * g + HD], hid[:, 1, nt, NC * g:NC * g + NC], w2v[:, nt, :],
                                       start=nt == 0, stop=nt == 1)
                mm.then_inc(s_w2, 1)
                pe.wait_ge(s_mid, pl.ua[8 * B1G])
                keep_warm(4, 4)
                pe.wait_ge(s_kv, 2)
                pe.wait_ge(s_kcp, 128)
                pe.wait_ge(s_mid, pl.ua[8 * B1G])

                def scores(h):
                    if h:
                        pe.wait_ge(s_Sev, h)
                    b, g = slice(64 * (h % 2), 64 * (h % 2) + 64), h // 4
                    for qt in range(2):
                        q = qT[b, h // 2, P * qt:P * qt + P]
                        nk = P * (qt + 1)
                        pe.matmul(ps[qt][:, 0:NCP + nk], q, kc[b, g, 0:NCP + nk], start=True, stop=True)
                        mm = pe.matmul(score_psum(qt, 2), q, kw[b, g, 0:nk], start=True, stop=True)
                    mm.then_inc(s_S, 1)

                def turn(h):
                    hb = h % 2
                    pe.wait_ge(s_p, h + 1)
                    if h:
                        pe.wait_ge(s_Tev, 2 * h)
                        pe.wait_ge(s_TevD, 2 * h)
                    for br in (1, 2):
                        bank = ps[2 + br]
                        for qt in range(2):
                            at_ = part(qt, br).start
                            for kt in range(qt + 1):
                                pe.transpose(bank[:, (kt * T + (qt - kt) * P):(kt * T + (qt - kt) * P) + P],
                                             pp[:, hb, at_ + P * kt:at_ + P * kt + P], ident[:, :])
                        mm = pe.transpose(bank[0:NCP, 384:512], pp[:, hb, part(br - 1, 0)], ident[:, :])
                    mm.then_inc(s_T, 1)

                def values(h):
                    hb, g = h % 2, h // 4
                    if h % 2 == 0 and h >= 4:
                        pe.wait_ge(s_oev, h // 2 - 1)
                    pe.wait_ge(s_Tev, 2 * h + 2)
                    pe.wait_ge(s_TevD, 2 * h + 2)
                    o = ps[5 + (h // 2) % 2][64 * (h % 2):64 * (h % 2) + 64, :]
                    n = slice(HD * g, HD * g + HD)
                    pe.matmul(o[:, 0:T], v_s[:, 0, n], pts[:, hb, 0:T], start=True, stop=False)
                    pe.matmul(o[:, P:T], v_s[:, 1, n], pts[:, hb, T:T + P], start=False, stop=False)
                    pe.matmul(o[:, P:T], v_w[:, 1, n], pts[:, hb, 512 + T:512 + T + P], start=False, stop=False)
                    for qt in range(2):
                        pe.matmul(o[:, P * qt:P * qt + P], vcs[0:NC, g, :], pts[0:NC, hb, 512 * qt + 384:512 * qt + 512],
                                  start=False, stop=False)
                    pe.matmul(o[:, 0:T], v_w[:, 0, n], pts[:, hb, 512:512 + T], start=False, stop=True).then_inc(s_O, 1)

                pe.wait_ge(s_rs, 5)
                scores(0)
                keep_warm(3, 4)
                scores(1)
                keep_warm(3, 4)
                for h in range(NH):
                    pe.wait_ge(s_Sev, min(h + 2, NH))
                    if h % 2 == 0 and h:
                        ada_col(B1G + (h - 2) // 8, (h - 2) % 8 // 2)
                    if h + 2 < NH:
                        scores(h + 2)
                    turn(h)
                    ada_chunk(8 * B1G + h)
                    values(h)
                ada_col(B1SC, 3)
                pe.wait_ge(s_oh, 8)
                pe.wait_ge(s_mod, B1SC + 1)
                for j in range(4):
                    linear_y(M_BO[j], j, hh, hl)
                if not has("ffn1"):
                    mean_square(5)

            if has("ffn1"):
                boundary(5, B2SH)
                pe.wait_ge(s_yfree, 12)
                ffn(1, 4)
                mean_square(7)

            if has("gla"):
                ada_part(B2G, 0, 1)
                pe.wait_ge(s_ctx, 16)
                for b in range(4):
                    pe.wait_ge(s_yfree, 16 - 3 + b)
                    for q in range(4):
                        kt, tt = 2 * b + q // 2, q % 2
                        mm = pe.transpose(ps[b][:, q * P:q * P + P], ctx_tm[:, tt, kt * P:kt * P + P], ident[:, :])
                    mm.then_inc(s_cT, 1)
                ada_part(B2G, 1, 2)
                mean_square(8, WARM_CTX)
                pe.wait_ge(s_cx, 4)
                mean_square(9)
                ada_part(B2G, 2)

                def linear_two(m, tm):
                    split_ready(m)
                    w = pl.width[m] // KT
                    for i, (ah, al_, t_) in enumerate(((hh, hl, tm[0]), (gh, gl, tm[1]))):
                        u = pl.um[m] + i
                        o = 5 + i if m == M_K2 else None
                        mid_free(u)
                        if t_:
                            mm = token_major(m, lambda tt: ps[4 + u % MID][:, w * tt:w * tt + w], ah, al_, o)
                        else:
                            mm = feature_major(m, lambda nt: ps[4 + u % MID][:, T * nt:T * nt + T], ah, al_, o=o)
                    mm.then_inc(s_mm, 1)

                linear_two(M_K2, (False, True))
                pe.wait_ge(s_mod, B2G + 1)
                for j in range(2):
                    linear_two(M_V2[j], (True, True))
                linear_two(M_AL, (False, False))
                linear_mid(M_Q2, hh, hl)
                pe.wait_ge(s_mid, pl.um[M_AL] + 2)
                pe.wait_ge(s_wab, 64)
                pe.wait_ge(s_gm3, 2)
                pe.wait_ge(s_cx, 4)
                for tt in range(2):
                    pe.matmul(ps[tt][:, :], alc[:, P * tt:P * tt + P], wab[:, :], start=True, stop=True)
                for j in range(4):
                    mm = pe.matmul(ps[2 + j // 2][:, T * (j % 2):T * (j % 2) + T], wab[:, P * j:P * j + P], alx[:, :], start=True, stop=True)
                mm.then_inc(s_gp, 1)
                for j in range(2):
                    linear_mid(M_OG[j], hh, hl)
                pe.wait_ge(s_gm3, 4)
                pe.wait_ge(s_g, 2)
                ones = one1[:, 0:P]
                pe.matmul(ps[0][:, 0:T], trif[:, :], gc[:, 0, 0:T], start=True, stop=False)
                pe.matmul(ps[0][:, 0:T], ones, gc[:, 1, 0:T], start=False, stop=True)
                pe.matmul(ps[1][:, 0:T], trif[:, :], gc[:, 1, 0:T], start=True, stop=True)
                pe.matmul(ps[0][:, T:512], trib[:, :], gc[:, 0, T:512], start=True, stop=True)
                pe.matmul(ps[1][:, T:512], trib[:, :], gc[:, 1, T:512], start=True, stop=False)
                pe.matmul(ps[1][:, T:512], ones, gc[:, 0, T:512], start=False, stop=True).then_inc(s_cum, 1)
                for j in range(2):
                    linear_mid(M_SC[j], hh, hl)
                pe.wait_ge(s_kd, 1)
                pe.wait_ge(s_g, 4)
                for f in range(2):
                    for h in range(GHD):
                        dst = ps[2][64 * (h % 2):64 * (h % 2) + 64, 256 * f + P * (h // 2):256 * f + P * (h // 2) + P]
                        for tt in range(2):
                            mm = pe.matmul(dst, wc[:, tt, 256 * f + 64 * h:256 * f + 64 * h + 64], vctx[:, tt, P * h:P * h + P],
                                           start=tt == 0, stop=tt == 1)
                mm.then_inc(s_st, 1)
                for j in range(2):
                    linear_mid(M_SX[j], hh, hl)
                for j in range(2):
                    linear_mid(M_SB[j], hh, hl)

                def level(n):
                    if n == 0:
                        pe.wait_ge(s_ste, 1)
                        pe.wait_ge(s_mid, pl.um[M_Q2] + 1)
                        op = qk[:, :, :]
                    else:
                        keep_warm(WARM_LEVEL, 7)
                        pe.wait_ge(s_E, n)
                        op = eb[:, (n - 1) % 2, :, :]
                    if n >= 2:
                        pe.wait_ge(s_A, n - 1)
                    for jt in range(2):
                        it = 1 - jt if n == 1 else jt
                        for h in range(GHD):
                            b = slice(64 * (h % 2), 64 * (h % 2) + 64)
                            c = 2 * jt + h // 2
                            mm = pe.matmul(ps[2 * (n % 2) + h % 2][:, P * c:P * c + P], op[b, 2 + h // 2, P * jt:P * jt + P],
                                           op[b, h // 2, P * it:P * it + P], start=True, stop=True)
                    mm.then_inc(s_lev, 1)

                level(0)
                for n in range(1, 9):
                    level(n)
                    ada_chunk(8 * B2SC + n - 1)
                    if n in (3, 5, 7):
                        ada_col(B2SC, (n - 3) // 2)
                ada_col(B2SC, 3)
                pe.wait_ge(s_qi, 1)
                pe.wait_ge(s_A, 9)
                pe.wait_ge(s_mid, pl.ua[8 * B2SC + 7] + 1)
                for h in range(GHD):
                    b = slice(64 * (h % 2), 64 * (h % 2) + 64)
                    o = ps[O_BANKS[h % 2]][:, T * (h // 2):T * (h // 2) + T]
                    for f in range(2):
                        pe.matmul(o, st[b, f, h // 2, :], qi[b, 2 * f + h // 2, :], start=f == 0, stop=False)
                    for it in range(2):
                        for jt in range(2):
                            a_ = (a_d if it == jt else a_x)[:, h % 2, jt, h // 2, :]
                            mm = pe.matmul(o[:, P * it:P * it + P], vx[:, jt, P * h:P * h + P], a_, start=False, stop=it + jt == 2)
                mm.then_inc(s_o4, 1)
                pe.wait_ge(s_o2, 1)
                pe.wait_ge(s_mod, B2SC + 1)
                for b in range(2):
                    mm = pe.matmul(ps[MS_BANKS[b]][:, :], onesm[:, :], o2[:, 2 * b:2 * b + 2, :].rearrange("p k t -> p (k t)"), start=True, stop=True)
                mm.then_inc(s_ms4, 1)
                def out_half(j, half, signal):
                    split_ready(M_WO[j])
                    wh, wl = w_of(M_WO[j])
                    for nt in range(2):
                        n, y = slice(P * nt, P * nt + P), ps[j][:, T * nt:T * nt + T]
                        for kt in range(4 * half, 4 * half + 4):
                            pe.matmul(y, wh[:, kt, n], hh[:, kt, :], start=False, stop=False, skip_group_check=True)
                            pe.matmul(y, wh[:, kt, n], hl[:, kt, :], start=False, stop=False, skip_group_check=True)
                            mm = pe.matmul(y, wl[:, kt, n], hh[:, kt, :], start=False, stop=False, skip_group_check=True)
                    if signal:
                        mm.then_inc(s_mm, 1)

                open_y()
                pe.wait_ge(s_cv, 1)
                for j in range(3):
                    out_half(j, 1, False)
                pe.wait_ge(s_gs, 1)
                for j in range(3):
                    out_half(j, 0, True)
                out_half(3, 1, False)
                out_half(3, 0, True)
                if not has("ffn2"):
                    mean_square(10)

            if has("ffn2"):
                boundary(10, None)
                pe.wait_ge(s_yfree, 20)
                pe.wait_ge(s_mid, pl.ua[8 * B2SC + 7] + 1)
                pe.wait_ge(s_mod, B2SC + 1)

                def up(m, bank, i=0, o=None):
                    split_ready(m, i)
                    feature_major(m, lambda nt: ps[bank][:, T * nt:T * nt + T], hh, hl, o=o).then_inc(s_mm, 1)

                def conv_body(c, i=0):
                    if c:
                        pe.wait_ge(s_ue, c + 2 * i)
                    up(M_UP + 3 * c + 2, 4 + (c + 1) % 2, i)
                    if c:
                        pe.wait_ge(s_fa, c + 2 * i)
                    up(M_UP + 3 * c + 3, 6 + (c + 1) % 2, i)
                    down(c, M_UP + 3 * c + 4, i)

                def down(c, m, i=0):
                    split_ready(m, i)
                    pe.wait_ge(s_cact, c + 1 + 2 * i)
                    rows_onto_y(m, chi[:, c % 2, :], clo[:, c % 2, :], last=c == CF - 1).then_inc(s_mm, 1)

                up(M_UP, 4, o=7)
                up(M_UP + 1, 6)
                open_y()
                conv_body(0)
                with pe.Fori(0, 4) as i:
                    for j in range(2):
                        conv_body(1 + j, i)
                conv_body(9)
                down(10, M_UP + 32)
                mean_square(12)

            pe.wait_ge(s_vec, 6)
            if N_UPD:
                pe.wait_ge(s_yfree, 4 * N_UPD)
            if has("gmlp"):
                pe.wait_ge(s_wTc, 2)
            for b in range(4):
                pe.wait_ge(s_x, 4 * N_UPD + b + 1)
                for q in range(4):
                    tt, kt = q // 2, 2 * b + q % 2
                    mm = pe.transpose(ps[b][:, q * P:q * P + P], x[:, kt, tt * P:tt * P + P], ident[:, :])
                mm.then_inc(s_oT, 1)

        @block.gpsimd
        def _(pool):
            chain = [0]

            def link(ins):
                ins.then_inc(g_ch, 1)
                chain[0] += 1
                pool.wait_ge(g_ch, chain[0])

            def split_two(m):
                pool.wait_ge(s_lo, m)
                for c in (m, m + 1):
                    pool.wait_ge(s_hi, c + 1)
                    w = pl.width[c]
                    pool.tensor_tensor(wlo[:, c % SPL, 0:w], raw[:, pl.nm[c] % RAW, 0:w], whi[:, c % SPL, 0:w],
                                       ALU.subtract).then_inc(s_lo, 1)

            link(pool.memset(ident[:, :], 0.0))
            pool.affine_select(out=ident[:, :], in_=ident[:, :], compare_op=ALU.not_equal, fill=1.0, base=0,
                               pattern=[[-1, P]], channel_multiplier=1).then_inc(s_const, 1)
            pool.memset(onesm[:, :], 1.0 / D).then_inc(s_const, 1)
            pool.memset(zb[:, :], 0.0).then_inc(s_const, 1)
            pool.memset(one1[:, :], 1.0).then_inc(s_const, 1)
            link(pool.memset(eps[:, :], EPS))
            pool.memset(zero1[:, :], 0.0).then_inc(s_const, 1)
            pool.memset(cpad[:, :, :, :], 0.0).then_inc(s_cpad0, 1)
            if has("gmlp"):
                pool.wait_ge(s_wTc, 2)
                pool.affine_select(out=wT[:, :, :], in_=wT[:, :, :], compare_op=ALU.is_ge, fill=0.0, base=0,
                                   pattern=[[0, 8], [1, P]], channel_multiplier=-1).then_inc(s_wT, 1)

            if has("ffn0"):
                split_two(M_FF[0])
            if has("attn"):
                pool.wait_ge(s_mm, M_FF[0] + 32)
                link(pool.memset(cmask[:, :], 0.0))
                pool.affine_select(out=cmask[:, :], in_=cmask[:, :], compare_op=ALU.is_ge, fill=NEG, base=P,
                                   pattern=[[-1, T]], channel_multiplier=1).then_inc(s_asm, 1)
                for m_, keep, fill in ((cmm, 0.0, NEG), (cm01, 1.0, 0.0)):
                    link(pool.memset(m_[:, :, :], keep))
                    pool.affine_select(out=m_[:, :, :], in_=m_[:, :, :], compare_op=ALU.is_ge, fill=fill, base=-31,
                                       pattern=[[P, 2], [-16, NCP]], channel_multiplier=1).then_inc(s_asm, 1)
                split_two(M_KC)
            if has("ffn1"):
                split_two(M_FF[1])

            if has("gla"):
                pool.wait_ge(s_mm, M_FF[1] + 32)
                pool.memset(wab[:, :], 0.0).then_inc(s_wz, 1)
                pool.wait_ge(s_wz, 1)
                for n, a in enumerate((alx, alc)):
                    pool.memset(a[32:33, :], 1.0).then_inc(s_gm3, 1)
                    pool.wait_ge(s_gm3, n + 1)
                split_two(M_K2)
                for tri, cm in ((trif, 1), (trib, -1)):
                    link(pool.memset(tri[:, :], 1.0))
                    pool.affine_select(out=tri[:, :], in_=tri[:, :], compare_op=ALU.is_ge, fill=0.0, base=-1,
                                       pattern=[[-cm, P]], channel_multiplier=cm).then_inc(s_gm3, 1)
                link(pool.memset(lmask[:, :, :], 1.0))
                for n in range(7):
                    s = 64 >> n
                    v = lmask[:, n, :].rearrange("p (b a e) -> p b a e", a=2, e=s)
                    link(pool.affine_select(out=v, in_=v, compare_op=ALU.is_ge, fill=0.0, base=-s,
                                            pattern=[[-2 * s, P // (2 * s)], [s, 2], [0, s]], channel_multiplier=1))
                    ins = pool.affine_select(out=v, in_=v, compare_op=ALU.is_ge, fill=0.0, base=2 * s - 1,
                                             pattern=[[2 * s, P // (2 * s)], [-s, 2], [0, s]], channel_multiplier=-1)
                    if n < 6:
                        link(ins)
                ins.then_inc(s_gm3, 5)
                pool.wait_ge(s_B, 1)
                for l in range(8):
                    s = 128 >> l
                    if l >= 2:
                        pool.wait_ge(s_lev, l)
                    blocks = lambda a: a.rearrange("p k (b e) -> p k b e", e=2 * s)
                    fw, bw = blocks(bx[:, 0:2, :]), blocks(bx[:, 2:4, :])
                    eq, ek = blocks(eb[:, l % 2, 0:2, :]), blocks(eb[:, l % 2, 2:4, :])
                    shape = [P, 2, T // (2 * s), s]
                    fm_, bm = fw[:, :, :, s - 1:s].broadcast_to(shape), bw[:, :, :, s:s + 1].broadcast_to(shape)
                    left, right = slice(0, s), slice(s, 2 * s)
                    pool.tensor_tensor(eq[:, :, :, right], fw[:, :, :, right], fm_, ALU.subtract)
                    pool.tensor_tensor(ek[:, :, :, left], fm_, fw[:, :, :, left], ALU.subtract)
                    pool.tensor_tensor(eq[:, :, :, left], bm, bw[:, :, :, left], ALU.subtract)
                    pool.tensor_tensor(ek[:, :, :, right], bw[:, :, :, right], bm, ALU.subtract).then_inc(s_D, 1)

            if has("ffn2"):
                split_two(M_UP)


_INS = ["x", "c", "ada_w", "ada_b", "norm_g", "a_w_in", "a_ln_g", "a_ln_b", "a_w_s", "a_b_s", "a_w_out", "kv_ada_w",
        "kv_ada_b", "kv_norm_g", "kv_w", "cmp_pos", "cmp_w1", "cmp_b1", "cmp_w2", "cmp_b2", "b_w_in", "b_w_out",
        "ff_w_in", "ff_w_out", "c_2", "ctx_2", "c_ctx_2", "w_ada_2", "b_ada_2", "g_pre_mix_2", "g_post_mix_2",
        "g_pre_ffn_2", "g_post_ffn_2", "w_in_2", "w_af_2", "b_af_2", "w_ab_2", "b_ab_2", "g_head_2", "w_sc_2",
        "b_sc_2", "w_out_2", "w_up_2", "w_cf_2", "b_cf_2", "w_down_2"]
_OUTS = [((1, 256, 1024), "float32")]


def kernel(**inputs):
    import numpy as _np
    import concourse.bacc as _bacc
    from concourse import mybir as _mybir
    from concourse.bass_utils import run_bass_kernel_spmd as _run

    nc = _bacc.Bacc("TRN2", target_bir_lowering=False, num_devices=1)
    arrays, args = {}, {}
    for name in _INS:
        a = _np.ascontiguousarray(inputs[name])
        arrays[f"in_{name}_dram"] = a
        args[name] = nc.dram_tensor(f"in_{name}_dram", a.shape, _mybir.dt.from_np(a.dtype), kind="ExternalInput").ap()
    shape, dtype = _OUTS[0]
    res = nc.dram_tensor("out_0_dram", shape, _mybir.dt.from_np(_np.dtype(dtype)), kind="ExternalOutput").ap()
    build(nc, args, res)
    r = _run(nc, [arrays], core_ids=[0])
    return r.results[0]["out_0_dram"]
```
